# Optimizing a Trainium2 kernel written in Bass

```python
import math
import jax, jax.numpy as jnp
from jax import lax
import numpy as np

D_MODEL = 1024
BATCH = 1
SEQ = 512
DEPTH = 1

MIX_WIDTH = D_MODEL
DIFF_WIDTH = MIX_WIDTH // 2
RET_WIDTH = MIX_WIDTH - DIFF_WIDTH
N_DIFF_HEADS = 4
DIFF_V_DIM = DIFF_WIDTH // N_DIFF_HEADS
DIFF_QK_DIM = DIFF_V_DIM // 2
N_RET_HEADS = 4
RET_V_DIM = RET_WIDTH // N_RET_HEADS
RET_QK_DIM = RET_V_DIM // 2
DIFF_QK_COLS = N_DIFF_HEADS * 2 * DIFF_QK_DIM
RET_QK_COLS = N_RET_HEADS * RET_QK_DIM
SPLIT_SIZES = (DIFF_QK_COLS, DIFF_QK_COLS, DIFF_WIDTH, RET_QK_COLS, RET_QK_COLS, RET_WIDTH, RET_WIDTH)
SPLIT_POINTS = (512, 1024, 1536, 1792, 2048, 2560)
IN_COLS = 3072

ROPE_THETA = 500000.0
ROPE_FRACTION = 4
RET_THETA = 10000.0
Q_BLOCK = 128
RET_CHUNK = 128

N_KEYS = 128
N_EXPERTS = N_KEYS * N_KEYS
PEER_HEADS = 8
PEER_TOPK = 16
PEER_KEY_DIM = 256
PEER_TOKEN_BLOCK = 128

EPS = 1e-6


def rmsnorm(x, g):
    x32 = x.astype(jnp.float32)
    y = x32 * lax.rsqrt(jnp.mean(x32 * x32, axis=-1, keepdims=True) + EPS)
    return (y * g.astype(jnp.float32)).astype(x.dtype)

def group_norm(o, g):
    mu = jnp.mean(o, axis=-1, keepdims=True)
    c = o - mu
    var = jnp.mean(c * c, axis=-1, keepdims=True)
    return c * lax.rsqrt(var + EPS) * g.astype(jnp.float32)

def rotate_prefix(x, pos, inv_freq):
    half = inv_freq.shape[0]
    rot = 2 * half
    ang = pos[:, None] * inv_freq[None, :]
    shape = (1, pos.shape[0]) + (1,) * (x.ndim - 3) + (half,)
    cos = jnp.cos(ang).reshape(shape)
    sin = jnp.sin(ang).reshape(shape)
    xf = x.astype(jnp.float32)
    x1 = xf[..., :half]
    x2 = xf[..., half:rot]
    out = jnp.concatenate([x1 * cos - x2 * sin, x2 * cos + x1 * sin, xf[..., rot:]], axis=-1)
    return out.astype(x.dtype)

def diff_attention(q, k, v, lam):
    B, S, H, _, d = q.shape
    nb = S // Q_BLOCK
    scale = d ** -0.5
    q_blocks = q.reshape(B, nb, Q_BLOCK, H, 2, d).transpose(1, 0, 2, 3, 4, 5)

    def one_block(qb):
        s = jnp.einsum('bqhmd,bkhmd->bhmqk', qb, k).astype(jnp.float32) * scale
        p = jax.nn.softmax(s, axis=-1)
        a = p[:, :, 0] - lam * p[:, :, 1]
        return jnp.einsum('bhqk,bkhe->bqhe', a.astype(v.dtype), v)

    o = lax.map(one_block, q_blocks)
    return o.transpose(1, 0, 2, 3, 4).reshape(B, S, H, v.shape[-1])

def retention_direction(q, k, v, log_gamma, strict):
    B, S, H, dk = q.shape
    dv = v.shape[-1]
    C = RET_CHUNK
    nc = S // C
    qc = q.reshape(B, nc, C, H, dk).transpose(1, 0, 3, 2, 4)
    kc = k.reshape(B, nc, C, H, dk).transpose(1, 0, 3, 2, 4)
    vc = v.reshape(B, nc, C, H, dv).transpose(1, 0, 3, 2, 4)
    idx = jnp.arange(C, dtype=jnp.float32)
    dist = idx[:, None] - idx[None, :]
    mask = (dist > 0) if strict else (dist >= 0)
    lg = log_gamma[:, None, None]
    decay_in = jnp.where(mask[None], jnp.exp(lg * jnp.maximum(dist, 0.0)[None]), 0.0)
    q_decay = jnp.exp(log_gamma[:, None] * (idx + 1.0)[None])[None, :, :, None]
    k_decay = jnp.exp(log_gamma[:, None] * (C - 1.0 - idx)[None])[None, :, :, None]
    chunk_decay = jnp.exp(log_gamma * C)[None, :, None, None]

    def step(state, inp):
        qi, ki, vi = inp
        inner = jnp.einsum('bhid,bhjd->bhij', qi, ki) * decay_in[None]
        o = jnp.einsum('bhij,bhjv->bhiv', inner, vi) + jnp.einsum('bhid,bhdv->bhiv', qi * q_decay, state)
        state = state * chunk_decay + jnp.einsum('bhjd,bhjv->bhdv', ki * k_decay, vi)
        return state, o

    state0 = jnp.zeros((B, H, dk, dv), jnp.float32)
    _, o = lax.scan(step, state0, (qc, kc, vc))
    return o.transpose(1, 0, 3, 2, 4).reshape(B, S, H, dv)

def peer_ffn(xn, w_query, sub_keys, expert_down, expert_up):
    B, S, D = xn.shape
    T = B * S
    nb = T // PEER_TOKEN_BLOCK
    x_blocks = xn.reshape(nb, PEER_TOKEN_BLOCK, D)

    def one_block(xb):
        tb = xb.shape[0]
        q = (xb @ w_query).reshape(tb, PEER_HEADS, 2, PEER_KEY_DIM // 2)
        s = jnp.einsum('thpd,hpnd->thpn', q, sub_keys).astype(jnp.float32)
        top_s, top_i = lax.top_k(s, PEER_TOPK)
        cand_s = (top_s[:, :, 0, :, None] + top_s[:, :, 1, None, :]).reshape(tb, PEER_HEADS, PEER_TOPK * PEER_TOPK)
        cand_i = (top_i[:, :, 0, :, None] * N_KEYS + top_i[:, :, 1, None, :]).reshape(tb, PEER_HEADS, PEER_TOPK * PEER_TOPK)
        best_s, pos = lax.top_k(cand_s, PEER_TOPK)
        eid = jnp.take_along_axis(cand_i, pos, axis=-1)
        gate = jax.nn.softmax(best_s, axis=-1)
        u = jnp.take(expert_down, eid, axis=0)
        act = jax.nn.gelu(jnp.einsum('thkd,td->thk', u, xb).astype(jnp.float32), approximate=False)
        v = jnp.take(expert_up, eid, axis=0)
        return jnp.einsum('thk,thkd->td', (gate * act).astype(v.dtype), v)

    out = lax.map(one_block, x_blocks)
    return out.reshape(B, S, D).astype(xn.dtype)

def first_inputs(seed: int = 0) -> dict:
    key = jax.random.key(seed)
    ks = jax.random.split(key, 16)
    f32 = jnp.float32
    nrm = jax.random.normal
    x = nrm(ks[0], (BATCH, SEQ, D_MODEL), f32)
    attn_norm_g = 1.0 + 0.02 * nrm(ks[1], (DEPTH, D_MODEL), f32)
    w_in = nrm(ks[2], (DEPTH, D_MODEL, IN_COLS), f32) * D_MODEL ** -0.5
    diff_lambda = 0.1 * nrm(ks[3], (DEPTH, 4, DIFF_QK_DIM), f32)
    diff_norm_g = 1.0 + 0.02 * nrm(ks[4], (DEPTH, DIFF_V_DIM), f32)
    gammas = 1.0 - jnp.exp2(-5.0 - jnp.arange(N_RET_HEADS, dtype=f32))
    base = jnp.log(-jnp.log(gammas))
    ret_log_decay = base[None, None, :] + 0.05 * nrm(ks[5], (DEPTH, 2, N_RET_HEADS), f32)
    ret_norm_g = 1.0 + 0.02 * nrm(ks[6], (DEPTH, N_RET_HEADS, RET_V_DIM), f32)
    w_out = nrm(ks[7], (DEPTH, MIX_WIDTH, D_MODEL), f32) * MIX_WIDTH ** -0.5
    ffn_norm_g = 1.0 + 0.02 * nrm(ks[8], (DEPTH, D_MODEL), f32)
    peer_w_query = nrm(ks[9], (DEPTH, D_MODEL, PEER_HEADS * PEER_KEY_DIM), f32) * D_MODEL ** -0.5
    peer_sub_keys = nrm(ks[10], (DEPTH, PEER_HEADS, 2, N_KEYS, PEER_KEY_DIM // 2), f32) * (PEER_KEY_DIM // 2) ** -0.5
    peer_u = nrm(ks[11], (DEPTH, N_EXPERTS, D_MODEL), f32) * D_MODEL ** -0.5
    peer_v = nrm(ks[12], (DEPTH, N_EXPERTS, D_MODEL), f32) * PEER_HEADS ** -0.5
    final_norm_g = 1.0 + 0.02 * nrm(ks[13], (D_MODEL,), f32)
    return {'x': x, 'attn_norm_g': attn_norm_g, 'w_in': w_in, 'diff_lambda': diff_lambda,
            'diff_norm_g': diff_norm_g, 'ret_log_decay': ret_log_decay, 'ret_norm_g': ret_norm_g,
            'w_out': w_out, 'ffn_norm_g': ffn_norm_g, 'peer_w_query': peer_w_query,
            'peer_sub_keys': peer_sub_keys, 'peer_u': peer_u, 'peer_v': peer_v,
            'final_norm_g': final_norm_g}

def first_block(x, attn_norm_g, w_in, diff_lambda, diff_norm_g, ret_log_decay, ret_norm_g,
              w_out, ffn_norm_g, peer_w_query, peer_sub_keys, peer_u, peer_v, final_norm_g):
    B, S, _ = x.shape
    pos = jnp.arange(S, dtype=jnp.float32)
    rot_dim = DIFF_QK_DIM // ROPE_FRACTION
    rope_inv = jnp.power(jnp.float32(ROPE_THETA), -jnp.arange(rot_dim // 2, dtype=jnp.float32) * 2.0 / rot_dim)
    ret_inv = 1.0 / jnp.power(jnp.float32(RET_THETA), jnp.linspace(0.0, 1.0, RET_QK_DIM // 2, dtype=jnp.float32))

    for l in range(DEPTH):
        lambda_init = 0.8 - 0.6 * math.exp(-0.3 * l)
        h = rmsnorm(x, attn_norm_g[l])
        proj = h @ w_in[l]
        dq, dk, dv, rq, rk, rv, rg = jnp.split(proj, SPLIT_POINTS, axis=-1)

        dq = rotate_prefix(dq.reshape(B, S, N_DIFF_HEADS, 2, DIFF_QK_DIM), pos, rope_inv)
        dk = rotate_prefix(dk.reshape(B, S, N_DIFF_HEADS, 2, DIFF_QK_DIM), pos, rope_inv)
        dv = dv.reshape(B, S, N_DIFF_HEADS, DIFF_V_DIM)
        lam_p = diff_lambda[l].astype(jnp.float32)
        lam = jnp.exp(jnp.sum(lam_p[0] * lam_p[1])) - jnp.exp(jnp.sum(lam_p[2] * lam_p[3])) + lambda_init
        a = diff_attention(dq, dk, dv, lam)
        a = rmsnorm(a, diff_norm_g[l]).astype(jnp.float32) * (1.0 - lambda_init)
        a = a.reshape(B, S, DIFF_WIDTH)

        rq = rotate_prefix(rq.reshape(B, S, N_RET_HEADS, RET_QK_DIM), pos, ret_inv).astype(jnp.float32)
        rk = rotate_prefix(rk.reshape(B, S, N_RET_HEADS, RET_QK_DIM), pos, ret_inv).astype(jnp.float32) * RET_QK_DIM ** -0.5
        rv = rv.reshape(B, S, N_RET_HEADS, RET_V_DIM).astype(jnp.float32)
        log_gamma = -jnp.exp(ret_log_decay[l].astype(jnp.float32))
        r_fwd = retention_direction(rq, rk, rv, log_gamma[0], False)
        r_bwd = retention_direction(rq[:, ::-1], rk[:, ::-1], rv[:, ::-1], log_gamma[1], True)[:, ::-1]
        r = group_norm(r_fwd + r_bwd, ret_norm_g[l]).reshape(B, S, RET_WIDTH)
        r = jax.nn.silu(rg.astype(jnp.float32)) * r

        mix = jnp.concatenate([a, r], axis=-1).astype(x.dtype)
        x = x + mix @ w_out[l]

        x = x + peer_ffn(rmsnorm(x, ffn_norm_g[l]), peer_w_query[l], peer_sub_keys[l], peer_u[l], peer_v[l])

    return rmsnorm(x, final_norm_g)


RWKV_HEAD = 64
D_RWKV = D_MODEL // 2
N_RWKV_HEADS = D_RWKV // RWKV_HEAD
DECAY_LORA = 64
AAA_LORA = 64
GATE_LORA = 160
LN_X_EPS = 64e-5
D_CONV = D_MODEL // 2
CONV_WIDTH = 3
N_MEM = 256
N_XHEADS = 4
XHEAD_DIM = D_MODEL // N_XHEADS
D_FF = 4 * D_MODEL
RMS_EPS = 1e-6

SPLITS = (D_RWKV, D_RWKV, D_RWKV, DECAY_LORA, AAA_LORA, GATE_LORA,
          D_CONV, D_CONV, D_CONV,
          D_MODEL, D_MODEL)
D_IN = sum(SPLITS)
RWKV_COLS = 3 * D_RWKV + DECAY_LORA + AAA_LORA + GATE_LORA


def rms_norm(x, g):
    xf = x.astype(jnp.float32)
    y = xf * lax.rsqrt(jnp.mean(xf * xf, axis=-1, keepdims=True) + RMS_EPS)
    return (y * g.astype(jnp.float32)).astype(x.dtype)

def token_shift(p):
    return jnp.pad(p[:, :-1], ((0, 0), (1, 0), (0, 0)))

def wkv7_scan(r, w, k, v, a, b):
    bsz, _, h, n = r.shape

    def step(state, inp):
        r_t, w_t, k_t, v_t, a_t, b_t = inp
        sa = jnp.einsum("bhvk,bhk->bhv", state, a_t)
        state = (state * w_t[:, :, None, :]
                 + sa[..., None] * b_t[:, :, None, :]
                 + v_t[..., None] * k_t[:, :, None, :])
        return state, jnp.einsum("bhvk,bhk->bhv", state, r_t)

    xs = tuple(jnp.moveaxis(t, 1, 0) for t in (r, w, k, v, a, b))
    s0 = jnp.zeros((bsz, h, n, n), jnp.float32)
    _, ys = lax.scan(step, s0, xs)
    return jnp.moveaxis(ys, 0, 1)

def rwkv7_branch(r, k, v, wd, ad, gd, w0, w_lora_w, a0, w_lora_a, w_lora_g,
                 k_k, k_a, r_k, ln_x_w, ln_x_b):
    bsz, s, _ = r.shape
    f32 = jnp.float32
    log_w = -jax.nn.softplus(-(w0 + jnp.tanh(wd) @ w_lora_w)) - 0.5
    decay = jnp.exp(-jnp.exp(log_w.astype(f32)))
    a = jax.nn.sigmoid(a0 + ad @ w_lora_a)
    g = jax.nn.sigmoid(gd) @ w_lora_g

    def heads(t):
        return t.reshape(bsz, s, N_RWKV_HEADS, RWKV_HEAD).astype(f32)

    kk = heads(k * k_k)
    kk = kk / jnp.maximum(jnp.sqrt(jnp.sum(kk * kk, axis=-1, keepdims=True)), 1e-12)
    k = k * (1.0 + (a - 1.0) * k_a)
    rh, kh, vh, ah, wh = heads(r), heads(k), heads(v), heads(a), heads(decay)
    y = wkv7_scan(rh, wh, kh, vh, -kk, kk * ah)
    mu = jnp.mean(y, axis=-1, keepdims=True)
    var = jnp.mean(jnp.square(y - mu), axis=-1, keepdims=True)
    y = (y - mu) * lax.rsqrt(var + LN_X_EPS)
    y = y.reshape(bsz, s, D_RWKV) * ln_x_w.astype(f32) + ln_x_b.astype(f32)
    bonus = jnp.sum(rh * kh * r_k.astype(f32), axis=-1, keepdims=True) * vh
    y = y + bonus.reshape(bsz, s, D_RWKV)
    return y.astype(r.dtype) * g

def short_conv_branch(bg, cg, xc, conv_w):
    u = cg * xc
    y = lax.conv_general_dilated(
        u, conv_w.astype(u.dtype), window_strides=(1,),
        padding=[(CONV_WIDTH - 1, 0)],
        dimension_numbers=("NWC", "WIO", "NWC"),
        feature_group_count=D_CONV)
    return bg * y

def memory_cross_attention(h, mem_n, w_q, w_kv, w_xo):
    bsz, s, _ = h.shape
    n_mem = mem_n.shape[1]
    q = (h @ w_q).reshape(bsz, s, N_XHEADS, XHEAD_DIM)
    k, v = jnp.split(mem_n @ w_kv, 2, axis=-1)
    k = k.reshape(bsz, n_mem, N_XHEADS, XHEAD_DIM)
    v = v.reshape(bsz, n_mem, N_XHEADS, XHEAD_DIM)
    scores = jnp.einsum("bshd,bmhd->bhsm", q, k).astype(jnp.float32) / math.sqrt(XHEAD_DIM)
    probs = jax.nn.softmax(scores, axis=-1).astype(v.dtype)
    o = jnp.einsum("bhsm,bmhd->bshd", probs, v).reshape(bsz, s, D_MODEL)
    return o @ w_xo

def second_inputs(seed: int = 0) -> dict:
    key = jax.random.key(seed)
    ks = jax.random.split(key, 32)
    it = iter(range(32))
    f32 = jnp.float32
    L = DEPTH

    def nrm(shape, scale):
        return scale * jax.random.normal(ks[next(it)], shape, f32)

    def gain(shape):
        return 1.0 + 0.05 * jax.random.normal(ks[next(it)], shape, f32)

    return {
        "x": nrm((BATCH, SEQ, D_MODEL), 1.0),
        "mem": nrm((BATCH, N_MEM, D_MODEL), 1.0),
        "norm_mix": gain((L, D_MODEL)),
        "w_in": nrm((L, D_MODEL, D_IN), D_MODEL ** -0.5),
        "b_gate": nrm((L, 2 * D_MODEL), 0.01),
        "mu_shift": jax.random.uniform(ks[next(it)], (L, RWKV_COLS), f32),
        "w0": jax.random.uniform(ks[next(it)], (L, D_RWKV), f32, -6.0, -1.0),
        "w_lora_w": nrm((L, DECAY_LORA, D_RWKV), 0.1 * DECAY_LORA ** -0.5),
        "a0": nrm((L, D_RWKV), 0.1),
        "w_lora_a": nrm((L, AAA_LORA, D_RWKV), AAA_LORA ** -0.5),
        "w_lora_g": nrm((L, GATE_LORA, D_RWKV), GATE_LORA ** -0.5),
        "k_k": 0.85 + nrm((L, D_RWKV), 0.05),
        "k_a": gain((L, D_RWKV)),
        "r_k": nrm((L, N_RWKV_HEADS, RWKV_HEAD), 0.1),
        "ln_x_w": gain((L, D_RWKV)),
        "ln_x_b": nrm((L, D_RWKV), 0.01),
        "conv_w": nrm((L, CONV_WIDTH, 1, D_CONV), CONV_WIDTH ** -0.5),
        "w_proj_a": nrm((L, D_RWKV, D_MODEL), D_RWKV ** -0.5),
        "w_proj_b": nrm((L, D_CONV, D_MODEL), D_CONV ** -0.5),
        "w_out_mix": nrm((L, D_MODEL, D_MODEL), D_MODEL ** -0.5),
        "norm_xattn": gain((L, D_MODEL)),
        "norm_mem": gain((L, D_MODEL)),
        "w_q": nrm((L, D_MODEL, D_MODEL), D_MODEL ** -0.5),
        "w_kv": nrm((L, D_MODEL, 2 * D_MODEL), D_MODEL ** -0.5),
        "w_xo": nrm((L, D_MODEL, D_MODEL), D_MODEL ** -0.5),
        "norm_mlp": gain((L, D_MODEL)),
        "w_up": nrm((L, D_MODEL, D_FF), D_MODEL ** -0.5),
        "w_down": nrm((L, D_FF, D_MODEL), D_FF ** -0.5),
        "norm_final": gain((D_MODEL,)),
    }

def second_block(x, mem, norm_mix, w_in, b_gate, mu_shift, w0, w_lora_w, a0, w_lora_a,
              w_lora_g, k_k, k_a, r_k, ln_x_w, ln_x_b, conv_w, w_proj_a, w_proj_b,
              w_out_mix, norm_xattn, norm_mem, w_q, w_kv, w_xo, norm_mlp, w_up,
              w_down, norm_final):
    offsets = np.cumsum(SPLITS)[:-1].tolist()
    for i in range(DEPTH):
        h = rms_norm(x, norm_mix[i])
        p = h @ w_in[i]
        p_rw = p[..., :RWKV_COLS]
        p_rw = p_rw + (token_shift(p_rw) - p_rw) * mu_shift[i]
        p = jnp.concatenate([p_rw, p[..., RWKV_COLS:]], axis=-1)
        r, k, v, wd, ad, gd, cb, cc, cx, ga, gb = jnp.split(p, offsets, axis=-1)
        out_a = rwkv7_branch(r, k, v, wd, ad, gd, w0[i], w_lora_w[i], a0[i], w_lora_a[i],
                             w_lora_g[i], k_k[i], k_a[i], r_k[i], ln_x_w[i], ln_x_b[i])
        out_b = short_conv_branch(cb, cc, cx, conv_w[i])
        bg_a, bg_b = jnp.split(b_gate[i], 2)
        merged = (jax.nn.sigmoid(ga + bg_a) * (out_a @ w_proj_a[i])
                  + jax.nn.sigmoid(gb + bg_b) * (out_b @ w_proj_b[i]))
        x = x + merged @ w_out_mix[i]
        mem_n = rms_norm(mem, norm_mem[i])
        x = x + memory_cross_attention(rms_norm(x, norm_xattn[i]), mem_n,
                                       w_q[i], w_kv[i], w_xo[i])
        hm = rms_norm(x, norm_mlp[i])
        x = x + jnp.square(jax.nn.relu(hm @ w_up[i])) @ w_down[i]
    return rms_norm(x, norm_final)


def setup_inputs(seed=0):
    out = dict(first_inputs(seed))
    for name, value in second_inputs(seed + 1).items():
        if name != "x":
            out[name + "_2"] = value
    return out


def reference(
    x, attn_norm_g, w_in, diff_lambda, diff_norm_g, ret_log_decay, ret_norm_g, w_out,
    ffn_norm_g, peer_w_query, peer_sub_keys, peer_u, peer_v, final_norm_g, mem_2, norm_mix_2,
    w_in_2, b_gate_2, mu_shift_2, w0_2, w_lora_w_2, a0_2, w_lora_a_2, w_lora_g_2, k_k_2, k_a_2,
    r_k_2, ln_x_w_2, ln_x_b_2, conv_w_2, w_proj_a_2, w_proj_b_2, w_out_mix_2, norm_xattn_2,
    norm_mem_2, w_q_2, w_kv_2, w_xo_2, norm_mlp_2, w_up_2, w_down_2, norm_final_2,
):
    x = first_block(
        x, attn_norm_g, w_in, diff_lambda, diff_norm_g, ret_log_decay, ret_norm_g, w_out,
        ffn_norm_g, peer_w_query, peer_sub_keys, peer_u, peer_v, final_norm_g,
    )
    return second_block(
        x, mem_2, norm_mix_2, w_in_2, b_gate_2, mu_shift_2, w0_2, w_lora_w_2, a0_2, w_lora_a_2,
        w_lora_g_2, k_k_2, k_a_2, r_k_2, ln_x_w_2, ln_x_b_2, conv_w_2, w_proj_a_2, w_proj_b_2,
        w_out_mix_2, norm_xattn_2, norm_mem_2, w_q_2, w_kv_2, w_xo_2, norm_mlp_2, w_up_2,
        w_down_2, norm_final_2,
    )


_drawn_inputs = setup_inputs


def setup_inputs(seed=0):
    import zlib

    import numpy as np

    out = dict(_drawn_inputs(seed))
    spreads = {}
    factors = {'diff_lambda': 3.791,
     'ret_norm_g': 2.721,
     'b_gate_2': 8.0,
     'w_lora_w_2': 8.0,
     'a0_2': 5.353,
     'k_k_2': 3.568,
     'k_a_2': 3.192,
     'ln_x_w_2': 4.117,
     'ln_x_b_2': 8.0,
     'norm_xattn_2': 8.0,
     'norm_mem_2': 7.927,
     'norm_mlp_2': 6.406}
    for name, (base, spread) in spreads.items():
        noise = np.random.default_rng([zlib.crc32(name.encode()), seed]).standard_normal(out[name].shape)
        drawn = base * np.exp(spread * noise) if base else spread * noise
        out[name] = __import__('jax').numpy.asarray(drawn.astype(out[name].dtype))
    for name, factor in factors.items():
        out[name] = (out[name] * factor).astype(out[name].dtype)
    return out
```

```python
import math

import concourse.bass as bass
from concourse import mybir
from contextlib import ExitStack

F32 = mybir.dt.float32
F32R = mybir.dt.float32r
U32 = mybir.dt.uint32
ALU = mybir.AluOpType
ACT = mybir.ActivationFunctionType
AX = mybir.AxisListType

P = 128
T = 512
TT = T // P
D = 1024
C = D // P
UNIT = C * P
RING = 4
EPS = 1e-6

IN_SLABS = 24
DQ, DK, DV, RQ, RK, RV, RG = 0, 4, 8, 12, 14, 16, 20
HEADS = 4
N_KEYS = 128
DIFF_QK = 64
RET_QK = 64
LAMBDA_INIT = 0.8 - 0.6
PEER_HEADS = 8
TOPK = 16
LOWEST = -3.0e38
LISTS = 2 * PEER_HEADS
PICKS = PEER_HEADS * TOPK
EXPERT_GROUPS = N_KEYS // C
MLP_GROUPS = 4
M = 256
RWKV_SLABS = 15
RWKV_LN_EPS = 64e-5
GT = 64
GBLOCKS = T // GT


class Signal:

    def __init__(self, ctx, nc, name):
        self.sem = ctx.enter_context(nc.semaphore(name))
        self.base = 0

    def at(self, n):
        return n + self.base


class Weights:

    AHEAD = 2

    def __init__(self, ctx, nc, sources):
        self.nc = nc
        self.raw = ctx.enter_context(nc.sbuf_tensor("weights_raw", [P, RING, UNIT], F32))
        self.hi = [ctx.enter_context(nc.sbuf_tensor(f"weights_hi{k}", [P, C, P], F32R)) for k in range(RING)]
        self.lo = [ctx.enter_context(nc.sbuf_tensor(f"weights_lo{k}", [P, C, P], F32R)) for k in range(RING)]
        self.loaded = [Signal(ctx, nc, f"weights_loaded{k}") for k in range(RING)]
        self.hi_ready = Signal(ctx, nc, "weights_hi_ready")
        self.lo_ready = Signal(ctx, nc, "weights_lo_ready")
        self.unit_done = Signal(ctx, nc, "unit_done")
        self.sources = sources
        self.total = sum(n for _, n in sources)
        self.u0 = 0

    def source(self, v):
        for dram, n in self.sources:
            if v < n:
                return dram, v
            v -= n
        raise IndexError

    def done(self, k):
        return k + (self.u0 + RING + 1)

    def load(self, sp, k, slot, dram, index, free=True):
        if free:
            sp.wait_ge(self.lo_ready.sem, k + (self.u0 + 1 - RING))
        sp.dma_start(self.raw[:, slot, :], dram[index]).then_inc(self.loaded[slot].sem, 16)

    def load_first(self, sp):
        for v in range(RING):
            dram, index = self.source(v)
            self.load(sp, v, v, dram, index, free=False)

    def load_stage(self, sp, n):
        first, last = self.u0 + RING, min(self.u0 + RING + n, self.total)
        v = first
        while v < last:
            dram, index = self.source(v)
            run = min(last - v, dram.shape[0] - index)
            if run >= 2 * RING:
                with sp.Fori(0, run // RING) as i:
                    for k in range(RING):
                        self.load(sp, i * RING + (v + k - self.u0), (v + k) % RING, dram, i * RING + (index + k))
                run -= run % RING
            else:
                for k in range(run):
                    self.load(sp, v + k - self.u0, (v + k) % RING, dram, index + k)
            v += run

    def hi_step(self, act, loop, k, per):
        slot = (self.u0 + k) % RING
        turn = (self.u0 + k - slot) // RING + 1
        act.wait_ge(self.loaded[slot].sem, 16 * turn if loop is None else loop * (16 * per // RING) + 16 * turn)
        act.wait_ge(self.unit_done.sem, self.u0 + k + 1 if loop is None else loop * per + (self.u0 + k + 1))
        self.nc.scalar.activation(self.hi[slot][:, :, :], self.raw[:, slot, :].rearrange("p (c n) -> p c n", c=C),
                                  ACT.Copy).then_inc(self.hi_ready.sem, 1)

    def lo_step(self, dve, loop, k, per):
        slot = (self.u0 + k) % RING
        dve.wait_ge(self.hi_ready.sem, self.u0 + k + 1 if loop is None else loop * per + (self.u0 + k + 1))
        self.nc.vector.tensor_tensor(self.lo[slot][:, :, :], self.raw[:, slot, :].rearrange("p (c n) -> p c n", c=C),
                                     self.hi[slot][:, :, :].bitcast(F32), ALU.subtract).then_inc(self.lo_ready.sem, 1)

    def multiply_chunk(self, pe, loop, k, per, out, acts, c):
        slot = (self.u0 + k) % RING
        if c == 0:
            pe.wait_ge(self.lo_ready.sem, loop * per + (self.u0 + k + 1))
        for n, (w, a) in enumerate(((self.hi, acts[0]), (self.hi, acts[1]), (self.lo, acts[0]))):
            mm = self.nc.tensor.matmul(out, w[slot][:, c, :], a[:, c, :], start=c == 0 and n == 0, stop=c == C - 1 and n == 2)
        return mm

    def multiply(self, pe, loop, k, per, out, acts, first=True, last=True, chunks=range(C), tokens=T):
        slot = (self.u0 + k) % RING
        pe.wait_ge(self.lo_ready.sem, self.u0 + k + 1 if loop is None else loop * per + (self.u0 + k + 1))
        hi, lo = acts
        n = 0
        for j, c in enumerate(chunks):
            for w, a in ((self.hi, hi), (self.hi, lo), (self.lo, hi)):
                n += 1
                mm = self.nc.tensor.matmul(out, w[slot][:, c, :], a[:, j, 0:tokens],
                                           start=first and n == 1, stop=last and n == 3 * len(chunks))
        return mm


def build_program(nc, aps, out_t, stop=99):
    (x_t, norm_gains, rope_tables, swap, ident_in, distance, lam_in, diff_gain, ret_decay, ret_gain, keys_t, iota_in,
     conv_taps, gate_bias_in, mem_t) = (aps[n] for n in (
         "x_t", "norm_gains", "rope_tables", "swap", "ident_in", "distance", "lam_in", "diff_gain", "ret_decay", "ret_gain",
         "keys_t", "iota_in", "conv_taps", "gate_bias_in", "mem_t"))
    rwkv = {k[5:]: v for k, v in aps.items() if k.startswith("rwkv_")}
    units = [(v, v.shape[0]) for k, v in aps.items() if k.startswith("u_")]
    ctx = ExitStack()
    with ctx:
        uses = {}

        def fresh(name):
            uses[name] = uses.get(name, 0) + 1
            return name if uses[name] == 1 else f"{name}_{uses[name]}"

        def sb(name, shape, dt=F32, c=None):
            name = fresh(name)
            return (c or ctx).enter_context(nc.sbuf_tensor(name, shape, dt))

        def sig(name):
            return Signal(ctx, nc, name)

        weights = Weights(ctx, nc, units)
        gates_dram = nc.dram_tensor("gates_dram", [GBLOCKS, P, N_KEYS * GT], F32).ap()
        x = sb("x", [P, C, T])
        gains = sb("gains", [P, 8, C])
        ident = sb("ident", [P, P])
        ones = sb("ones", [P, P])
        psum = ctx.enter_context(nc.psum_tensor("psum", [P, 8, T], F32))
        consts_loaded = sig("consts_loaded")
        norm_sq = sig("norm_squares_ready")
        norm_acc = sig("norm_partial_sums_ready")
        norm_sum = sig("norm_sum_ready")
        norm_root = sig("norm_root_ready")
        norm_rstd = sig("norm_rstd_ready")
        norm_y = sig("norm_scaled_ready")
        norm_hi = sig("norm_hi_ready")

        def rms_norm(src, gain, out_f32=None, out_split=None, width=T, before=None):
            with ExitStack() as local, nc.Block() as block:
                sq = sb("norm_squares", [P, 2, width], F32, local)
                acc = sb("norm_sums", [P, 2, width], F32, local)
                rstd = sb("norm_rstd", [P, width], F32, local)
                y = out_f32 if out_f32 is not None else sb("norm_scaled", [P, 2, width], F32, local)
                total = psum[:, 7, 0:width]

                @block.sync
                def _(sp):
                    if before:
                        before(sp)

                @block.scalar
                def _(act):
                    if before:
                        act.wait_ge(consts_loaded.sem, 16 * before.loads)
                    for c in range(C):
                        if c >= 2:
                            act.wait_ge(norm_acc.sem, norm_acc.at(c - 1))
                        nc.scalar.activation(sq[:, c % 2, :], src[:, c, 0:width], ACT.Square).then_inc(norm_sq.sem, 1)
                    act.wait_ge(norm_sum.sem, norm_sum.at(1))
                    nc.scalar.activation(rstd[:], total, ACT.Ln, bias=eps_ap[:, 0:1], scale=1.0 / D).then_inc(norm_root.sem, 1)
                    act.wait_ge(norm_root.sem, norm_root.at(1))
                    nc.scalar.activation(rstd[:], rstd[:], ACT.Exp, scale=-0.5).then_inc(norm_rstd.sem, 1)
                    if out_split:
                        for c in range(C):
                            act.wait_ge(norm_y.sem, norm_y.at(c + 1))
                            nc.scalar.activation(out_split[0][:, c, :], y[:, c % 2, :], ACT.Copy).then_inc(norm_hi.sem, 1)

                @block.tensor
                def _(pe):
                    pe.wait_ge(norm_acc.sem, norm_acc.at(C))
                    nc.tensor.matmul(total, ones[:], acc[:, 1, :], start=True, stop=True).then_inc(norm_sum.sem, 1)

                @block.vector
                def _(dve):
                    for c in range(C):
                        dve.wait_ge(norm_sq.sem, norm_sq.at(c + 1))
                        if c == 0:
                            nc.vector.tensor_copy(acc[:, 0, :], sq[:, 0, :]).then_inc(norm_acc.sem, 1)
                        else:
                            dve.wait_ge(norm_acc.sem, norm_acc.at(c))
                            nc.vector.tensor_tensor(acc[:, c % 2, :], acc[:, (c - 1) % 2, :], sq[:, c % 2, :],
                                                    ALU.add).then_inc(norm_acc.sem, 1)
                    dve.wait_ge(norm_rstd.sem, norm_rstd.at(1))
                    for c in range(C):
                        if out_split and c >= 2:
                            dve.wait_ge(norm_hi.sem, norm_hi.at(c - 1))
                        yc = y[:, c % 2, :] if out_split else y[:, c, 0:width]
                        nc.vector.scalar_tensor_tensor(yc, src[:, c, 0:width], gains[:, gain, c:c + 1], rstd[:],
                                                       ALU.mult, ALU.mult).then_inc(norm_y.sem, 1)
                        if out_split:
                            dve.wait_ge(norm_hi.sem, norm_hi.at(c + 1))
                            nc.vector.tensor_tensor(out_split[1][:, c, :], y[:, c % 2, :],
                                                    out_split[0][:, c, :].bitcast(F32), ALU.subtract)
            for s in (norm_sq, norm_acc, norm_y):
                s.base += C
            if out_split:
                norm_hi.base += C
            for s in (norm_sum, norm_root, norm_rstd):
                s.base += 1

        out_free = sig("product_read")

        def linear(n, acts, evacuate, engine, tokens=T, prologue=False, loop=None):
            w = weights
            loops = n // RING
            rest = range(loops * RING, n)
            u0, base = w.u0, out_free.base
            split_until = w.total - w.AHEAD - u0

            def bank(k):
                return (u0 + k) % 4

            with nc.Block() as block:
                @block.sync
                def _(sp):
                    w.load_stage(sp, n)

                def evac(eng, loop, k):
                    eng.wait_ge(w.unit_done.sem, w.done(k) if loop is None else loop * RING + w.done(k))
                    evacuate(loop, k, psum[:, bank(k), 0:tokens]).then_inc(out_free.sem, 1)

                @block.scalar
                def _(act):
                    if prologue:
                        for k in range(w.AHEAD):
                            w.hi_step(act, None, k, RING)
                    with act.Fori(0, loops) as i:
                        for k in range(RING):
                            w.hi_step(act, i, k + w.AHEAD, RING)
                            if engine == "scalar":
                                evac(act, i, k)
                    for k in rest:
                        if k < split_until:
                            w.hi_step(act, None, k + w.AHEAD, RING)
                        if engine == "scalar":
                            evac(act, None, k)

                @block.vector
                def _(dve):
                    if prologue:
                        for k in range(w.AHEAD):
                            w.lo_step(dve, None, k, RING)
                    with dve.Fori(0, loops) as i:
                        for k in range(RING):
                            w.lo_step(dve, i, k + w.AHEAD, RING)
                            if engine == "vector":
                                evac(dve, i, k)
                    for k in rest:
                        if k < split_until:
                            w.lo_step(dve, None, k + w.AHEAD, RING)
                        if engine == "vector":
                            evac(dve, None, k)

                @block.tensor
                def _(pe):
                    def step(loop, k):
                        pe.wait_ge(out_free.sem, base + k + 1 if loop is None else loop * RING + (base + k + 1))
                        w.multiply(pe, loop, k, RING, psum[:, bank(k), 0:tokens], acts,
                                   tokens=tokens).then_inc(w.unit_done.sem, 1)
                    if prologue:
                        pe.sem_inc(w.unit_done.sem, RING)
                        pe.sem_inc(out_free.sem, RING)
                    with pe.Fori(0, loops) as i:
                        for k in range(RING):
                            step(i, k)
                    for k in rest:
                        step(None, k)
            w.u0 += n
            out_free.base += n

        def at(loop, k):
            return k if loop is None else loop * RING + k

        eps_ap = sb("eps", [P, 1])

        def load_start(sp):
            sp.dma_start(x[:, :, :], x_t).then_inc(consts_loaded.sem, 16)
            sp.dma_start(gains[:, :, :], norm_gains).then_inc(consts_loaded.sem, 16)
            weights.load_first(sp)
            sp.dma_start(ident[:], ident_in).then_inc(consts_loaded.sem, 16)
        load_start.loads = 3

        ones_set = sig("ones_set")
        with nc.Block() as block:
            @block.gpsimd
            def _(pool):
                nc.gpsimd.memset(ones[:], 1.0).then_inc(ones_set.sem, 1)
                nc.gpsimd.memset(eps_ap[:], EPS).then_inc(ones_set.sem, 1)

        mix_stack = ExitStack()
        ctx.enter_context(mix_stack)
        proj = sb("projections", [P, IN_SLABS, T], F32, mix_stack)
        act_stack = ExitStack()
        act_hi = sb("act_hi_a", [P, C, T], F32R, act_stack)
        act_lo = sb("act_lo_a", [P, C, T], F32R, act_stack)
        rms_norm(x, 0, out_split=(act_hi, act_lo), before=load_start)

        linear(IN_SLABS, (act_hi, act_lo),
               lambda loop, k, bank: nc.scalar.activation(proj[:, at(loop, k), :], bank, ACT.Copy),
               "scalar", prologue=True)
        act_stack.close()

        gn_mean = sig("head_mean_ready")
        gn_centred = sig("head_centred")
        gn_square = sig("head_square_ready")
        gn_var = sig("head_variance_ready")
        gn_floor = sig("head_variance_floored")
        gn_log = sig("head_log_ready")
        gn_rstd = sig("head_rstd_ready")
        gn_out = sig("head_scaled")

        def head_norm(src, average, eps, center, floor=None):
            with ExitStack() as local, nc.Block() as block:
                sq = sb("head_squares", [P, 2, T], F32, local)
                rstd = sb("head_rstd", [P, 2, T], F32, local)

                @block.tensor
                def _(pe):
                    if center:
                        for j in range(4):
                            nc.tensor.matmul(psum[:, j, :], average, src[:, j, :], start=True, stop=True).then_inc(gn_mean.sem, 1)
                    for j in range(4):
                        pe.wait_ge(gn_square.sem, gn_square.at(j + 1))
                        nc.tensor.matmul(psum[:, 4 + j, :], average, sq[:, j % 2, :], start=True, stop=True).then_inc(gn_var.sem, 1)

                @block.scalar
                def _(act):
                    def square(j):
                        if center:
                            act.wait_ge(gn_centred.sem, gn_centred.at(j + 1))
                        if j >= 2:
                            act.wait_ge(gn_var.sem, gn_var.at(j - 1))
                        nc.scalar.activation(sq[:, j % 2, :], src[:, j, :], ACT.Square).then_inc(gn_square.sem, 1)
                    square(0)
                    for j in range(4):
                        if j < 3:
                            square(j + 1)
                        if floor is not None:
                            act.wait_ge(gn_floor.sem, gn_floor.at(j + 1))
                        else:
                            act.wait_ge(gn_var.sem, gn_var.at(j + 1))
                            if j >= 2:
                                act.wait_ge(gn_out.sem, gn_out.at(j - 1))
                        source = rstd[:, j % 2, :] if floor is not None else psum[:, 4 + j, :]
                        nc.scalar.activation(rstd[:, j % 2, :], source, ACT.Ln, bias=eps, scale=1.0).then_inc(gn_log.sem, 1)
                        act.wait_ge(gn_log.sem, gn_log.at(j + 1))
                        nc.scalar.activation(rstd[:, j % 2, :], rstd[:, j % 2, :], ACT.Exp, scale=-0.5).then_inc(gn_rstd.sem, 1)

                @block.vector
                def _(dve):
                    if center:
                        for j in range(4):
                            dve.wait_ge(gn_mean.sem, gn_mean.at(j + 1))
                            nc.vector.tensor_tensor(src[:, j, :], src[:, j, :], psum[:, j, :], ALU.subtract).then_inc(gn_centred.sem, 1)

                    def floored(j):
                        dve.wait_ge(gn_var.sem, gn_var.at(j + 1))
                        if j >= 2:
                            dve.wait_ge(gn_out.sem, gn_out.at(j - 1))
                        nc.vector.tensor_scalar(rstd[:, j % 2, :], psum[:, 4 + j, :], floor, None, ALU.max).then_inc(gn_floor.sem, 1)
                    if floor is not None:
                        floored(0)
                    for j in range(4):
                        if floor is not None and j < 3:
                            floored(j + 1)
                        dve.wait_ge(gn_rstd.sem, gn_rstd.at(j + 1))
                        nc.vector.tensor_tensor(src[:, j, :], src[:, j, :], rstd[:, j % 2, :], ALU.mult).then_inc(gn_out.sem, 1)
            for s, used in ((gn_mean, center), (gn_centred, center), (gn_square, True), (gn_var, True), (gn_floor, floor is not None),
                            (gn_log, True), (gn_rstd, True), (gn_out, True)):
                s.base += 4 * used

        split_hi_ready = sig("split_hi_ready")

        def split(slabs, hi, lo, at_slab=0):
            with nc.Block() as block:
                @block.scalar
                def _(act):
                    for j, (src, gain) in enumerate(slabs):
                        nc.scalar.activation(hi[:, at_slab + j, :], src, ACT.Copy, scale=gain).then_inc(split_hi_ready.sem, 1)

                @block.vector
                def _(dve):
                    for j, (src, gain) in enumerate(slabs):
                        dve.wait_ge(split_hi_ready.sem, split_hi_ready.at(j + 1))
                        nc.vector.scalar_tensor_tensor(lo[:, at_slab + j, :], src, gain, hi[:, at_slab + j, :].bitcast(F32),
                                                       ALU.mult, ALU.subtract)
            split_hi_ready.base += len(slabs)

        mix_hi = sb("mix_hi", [P, C, T], F32R, mix_stack)
        mix_lo = sb("mix_lo", [P, C, T], F32R, mix_stack)
        v_tok = sb("values_by_token", [P, 2 * HEADS, T], F32, mix_stack)
        average128 = sb("average128", [P, P], F32, mix_stack)
        small = sb("attention_scalars", [P, 64], F32, mix_stack)
        neg_lam, gain_d, gain_r, lgf = small[:, 0:1], small[:, 4:5], small[:, 8:12], small[:, 16:24]
        lam_v = sb("lambda_vectors", [P, 4, 64], F32, mix_stack)
        lam_loaded = sig("attention_scalars_loaded")
        tables_loaded = sig("tables_loaded")
        rope_swapped, rope_cos, rope_sin, rope_done = (sig(n) for n in ("rope_swapped", "rope_cos", "rope_sin", "rope_done"))
        v_turned = sig("values_transposed")
        v_copied = sig("values_copied")
        lam_step = sig("lambda_step")
        lam_exp = sig("lambda_exp_ready")
        rotary = [(n, 0) for n in range(DQ, DV)] + [(n, 1) for n in range(RQ, RV)]
        values = list(range(DV, DV + HEADS)) + list(range(RV, RV + HEADS))
        with ExitStack() as local, nc.Block() as block:
            tables = sb("rope_tables_sb", [P, 4, T], F32, local)
            swaps = sb("rope_swaps", [P, 2, P], F32, local)
            by_cos = sb("rope_by_cos", [P, 2, T], F32, local)
            by_sin = sb("rope_by_sin", [P, 2, T], F32, local)

            @block.sync
            def _(sp):
                sp.dma_start(tables[:, :, :], rope_tables).then_inc(tables_loaded.sem, 16)
                sp.dma_start(swaps[:, :, :], swap).then_inc(tables_loaded.sem, 16)
                sp.dma_start(lam_v[:, :, :], lam_in).then_inc(lam_loaded.sem, 16)
                sp.dma_start(small[:, 4:5], diff_gain).then_inc(lam_loaded.sem, 16)
                sp.dma_start(small[:, 8:12], ret_gain).then_inc(lam_loaded.sem, 16)
                sp.dma_start(small[:, 16:24], ret_decay).then_inc(lam_loaded.sem, 16)

            @block.tensor
            def _(pe):
                for j, n in enumerate(values):
                    if j >= 2:
                        pe.wait_ge(v_copied.sem, j - 1)
                    for tile in range(TT):
                        mm = nc.tensor.transpose(psum[:, 4 + j % 2, tile * P:(tile + 1) * P], proj[:, n, tile * P:(tile + 1) * P], ident[:])
                    mm.then_inc(v_turned.sem, 1)
                pe.wait_ge(tables_loaded.sem, 32)
                for j, (n, kind) in enumerate(rotary):
                    if j >= 2:
                        pe.wait_ge(rope_sin.sem, j - 1)
                    nc.tensor.matmul(psum[:, j % 2, :], swaps[:, kind, :], proj[:, n, :], start=True, stop=True).then_inc(rope_swapped.sem, 1)

            @block.scalar
            def _(act):
                for j in range(len(values)):
                    act.wait_ge(v_turned.sem, j + 1)
                    nc.scalar.activation(v_tok[:, j, :], psum[:, 4 + j % 2, :], ACT.Copy).then_inc(v_copied.sem, 1)
                act.wait_ge(lam_loaded.sem, 64)
                act.wait_ge(lam_step.sem, 2)
                nc.scalar.activation(small[:, 2:4], small[:, 2:4], ACT.Exp).then_inc(lam_exp.sem, 1)
                nc.scalar.activation(lgf, lgf, ACT.Exp).then_inc(lam_exp.sem, 1)

            @block.gpsimd
            def _(pool):
                nc.gpsimd.memset(average128[:], 1.0 / P)
                pool.wait_ge(tables_loaded.sem, 32)
                for j, (n, kind) in enumerate(rotary):
                    if j >= 2:
                        pool.wait_ge(rope_done.sem, j - 1)
                    nc.gpsimd.tensor_tensor(by_cos[:, j % 2, :], proj[:, n, :], tables[:, 2 * kind, :], ALU.mult).then_inc(rope_cos.sem, 1)

            @block.vector
            def _(dve):
                for j, (n, kind) in enumerate(rotary):
                    dve.wait_ge(rope_swapped.sem, j + 1)
                    if j == 0:
                        dve.wait_ge(tables_loaded.sem, 32)
                    if j >= 2:
                        dve.wait_ge(rope_done.sem, j - 1)
                    nc.vector.tensor_tensor(by_sin[:, j % 2, :], psum[:, j % 2, :], tables[:, 2 * kind + 1, :], ALU.mult).then_inc(rope_sin.sem, 1)
                    dve.wait_ge(rope_cos.sem, j + 1)
                    dve.wait_ge(rope_sin.sem, j + 1)
                    nc.vector.tensor_tensor(proj[:, n, :], by_cos[:, j % 2, :], by_sin[:, j % 2, :], ALU.add).then_inc(rope_done.sem, 1)
                dve.wait_ge(lam_loaded.sem, 64)
                nc.vector.tensor_tensor(lam_v[:, 0::2, :], lam_v[:, 0::2, :], lam_v[:, 1::2, :], ALU.mult).then_inc(lam_step.sem, 1)
                dve.wait_ge(lam_step.sem, 1)
                nc.vector.tensor_reduce(small[:, 2:4], lam_v[:, 0::2, :], AX.X, ALU.add).then_inc(lam_step.sem, 1)
                dve.wait_ge(lam_exp.sem, 2)
                nc.vector.tensor_tensor(neg_lam, small[:, 3:4], small[:, 2:3], ALU.subtract).then_inc(lam_step.sem, 1)
                dve.wait_ge(lam_step.sem, 3)
                nc.vector.tensor_scalar(neg_lam, neg_lam, -LAMBDA_INIT, None, ALU.add)
                nc.vector.tensor_scalar(gain_d, gain_d, 1.0 - LAMBDA_INIT, None, ALU.mult)
                nc.vector.tensor_scalar(lgf, lgf, -1.0, None, ALU.mult)

        scored, maxed, neg_maxed, exped = (sig(n) for n in ("diff_scores_ready", "diff_max_ready", "diff_neg_max_ready", "diff_exp_ready"))
        inv_ready, scaled0, combined = (sig(n) for n in ("diff_inverse_sum_ready", "diff_first_map_scaled", "diff_maps_combined"))
        turned, turned_read, mixed, mixed_read = (sig(n) for n in ("diff_map_transposed", "diff_map_copied", "diff_out_ready", "diff_out_copied"))
        heads_out = sb("diff_heads_out", [P, HEADS, T], F32, mix_stack)
        scale = DIFF_QK ** -0.5
        steps = HEADS * TT
        with ExitStack() as local, nc.Block() as block:
            probs = sb("diff_probs", [P, 2, 2, T], F32, local)
            amap = sb("diff_map", [P, 2, T], F32, local)
            amap_t = sb("diff_map_t", [P, 2, TT, T], F32, local)
            stats = sb("diff_stats", [P, steps, 8], F32, local)

            @block.tensor
            def _(pe):
                def scores(it):
                    h, q = divmod(it, TT)
                    if it >= 2:
                        pe.wait_ge(exped.sem, 2 * (it - 1))
                    for m in range(2):
                        rows = slice(64 * m, 64 * m + 64)
                        nc.tensor.matmul(psum[:, 2 * (it % 2) + m, :], proj[rows, DQ + h, q * P:(q + 1) * P],
                                         proj[rows, DK + h, :], start=True, stop=True).then_inc(scored.sem, 1)
                scores(0)
                for it in range(steps):
                    h, q = divmod(it, TT)
                    if it + 1 < steps:
                        scores(it + 1)
                    pe.wait_ge(combined.sem, it + 1)
                    if it >= 2:
                        pe.wait_ge(turned_read.sem, it - 1)
                    for kt in range(TT):
                        mm = nc.tensor.transpose(psum[:, 4 + it % 2, kt * P:(kt + 1) * P], amap[:, it % 2, kt * P:(kt + 1) * P], ident[:])
                    mm.then_inc(turned.sem, 1)
                    if q == TT - 1:
                        pe.wait_ge(turned_read.sem, it + 1)
                        if h >= 2:
                            pe.wait_ge(mixed_read.sem, h - 1)
                        for kt in range(TT):
                            mm = nc.tensor.matmul(psum[:, 6 + h % 2, :], v_tok[:, h, kt * P:(kt + 1) * P],
                                                  amap_t[:, h % 2, kt, :], start=kt == 0, stop=kt == TT - 1)
                        mm.then_inc(mixed.sem, 1)

            @block.scalar
            def _(act):
                def exps(it):
                    act.wait_ge(neg_maxed.sem, it + 1)
                    if it >= 2:
                        act.wait_ge(combined.sem, it - 1)
                    for m in range(2):
                        nc.scalar.activation(probs[:, it % 2, m, :], psum[:, 2 * (it % 2) + m, :], ACT.Exp, bias=stats[:, it, 2 + m:3 + m],
                                             scale=scale, accum_out=stats[:, it, 4 + m:5 + m]).then_inc(exped.sem, 1)
                exps(0)
                for it in range(steps):
                    h, q = divmod(it, TT)
                    if it + 1 < steps:
                        exps(it + 1)
                    act.wait_ge(turned.sem, it + 1)
                    if h >= 2:
                        act.wait_ge(mixed.sem, h - 1)
                    nc.scalar.activation(amap_t[:, h % 2, :, q * P:(q + 1) * P], psum[:, 4 + it % 2, :].rearrange("p (k q) -> p k q", k=TT),
                                         ACT.Copy).then_inc(turned_read.sem, 1)
                    if q == TT - 1:
                        act.wait_ge(mixed.sem, h + 1)
                        nc.scalar.activation(heads_out[:, h, :], psum[:, 6 + h % 2, :], ACT.Copy).then_inc(mixed_read.sem, 1)

            @block.vector
            def _(dve):
                def maxima(it):
                    dve.wait_ge(scored.sem, 2 * (it + 1))
                    nc.vector.tensor_reduce(stats[:, it, 0:2], psum[:, 2 * (it % 2):2 * (it % 2) + 2, :], AX.X, ALU.max).then_inc(maxed.sem, 1)
                    dve.wait_ge(maxed.sem, it + 1)
                    nc.vector.tensor_scalar(stats[:, it, 2:4], stats[:, it, 0:2], -scale, None, ALU.mult).then_inc(neg_maxed.sem, 1)
                maxima(0)
                for it in range(steps):
                    if it + 1 < steps:
                        maxima(it + 1)
                    dve.wait_ge(exped.sem, 2 * (it + 1))
                    nc.vector.reciprocal(stats[:, it, 6:8], stats[:, it, 4:6]).then_inc(inv_ready.sem, 1)
                    dve.wait_ge(inv_ready.sem, 2 * it + 1)
                    nc.vector.tensor_tensor(stats[:, it, 7:8], stats[:, it, 7:8], neg_lam, ALU.mult).then_inc(inv_ready.sem, 1)
                    nc.vector.tensor_scalar(probs[:, it % 2, 0, :], probs[:, it % 2, 0, :], stats[:, it, 6:7], None, ALU.mult).then_inc(scaled0.sem, 1)
                    dve.wait_ge(inv_ready.sem, 2 * it + 2)
                    dve.wait_ge(scaled0.sem, it + 1)
                    if it >= 2:
                        dve.wait_ge(turned.sem, it - 1)
                    nc.vector.scalar_tensor_tensor(amap[:, it % 2, :], probs[:, it % 2, 1, :], stats[:, it, 7:8], probs[:, it % 2, 0, :],
                                                   ALU.mult, ALU.add).then_inc(combined.sem, 1)

        head_norm(heads_out, average128[:], eps_ap[:, 0:1], center=False)
        split([(heads_out[:, h, :], gain_d) for h in range(HEADS)], mix_hi, mix_lo)

        dist_loaded, arg0_ready, arg_ready, decay_ready = (sig(n) for n in ("distances_loaded", "decay_half_ready", "decay_log_ready", "decay_ready"))
        ret_scored, ret_decayed, ret_mixed, ret_read = (sig(n) for n in ("ret_scores_ready", "ret_scores_decayed", "ret_out_ready", "ret_out_copied"))
        gate_ready = sig("ret_gate_ready")
        SPAN = T + (TT - 1) * P
        with ExitStack() as local, nc.Block() as block:
            dist = sb("ret_distances", [P, 2, SPAN], F32, local)
            args = sb("ret_decay_log", [P, 2, SPAN], F32, local)
            decay = sb("ret_decay", [P, 2, SPAN], F32, local)
            weighed = sb("ret_scores", [P, 4, T], F32, local)

            @block.sync
            def _(sp):
                sp.dma_start(dist[:, :, :], distance).then_inc(dist_loaded.sem, 16)

            @block.tensor
            def _(pe):
                def scores(it):
                    h, kt = divmod(it, TT)
                    rows = slice(64 * (h % 2), 64 * (h % 2) + 64)
                    if it >= 4:
                        pe.wait_ge(ret_decayed.sem, it - 3)
                    nc.tensor.matmul(psum[:, it % 4, :], proj[rows, RK + h // 2, kt * P:(kt + 1) * P], proj[rows, RQ + h // 2, :],
                                     start=True, stop=True).then_inc(ret_scored.sem, 1)
                scores(0)
                scores(1)
                for it in range(steps):
                    h, kt = divmod(it, TT)
                    if it + 2 < steps:
                        scores(it + 2)
                    pe.wait_ge(ret_decayed.sem, it + 1)
                    if kt == 0 and h >= 2:
                        pe.wait_ge(ret_read.sem, h - 1)
                    nc.tensor.matmul(psum[:, 4 + h % 2, :], v_tok[:, HEADS + h, kt * P:(kt + 1) * P], weighed[:, it % 4, :],
                                     start=kt == 0, stop=kt == TT - 1).then_inc(ret_mixed.sem, 1)

            @block.scalar
            def _(act):
                for h in range(HEADS):
                    act.wait_ge(arg_ready.sem, h + 1)
                    if h >= 2:
                        act.wait_ge(ret_decayed.sem, TT * (h - 1))
                    nc.scalar.activation(decay[:, h % 2, :], args[:, h % 2, :], ACT.Exp).then_inc(decay_ready.sem, 1)
                    if h >= 1:
                        act.wait_ge(ret_mixed.sem, TT * h)
                        nc.scalar.activation(heads_out[:, h - 1, :], psum[:, 4 + (h - 1) % 2, :], ACT.Copy).then_inc(ret_read.sem, 1)
                act.wait_ge(ret_mixed.sem, TT * HEADS)
                nc.scalar.activation(heads_out[:, HEADS - 1, :], psum[:, 4 + (HEADS - 1) % 2, :], ACT.Copy).then_inc(ret_read.sem, 1)
                for h in range(HEADS):
                    nc.scalar.activation(proj[:, RG + h, :], proj[:, RG + h, :], ACT.Silu)

            @block.vector
            def _(dve):
                dve.wait_ge(dist_loaded.sem, 16)

                def log_decay(h):
                    if h >= 2:
                        dve.wait_ge(decay_ready.sem, h - 1)
                    nc.vector.tensor_scalar(args[:, h % 2, :], dist[:, 0, :], lgf[:, h:h + 1], None, ALU.mult).then_inc(arg0_ready.sem, 1)
                    dve.wait_ge(arg0_ready.sem, h + 1)
                    nc.vector.scalar_tensor_tensor(args[:, h % 2, :], dist[:, 1, :], lgf[:, HEADS + h:HEADS + h + 1], args[:, h % 2, :],
                                                   ALU.mult, ALU.add).then_inc(arg_ready.sem, 1)
                log_decay(0)
                for it in range(steps):
                    h, kt = divmod(it, TT)
                    if kt == 0 and h + 1 < HEADS:
                        log_decay(h + 1)
                    dve.wait_ge(ret_scored.sem, it + 1)
                    dve.wait_ge(decay_ready.sem, h + 1)
                    if it >= 4:
                        dve.wait_ge(ret_mixed.sem, it - 3)
                    first = (TT - 1 - kt) * P
                    nc.vector.scalar_tensor_tensor(weighed[:, it % 4, :], psum[:, it % 4, :], RET_QK ** -0.5, decay[:, h % 2, first:first + T],
                                                   ALU.mult, ALU.mult).then_inc(ret_decayed.sem, 1)

        head_norm(heads_out, average128[:], eps_ap[:, 0:1], center=True)
        with nc.Block() as block:
            @block.vector
            def _(dve):
                for h in range(HEADS):
                    nc.vector.tensor_tensor(heads_out[:, h, :], heads_out[:, h, :], proj[:, RG + h, :], ALU.mult)
        split([(heads_out[:, h, :], gain_r[:, h:h + 1]) for h in range(HEADS)], mix_hi, mix_lo, HEADS)

        linear(C, (mix_hi, mix_lo),
               lambda loop, k, bank: nc.vector.tensor_tensor(x[:, at(loop, k), :], x[:, at(loop, k), :], bank, ALU.add), "vector")
        mix_stack.close()
        if stop == 1:
            return

        peer_stack = ExitStack()
        ctx.enter_context(peer_stack)
        act_hi = sb("act_hi", [P, C, T], F32R, peer_stack)
        act_lo = sb("act_lo", [P, C, T], F32R, peer_stack)
        rms_norm(x, 1, out_split=(act_hi, act_lo))
        picks_t = sb("picks_t", [P, 3, T], F32, peer_stack)
        iota = sb("iota", [P, P], F32, peer_stack)
        peer_local = ExitStack()
        queries = sb("queries", [P, LISTS, T], F32, peer_local)
        linear(LISTS, (act_hi, act_lo),
               lambda loop, k, bank: nc.scalar.activation(queries[:, at(loop, k), :], bank, ACT.Copy), "scalar")

        keys_loaded, list_scored, list_copied = sig("keys_loaded"), sig("peer_scores_ready"), sig("peer_scores_copied")
        top, choose, second, first_j = sig("top_step"), sig("choice_step"), sig("second_key_step"), sig("second_key_input")
        gate_inv = sig("gate_inverse_ready")
        gate_exp, picks_turned, picks_copied = sig("gate_exp_ready"), sig("picks_transposed"), sig("picks_copied")
        TOP_STEPS = 5 * LISTS + 5 * PEER_HEADS + 1
        CHOOSE_STEPS = 11
        with peer_local, nc.Block() as block:
            local = peer_local
            keys = sb("keys", [P, LISTS, P], F32, local)
            scores_sb = sb("peer_scores", [P, 2, LISTS, P], F32, local)
            rest_sb = sb("peer_scores_rest", [P, LISTS, P], F32, local)
            top_s = sb("top_scores", [P, LISTS, TOPK], F32, local)
            top_i = sb("top_keys", [P, LISTS, TOPK], U32, local)
            top_f = sb("top_keys_f32", [P, LISTS, TOPK], F32, local)
            cand = sb("candidates", [P, PEER_HEADS, TOPK * TOPK], F32, local)
            cand_rest = sb("candidates_rest", [P, PEER_HEADS, TOPK * TOPK], F32, local)
            best = sb("best_scores", [P, PEER_HEADS, TOPK], F32, local)
            place = sb("best_places", [P, PICKS], U32, local)
            place_a = sb("best_first", [P, PICKS], U32, local)
            place_b = sb("best_second", [P, PICKS], U32, local)
            places = sb("best_places_f32", [P, 2, PICKS], F32, local)
            hot = sb("place_one_hot", [P, 2, PICKS, TOPK], F32, local)
            picks = sb("picks", [P, 3, PICKS], F32, local)
            gate_sum = sb("gate_sum", [P, 2, PEER_HEADS], F32, local)

            @block.sync
            def _(sp):
                sp.dma_start(keys[:, :, :], keys_t).then_inc(keys_loaded.sem, 16)
                sp.dma_start(iota[:, :], iota_in).then_inc(keys_loaded.sem, 16)

            @block.tensor
            def _(pe):
                pe.wait_ge(keys_loaded.sem, 32)

                def lists(tile):
                    if tile:
                        pe.wait_ge(list_copied.sem, tile)
                    for l in range(LISTS):
                        mm = nc.tensor.matmul(psum[:, l // 4, (l % 4) * P:(l % 4 + 1) * P], queries[:, l, tile * P:(tile + 1) * P],
                                              keys[:, l, :], start=True, stop=True)
                    mm.then_inc(list_scored.sem, 1)
                lists(0)
                for tile in range(TT):
                    if tile + 1 < TT:
                        lists(tile + 1)
                    pe.wait_ge(choose.sem, CHOOSE_STEPS * (tile + 1))
                    if tile:
                        pe.wait_ge(picks_copied.sem, tile)
                    for r in range(3):
                        mm = nc.tensor.transpose(psum[:, 4, r * P:(r + 1) * P], picks[:, r, :], ident[:])
                    mm.then_inc(picks_turned.sem, 1)

            @block.scalar
            def _(act):
                def copy_scores(tile):
                    act.wait_ge(list_scored.sem, tile + 1)
                    if tile >= 2:
                        act.wait_ge(top.sem, TOP_STEPS * (tile - 2) + 4 * LISTS)
                    nc.scalar.activation(scores_sb[:, tile % 2, :, :], psum[:, 0:4, :].rearrange("p b (l n) -> p (b l) n", n=P),
                                         ACT.Copy).then_inc(list_copied.sem, 1)
                copy_scores(0)
                for tile in range(TT):
                    if tile + 1 < TT:
                        copy_scores(tile + 1)
                    act.wait_ge(choose.sem, CHOOSE_STEPS * tile + 1)
                    nc.scalar.activation(picks[:, 2, :], picks[:, 2, :], ACT.Exp).then_inc(gate_exp.sem, 1)
                    act.wait_ge(picks_turned.sem, tile + 1)
                    nc.scalar.activation(picks_t[:, :, tile * P:(tile + 1) * P], psum[:, 4, 0:3 * P].rearrange("p (r t) -> p r t", r=3),
                                         ACT.Copy).then_inc(picks_copied.sem, 1)

            def by_keys(eng, side):
                hot_h = hot[:, side, :, :].rearrange("p (h k) a -> p h k a", h=PEER_HEADS)
                keys_h = top_f[:, side::2, :].unsqueeze(2).to_broadcast([P, PEER_HEADS, TOPK, TOPK])
                return eng.tensor_tensor(hot_h, hot_h, keys_h, ALU.mult)

            @block.gpsimd
            def _(pool):
                for tile in range(TT):
                    pool.wait_ge(first_j.sem, tile + 1)
                    by_keys(nc.gpsimd, 1).then_inc(second.sem, 1)

            @block.vector
            def _(dve):
                dve.wait_ge(keys_loaded.sem, 32)
                for tile in range(TT):
                    n0 = TOP_STEPS * tile
                    dve.wait_ge(list_copied.sem, tile + 1)
                    if tile:
                        dve.wait_ge(picks_turned.sem, tile)
                    s = scores_sb[:, tile % 2, :, :]
                    for l in range(LISTS):
                        nc.vector.max(top_s[:, l, 0:8], s[:, l, :]).then_inc(top.sem, 1)
                    for l in range(LISTS):
                        dve.wait_ge(top.sem, n0 + l + 1)
                        nc.vector.match_replace(rest_sb[:, l, :], top_s[:, l, 0:8], s[:, l, :], LOWEST).then_inc(top.sem, 1)
                    for l in range(LISTS):
                        nc.vector.max_index(top_i[:, l, 0:8], top_s[:, l, 0:8], s[:, l, :]).then_inc(top.sem, 1)
                    for l in range(LISTS):
                        dve.wait_ge(top.sem, n0 + LISTS + l + 1)
                        nc.vector.max(top_s[:, l, 8:16], rest_sb[:, l, :]).then_inc(top.sem, 1)
                    for l in range(LISTS):
                        dve.wait_ge(top.sem, n0 + 3 * LISTS + l + 1)
                        nc.vector.max_index(top_i[:, l, 8:16], top_s[:, l, 8:16], rest_sb[:, l, :]).then_inc(top.sem, 1)
                    n1 = n0 + 5 * LISTS
                    pairs = cand[:, :, :].rearrange("p h (a b) -> p h a b", a=TOPK)
                    nc.vector.tensor_tensor(pairs, top_s[:, 0::2, :].unsqueeze(3).to_broadcast([P, PEER_HEADS, TOPK, TOPK]),
                                            top_s[:, 1::2, :].unsqueeze(2).to_broadcast([P, PEER_HEADS, TOPK, TOPK]), ALU.add).then_inc(top.sem, 1)
                    dve.wait_ge(top.sem, n1 + 1)
                    for h in range(PEER_HEADS):
                        nc.vector.max(best[:, h, 0:8], cand[:, h, :]).then_inc(top.sem, 1)
                    for h in range(PEER_HEADS):
                        dve.wait_ge(top.sem, n1 + 1 + h + 1)
                        nc.vector.match_replace(cand_rest[:, h, :], best[:, h, 0:8], cand[:, h, :], LOWEST).then_inc(top.sem, 1)
                    for h in range(PEER_HEADS):
                        nc.vector.max_index(place[:, h * TOPK:h * TOPK + 8], best[:, h, 0:8], cand[:, h, :]).then_inc(top.sem, 1)
                    for h in range(PEER_HEADS):
                        dve.wait_ge(top.sem, n1 + 1 + PEER_HEADS + h + 1)
                        nc.vector.max(best[:, h, 8:16], cand_rest[:, h, :]).then_inc(top.sem, 1)
                    for h in range(PEER_HEADS):
                        dve.wait_ge(top.sem, n1 + 1 + 3 * PEER_HEADS + h + 1)
                        nc.vector.max_index(place[:, h * TOPK + 8:(h + 1) * TOPK], best[:, h, 8:16], cand_rest[:, h, :]).then_inc(top.sem, 1)
                    m0 = CHOOSE_STEPS * tile
                    gates = picks[:, 2, :].rearrange("p (h k) -> p h k", h=PEER_HEADS)
                    nc.vector.tensor_tensor(gates, best[:, :, :], best[:, :, 0:1].to_broadcast([P, PEER_HEADS, TOPK]), ALU.subtract).then_inc(choose.sem, 1)
                    dve.wait_ge(top.sem, n0 + TOP_STEPS)
                    nc.vector.tensor_scalar(place_a[:], place[:], 4, None, ALU.logical_shift_right).then_inc(choose.sem, 1)
                    nc.vector.tensor_scalar(place_b[:], place[:], TOPK - 1, None, ALU.bitwise_and).then_inc(choose.sem, 1)
                    nc.vector.tensor_copy(top_f[:, :, :], top_i[:, :, :])
                    dve.wait_ge(choose.sem, m0 + 3)
                    nc.vector.tensor_copy(places[:, 0, :], place_a[:]).then_inc(choose.sem, 1)
                    nc.vector.tensor_copy(places[:, 1, :], place_b[:]).then_inc(choose.sem, 1)
                    dve.wait_ge(choose.sem, m0 + 5)
                    for side, one_hots in ((1, first_j), (0, choose)):
                        nc.vector.tensor_tensor(hot[:, side, :, :], iota[:, 0:TOPK].unsqueeze(1).to_broadcast([P, PICKS, TOPK]),
                                                places[:, side, :].unsqueeze(2).to_broadcast([P, PICKS, TOPK]), ALU.is_equal).then_inc(one_hots.sem, 1)
                    dve.wait_ge(choose.sem, m0 + 6)
                    by_keys(nc.vector, 0).then_inc(choose.sem, 1)
                    dve.wait_ge(choose.sem, m0 + 7)
                    nc.vector.tensor_reduce(picks[:, 0, :], hot[:, 0, :, :], AX.X, ALU.add).then_inc(choose.sem, 1)
                    dve.wait_ge(second.sem, tile + 1)
                    nc.vector.tensor_reduce(picks[:, 1, :], hot[:, 1, :, :], AX.X, ALU.add).then_inc(choose.sem, 1)
                    dve.wait_ge(gate_exp.sem, tile + 1)
                    nc.vector.tensor_reduce(gate_sum[:, 0, :], gates, AX.X, ALU.add).then_inc(choose.sem, 1)
                    dve.wait_ge(choose.sem, m0 + 10)
                    nc.vector.reciprocal(gate_sum[:, 1, :], gate_sum[:, 0, :]).then_inc(gate_inv.sem, 1)
                    dve.wait_ge(gate_inv.sem, tile + 1)
                    nc.vector.tensor_tensor(gates, gates, gate_sum[:, 1, :].unsqueeze(2).to_broadcast([P, PEER_HEADS, TOPK]), ALU.mult).then_inc(choose.sem, 1)
        if stop == 2:
            return

        hot1_ready, hot2_ready, dense_ready, dense_copied = (sig(n) for n in ("first_one_hots_ready", "gated_one_hots_ready", "dense_gates_ready", "dense_gates_copied"))
        gates_stored = [sig(f"gates_stored{k}") for k in range(2)]
        QUAD = 4
        GSTEPS = GT // QUAD
        with ExitStack() as local, nc.Block() as block:
            hot1 = [sb("hot1", [P, QUAD, P], F32, local) for _ in range(2)]
            hot2 = [sb("hot2", [P, QUAD, P], F32, local) for _ in range(2)]
            stage = sb("gates_stage", [P, 2, N_KEYS, GT], F32, local)

            @block.vector
            def _(dve):
                with dve.Fori(0, T // QUAD // 2) as i:
                    for k in range(2):
                        dve.wait_ge(dense_ready.sem, i * 2 + (k + 1))
                        nc.vector.tensor_tensor(hot1[k][:, :, :], iota[:, :].unsqueeze(1).to_broadcast([P, QUAD, P]),
                                                picks_t[:, 0, bass.ds(i * (2 * QUAD) + k * QUAD, QUAD)].unsqueeze(2).to_broadcast([P, QUAD, P]),
                                                ALU.is_equal).then_inc(hot1_ready.sem, 1)
                        for t in range(QUAD):
                            token = i * (2 * QUAD) + (k * QUAD + t)
                            ins = nc.vector.tensor_scalar(hot2[k][:, t, :], iota[:, :], picks_t[:, 1, bass.ds(token, 1)], picks_t[:, 2, bass.ds(token, 1)],
                                                          ALU.is_equal, ALU.mult)
                        ins.then_inc(hot2_ready.sem, 1)

            @block.tensor
            def _(pe):
                pe.sem_inc(dense_copied.sem, 2)
                pe.sem_inc(dense_ready.sem, 2)
                with pe.Fori(0, T // QUAD // 2) as i:
                    for k in range(2):
                        pe.wait_ge(hot1_ready.sem, i * 2 + (k + 1))
                        pe.wait_ge(hot2_ready.sem, i * 2 + (k + 1))
                        pe.wait_ge(dense_copied.sem, i * 2 + (k + 1))
                        for t in range(QUAD):
                            mm = nc.tensor.matmul(psum[:, k, t * P:(t + 1) * P], hot1[k][:, t, :], hot2[k][:, t, :], start=True, stop=True)
                        mm.then_inc(dense_ready.sem, 1)

            @block.scalar
            def _(act):
                act.sem_inc(gates_stored[0].sem, 16)
                act.sem_inc(gates_stored[1].sem, 16)
                with act.Fori(0, GBLOCKS // 2) as o:
                    for half in range(2):
                        act.wait_ge(gates_stored[half].sem, o * 16 + 16)
                        with act.Fori(0, GSTEPS // 2) as i:
                            for k in range(2):
                                act.wait_ge(dense_ready.sem, o * (2 * GSTEPS) + i * 2 + (half * GSTEPS + k + 3))
                                nc.scalar.activation(stage[:, half, :, bass.ds(i * (2 * QUAD) + k * QUAD, QUAD)],
                                                     psum[:, k, :].rearrange("p (t j) -> p j t", t=QUAD), ACT.Copy).then_inc(dense_copied.sem, 1)

            @block.sync
            def _(sp):
                with sp.Fori(0, GBLOCKS // 2) as o:
                    for half in range(2):
                        sp.wait_ge(dense_copied.sem, o * (2 * GSTEPS) + (half * GSTEPS + GSTEPS + 2))
                        sp.dma_start(gates_dram[o * 2 + half], stage[:, half, :, :].rearrange("p j t -> p (j t)")).then_inc(gates_stored[half].sem, 16)
                for half in range(2):
                    sp.wait_ge(gates_stored[half].sem, 16 * (GBLOCKS // 2 + 1))

        activated = sig("ffn_activated")
        gated, ffn_hi, ffn_lo = sig("ffn_gated"), sig("ffn_hi_ready"), sig("ffn_lo_ready")
        gates_loaded = sig("gates_loaded")
        started = [False]

        def feed_forward(groups, acts, function, gates, h_hi, h_lo, raw_act, raw_gated, gate_tile=None):
            w = weights
            u0, base, per = w.u0, out_free.base, 2 * C
            a0, g0, h0 = activated.base, gated.base, ffn_lo.base
            first = not started[0]
            started[0] = True
            with nc.Block() as block:
                def gates_of(g):
                    return gates_dram[:, :, bass.ds(g * (C * GT), C * GT)].rearrange("b i n -> i b n")

                @block.sync
                def _(sp):
                    if gates:
                        sp.dma_start(gate_tile[:, :, :], gates_of(0)).then_inc(gates_loaded.sem, 16)
                    dram, index = w.source(u0)
                    with sp.Fori(0, groups - 1) as i:
                        for k in range(per):
                            w.load(sp, i * per + (k + RING), (u0 + k) % RING, dram, i * per + (index + k + RING))
                            if gates and k == per - RING - 1:
                                sp.wait_ge(gated.sem, i * C + (g0 + C))
                                sp.dma_start(gate_tile[:, :, :], gates_of(i + 1)).then_inc(gates_loaded.sem, 16)
                    for k in range(per):
                        v = u0 + (groups - 1) * per + k + RING
                        if v < w.total:
                            dram, index = w.source(v)
                            w.load(sp, (groups - 1) * per + k + RING, v % RING, dram, index)

                @block.tensor
                def _(pe):
                    if first:
                        pe.sem_inc(activated.sem, RING)
                    with pe.Fori(0, groups) as i:
                        for k in range(C):
                            pe.wait_ge(activated.sem, i * C + (a0 + k + 1))
                            w.multiply(pe, i, k, per, psum[:, k % RING, :], acts).then_inc(w.unit_done.sem, 1)
                        for d in range(C):
                            pe.wait_ge(out_free.sem, i * C + (base + d + 1))
                            bank = psum[:, 4 + d % RING, :]
                            for c in range(C):
                                if d == 0:
                                    pe.wait_ge(ffn_lo.sem, i * C + (h0 + c + 1))
                                mm = w.multiply_chunk(pe, i, C + d, per, bank, (h_hi, h_lo), c)
                            mm.then_inc(w.unit_done.sem, 1)

                @block.scalar
                def _(act):
                    def body(i, last):
                        for k in range(per):
                            if not (last and w.u0 + (groups - 1) * per + k + w.AHEAD >= w.total):
                                w.hi_step(act, i, k + w.AHEAD, per)
                            if k < C:
                                act.wait_ge(w.unit_done.sem, i * per + w.done(k))
                                if k >= 2:
                                    act.wait_ge(gated.sem, i * C + (g0 + k - 1))
                                nc.scalar.activation(raw_act[:, k % 2, :], psum[:, k % RING, :], function).then_inc(activated.sem, 1)
                                act.wait_ge(gated.sem, i * C + (g0 + k + 1))
                                nc.scalar.activation(h_hi[:, k, :], raw_gated[:, k % 2, :], ACT.Copy).then_inc(ffn_hi.sem, 1)
                    with act.Fori(0, groups - 1) as i:
                        body(i, False)
                    body(groups - 1, True)

                @block.vector
                def _(dve):
                    def body(i, last):
                        for k in range(per):
                            if not (last and w.u0 + (groups - 1) * per + k + w.AHEAD >= w.total):
                                w.lo_step(dve, i, k + w.AHEAD, per)
                            if k < C:
                                dve.wait_ge(activated.sem, i * C + (a0 + RING + k + 1))
                                if gates and k == 0:
                                    dve.wait_ge(gates_loaded.sem, i * 16 + 16)
                                other = gate_tile[:, :, k * GT:(k + 1) * GT] if gates else raw_act[:, k % 2, :]
                                one = raw_act[:, k % 2, :]
                                out = raw_gated[:, k % 2, :]
                                if gates:
                                    one, out = (a.rearrange("p (b t) -> p b t", t=GT) for a in (one, out))
                                nc.vector.tensor_tensor(out, one, other, ALU.mult).then_inc(gated.sem, 1)
                                dve.wait_ge(ffn_hi.sem, i * C + (g0 + k + 1))
                                nc.vector.tensor_tensor(h_lo[:, k, :], raw_gated[:, k % 2, :], h_hi[:, k, :].bitcast(F32),
                                                        ALU.subtract).then_inc(ffn_lo.sem, 1)
                            else:
                                d = k - C
                                dve.wait_ge(w.unit_done.sem, i * per + w.done(k))
                                nc.vector.tensor_tensor(x[:, d, :], x[:, d, :], psum[:, 4 + d % RING, :], ALU.add).then_inc(out_free.sem, 1)
                    with dve.Fori(0, groups - 1) as i:
                        body(i, False)
                    body(groups - 1, True)
            w.u0 += groups * per
            for s in (activated, gated, ffn_hi, ffn_lo, out_free):
                s.base += groups * C

        with ExitStack() as local:
            inner_hi = sb("inner_hi", [P, C, T], F32R, local)
            inner_lo = sb("inner_lo", [P, C, T], F32R, local)
            raw_act = sb("inner_activated", [P, 2, T], F32, local)
            raw_gated = sb("inner_gated", [P, 2, T], F32, local)
            gate_tile = sb("gates_of_group", [P, GBLOCKS, C * GT], F32, local)
            feed_forward(EXPERT_GROUPS, (act_hi, act_lo), ACT.Gelu, True, inner_hi, inner_lo, raw_act, raw_gated, gate_tile)
        peer_stack.close()
        rms_norm(x, 2, out_f32=x)
        if stop == 3:
            return

        y = sb("rwkv_out", [P, 4, T], F32)
        rwkv_stack = ExitStack()
        ctx.enter_context(rwkv_stack)
        rw = sb("rwkv_projections", [P, RWKV_SLABS, T + 1], F32, rwkv_stack)
        with ExitStack() as local:
            act_hi = sb("act_hi", [P, C, T], F32R, local)
            act_lo = sb("act_lo", [P, C, T], F32R, local)
            rms_norm(x, 3, out_split=(act_hi, act_lo))
            linear(RWKV_SLABS, (act_hi, act_lo),
                   lambda loop, k, bank: nc.scalar.activation(rw[:, at(loop, k), 1:T + 1], bank, ACT.Copy), "scalar")

        def R(n):
            return rw[:, n, 1:T + 1]

        R_, K_, V_, WA_, G_ = 0, 4, 8, 12, 13
        kk = sb("rwkv_kk", [P, 4, T], F32, rwkv_stack)
        bb = sb("rwkv_b", [P, 4, T], F32, rwkv_stack)
        bonus = sb("rwkv_bonus", [P, 4, T], F32, rwkv_stack)
        vecs = sb("rwkv_vectors_sb", [P, 64], F32, rwkv_stack)
        mu, kkv, kav, rkv, a0v, lnw, lnb = vecs[:, 0:15], vecs[:, 16:20], vecs[:, 20:24], vecs[:, 24:28], vecs[:, 28:32], vecs[:, 32:36], vecs[:, 36:40]
        block_ones = sb("block_ones", [P, P], F32, rwkv_stack)
        block_avg = sb("block_average", [P, P], F32, rwkv_stack)
        lora = sb("rwkv_lora", [P, 4, T], F32, rwkv_stack)
        w0_row = sb("rwkv_w0", [1, T], F32, rwkv_stack)
        ln_eps = sb("rwkv_eps", [P, 1], F32, rwkv_stack)
        mid_decay = sb("mid_decay", [P, 2, 4, TT], F32, rwkv_stack)
        turned_stack = ExitStack()
        rwkv_stack.enter_context(turned_stack)
        decay_in = sb("decay_gate", [P, TT, T], F32, turned_stack)

        rwkv_loaded, shift_diff, shifted = sig("rwkv_loaded"), sig("shift_difference_ready"), sig("token_shifted")
        lora_in, decay_product, decay_gate = sig("lora_inputs_ready"), sig("decay_product_ready"), sig("decay_gate_ready")
        a_product, a_ready = sig("a_product_ready"), sig("a_ready")
        with ExitStack() as local, nc.Block() as block:
            diff = sb("shift_difference", [P, 2, T], F32, local)

            @block.sync
            def _(sp):
                for dst, src in ((vecs[:, 0:40], rwkv["vectors"]), (block_ones[:], rwkv["block_ones"]), (block_avg[:], rwkv["block_average"]),
                                 (lora[:, 0, :], rwkv["lora_wa"]), (lora[:, 1, :], rwkv["lora_g"][0:P, :]),
                                 (lora[0:32, 2, :], rwkv["lora_g"][P:P + 32, :]), (w0_row[:, :], rwkv["w0"])):
                    sp.dma_start(dst, src).then_inc(rwkv_loaded.sem, 16)

            order = [WA_, G_, G_ + 1] + list(range(12))

            @block.gpsimd
            def _(pool):
                nc.gpsimd.memset(rw[:, :, 0:1], 0.0).then_inc(shift_diff.sem, 1)
                nc.gpsimd.memset(ln_eps[:], RWKV_LN_EPS)
                pool.wait_ge(shift_diff.sem, 1)
                for j, n in enumerate(order):
                    if j >= 2:
                        pool.wait_ge(shifted.sem, j - 1)
                    nc.gpsimd.tensor_tensor(diff[:, j % 2, :], rw[:, n, 0:T], rw[:, n, 1:T + 1], ALU.subtract).then_inc(shift_diff.sem, 1)

            @block.vector
            def _(dve):
                dve.wait_ge(rwkv_loaded.sem, 7 * 16)
                for j, n in enumerate(order):
                    dve.wait_ge(shift_diff.sem, j + 2)
                    nc.vector.scalar_tensor_tensor(R(n), diff[:, j % 2, :], mu[:, n:n + 1], R(n), ALU.mult, ALU.add).then_inc(shifted.sem, 1)
                for j in range(4):
                    dve.wait_ge(shifted.sem, len(order))
                    nc.vector.tensor_scalar(kk[:, j, :], R(K_ + j), kkv[:, j:j + 1], None, ALU.mult)

            @block.tensor
            def _(pe):
                pe.wait_ge(rwkv_loaded.sem, 7 * 16)
                pe.wait_ge(lora_in.sem, 1)
                for tile in range(TT):
                    tokens = slice(1 + tile * P, 1 + (tile + 1) * P)
                    nc.tensor.matmul(psum[:, tile, :], rw[0:64, WA_, tokens], lora[0:64, 0, :], start=True, stop=False)
                    nc.tensor.matmul(psum[:, tile, :], ones[0:1, :], w0_row[0:1, :], start=False, stop=True).then_inc(decay_product.sem, 1)
                for j in range(4):
                    nc.tensor.matmul(psum[:, 4 + j, :], lora[64:128, 0, j * P:(j + 1) * P], rw[64:128, WA_, 1:T + 1],
                                     start=True, stop=True).then_inc(a_product.sem, 1)

            @block.scalar
            def _(act):
                act.wait_ge(shifted.sem, 3)
                nc.scalar.activation(rw[0:64, WA_, 1:T + 1], rw[0:64, WA_, 1:T + 1], ACT.Tanh).then_inc(lora_in.sem, 1)
                nc.scalar.activation(R(G_), R(G_), ACT.Sigmoid)
                nc.scalar.activation(rw[0:32, G_ + 1, 1:T + 1], rw[0:32, G_ + 1, 1:T + 1], ACT.Sigmoid)
                for tile in range(TT):
                    act.wait_ge(decay_product.sem, tile + 1)
                    nc.scalar.activation(decay_in[:, tile, :], psum[:, tile, :], ACT.Sigmoid)
                act.wait_ge(rwkv_loaded.sem, 7 * 16)
                for j in range(4):
                    act.wait_ge(a_product.sem, j + 1)
                    nc.scalar.activation(bb[:, j, :], psum[:, 4 + j, :], ACT.Sigmoid, bias=a0v[:, j:j + 1])

        head_norm(kk, block_ones[:], 0.0, center=False, floor=1e-24)

        KAPPA = math.exp(-0.5)
        sums_ready, sums_read = sig("decay_sums_ready"), sig("decay_sums_read")
        ops, bonus_sum, k_step = sig("rwkv_operand_ready"), sig("bonus_sum_ready"), sig("k_factor_ready")
        with ExitStack() as local, nc.Block() as block:
            sum_masks = sb("decay_sum_masks", [P, 2, P], F32, local)
            till = sb("decay_till", [P, 4, T], F32, local)
            before = sb("decay_before", [P, 4, T], F32, local)
            back = sb("decay_inverse", [P, 4, T], F32, local)
            factor = sb("k_factor", [P, 4, T], F32, local)
            masks_loaded = sig("decay_masks_loaded")

            @block.sync
            def _(sp):
                sp.dma_start(sum_masks[:, :, :], rwkv["sum_masks"]).then_inc(masks_loaded.sem, 16)

            @block.tensor
            def _(pe):
                pe.wait_ge(masks_loaded.sem, 16)
                for j in range(4):
                    for pair in range(2):
                        n = 2 * j + pair
                        if n >= 4:
                            pe.wait_ge(sums_read.sem, n - 3)
                        for half in range(2):
                            tile = 2 * pair + half
                            mm = nc.tensor.matmul(psum[:, n % 4, half * 2 * P:(half + 1) * 2 * P], decay_in[:, tile, j * P:(j + 1) * P],
                                                  sum_masks[:, :, :], start=True, stop=True)
                        mm.then_inc(sums_ready.sem, 1)
                for j in range(4):
                    pe.wait_ge(ops.sem, j + 1)
                    nc.tensor.matmul(psum[:, 4 + j, :], block_ones[:], bonus[:, j, :], start=True, stop=True).then_inc(bonus_sum.sem, 1)

            @block.scalar
            def _(act):
                for j in range(4):
                    for pair in range(2):
                        n = 2 * j + pair
                        act.wait_ge(sums_ready.sem, n + 1)
                        sums = psum[:, n % 4, :].rearrange("p (h m t) -> p h m t", h=2, m=2)
                        span = slice(2 * pair * P, 2 * (pair + 1) * P)

                        def two(buf):
                            return buf[:, j, span].rearrange("p (h t) -> p h t", h=2)
                        nc.scalar.activation(two(till), sums[:, :, 0, :], ACT.Exp, scale=-KAPPA)
                        nc.scalar.activation(two(back), sums[:, :, 0, :], ACT.Exp, scale=KAPPA)
                        nc.scalar.activation(two(before), sums[:, :, 1, :], ACT.Exp, scale=-KAPPA)
                        nc.scalar.activation(mid_decay[:, 1, j, 2 * pair:2 * pair + 2], sums[:, :, 0, P - 1], ACT.Exp, scale=-KAPPA)
                        nc.scalar.activation(mid_decay[:, 0, j, 2 * pair:2 * pair + 2], sums[:, :, 1, 0], ACT.Exp, scale=KAPPA).then_inc(sums_read.sem, 1)

            @block.vector
            def _(dve):
                for j in range(4):
                    nc.vector.tensor_scalar(factor[:, j, :], bb[:, j, :], 1.0, kav[:, j:j + 1], ALU.subtract, ALU.mult).then_inc(k_step.sem, 1)
                for j in range(4):
                    dve.wait_ge(k_step.sem, j + 1)
                    nc.vector.scalar_tensor_tensor(R(K_ + j), factor[:, j, :], 1.0, R(K_ + j), ALU.add, ALU.mult).then_inc(k_step.sem, 1)
                for j in range(4):
                    dve.wait_ge(k_step.sem, 4 + j + 1)
                    nc.vector.scalar_tensor_tensor(bonus[:, j, :], R(R_ + j), rkv[:, j:j + 1], R(K_ + j), ALU.mult, ALU.mult).then_inc(ops.sem, 1)
                for j in range(4):
                    nc.vector.tensor_tensor(bb[:, j, :], bb[:, j, :], kk[:, j, :], ALU.mult).then_inc(k_step.sem, 1)
                for j in range(4):
                    dve.wait_ge(bonus_sum.sem, j + 1)
                    nc.vector.tensor_tensor(bonus[:, j, :], R(V_ + j), psum[:, 4 + j, :], ALU.mult)
                for j in range(4):
                    dve.wait_ge(sums_read.sem, 2 * (j + 1))
                    dve.wait_ge(k_step.sem, 8 + j + 1)
                    nc.vector.tensor_tensor(bb[:, j, :], bb[:, j, :], back[:, j, :], ALU.mult)
                    nc.vector.scalar_tensor_tensor(kk[:, j, :], kk[:, j, :], -1.0, before[:, j, :], ALU.mult, ALU.mult)
                    nc.vector.tensor_tensor(R(K_ + j), R(K_ + j), back[:, j, :], ALU.mult)
                    nc.vector.tensor_tensor(R(R_ + j), R(R_ + j), till[:, j, :], ALU.mult)
        turned_stack.close()

        tok_turned, tok_copied = sig("operand_transposed"), sig("operand_copied")
        v_t = sb("rwkv_v_by_token", [P, TT, T], F32, rwkv_stack)
        k_t = sb("rwkv_k_by_token", [P, TT, T], F32, rwkv_stack)
        b_t = sb("rwkv_b_by_token", [P, TT, T], F32, rwkv_stack)
        with nc.Block() as block:
            turns = [(dst, get, tile) for dst, get in ((v_t, lambda j: R(V_ + j)), (k_t, lambda j: R(K_ + j)), (b_t, lambda j: bb[:, j, :]))
                     for tile in range(TT)]

            @block.tensor
            def _(pe):
                for n, (dst, get, tile) in enumerate(turns):
                    if n >= 4:
                        pe.wait_ge(tok_copied.sem, n - 3)
                    for j in range(4):
                        mm = nc.tensor.transpose(psum[:, n % 4, j * P:(j + 1) * P], get(j)[:, tile * P:(tile + 1) * P], ident[:])
                    mm.then_inc(tok_turned.sem, 1)

            @block.scalar
            def _(act):
                for n, (dst, get, tile) in enumerate(turns):
                    act.wait_ge(tok_turned.sem, n + 1)
                    nc.scalar.activation(dst[:, tile, :], psum[:, n % 4, :], ACT.Copy).then_inc(tok_copied.sem, 1)

        LEVELS = 6
        PAIRS = 5
        pair_mm, pair_done = sig("pair_products_ready"), sig("pair_products_masked")
        inverse_first, inverse_t_first = sig("first_inverse_ready"), sig("first_inverse_t_ready")
        part_ready, times_l, prod_copied = sig("joining_blocks_ready"), sig("l_times_inverse_ready"), sig("l_times_inverse_copied")
        joined, stepped, unit_added = sig("joined_blocks_ready"), sig("inverse_stepped"), sig("inverse_t_scratch")
        x0_mm, x0_copied, sa_mm, sa_copied = sig("x0_ready"), sig("x0_copied"), sig("sa_ready"), sig("sa_copied")
        y_mm, y_copied, state_mm, state_done, state_step = sig("y_ready"), sig("y_copied"), sig("state_product_ready"), sig("state_updated"), sig("state_step")
        chunk_masks_loaded = sig("chunk_masks_loaded")
        with ExitStack() as local, nc.Block() as block:
            masks = sb("chunk_masks", [P, 11, P], F32, local)
            lak, lrb, lrk, low, inv, inv_t, prod, part = (sb(n, [P, 8, P], F32, local) for n in (
                "chunk_lak", "chunk_lrb", "chunk_lrk", "chunk_l_t", "chunk_inverse", "chunk_inverse_t", "chunk_l_inverse", "chunk_l_part"))
            state = sb("state", [P, 4, 64], F32, local)
            x0 = sb("chunk_x0", [P, 8, 64], F32, local)
            sa = sb("chunk_sa", [P, 8, 64], F32, local)

            def at_head(h):
                return (h % 2) * 4 + h // 2

            def rows(h):
                return slice(64 * (h % 2), 64 * (h % 2) + 64)

            def both(b):
                return psum[:, b:b + 2, :].rearrange("p b (h t) -> p (b h) t", t=P)

            def half(buf, g):
                return buf[:, 4 * g:4 * g + 4, :]

            def bank4(b):
                return psum[:, b, :].rearrange("p (h t) -> p h t", t=P)

            def mask(m, n):
                return masks[:, m, :].unsqueeze(1).to_broadcast([P, n, P])

            @block.sync
            def _(sp):
                sp.dma_start(masks[:, :, :], rwkv["chunk_masks"]).then_inc(chunk_masks_loaded.sem, 16)

            @block.tensor
            def _(pe):
                for c in range(TT):
                    tok, tok1 = slice(c * P, (c + 1) * P), slice(1 + c * P, 1 + (c + 1) * P)

                    def a_(h): return kk[rows(h), h // 2, tok]
                    def b_(h): return bb[rows(h), h // 2, tok]
                    def k_(h): return rw[rows(h), K_ + h // 2, tok1]
                    def r_(h): return rw[rows(h), R_ + h // 2, tok1]
                    if c:
                        pe.wait_ge(y_copied.sem, c)
                        pe.wait_ge(state_done.sem, c)
                    for n, (one, two) in enumerate(((a_, b_), (b_, a_), (k_, a_), (b_, r_), (k_, r_))):
                        m = c * PAIRS + n
                        if m >= 2:
                            pe.wait_ge(pair_done.sem, m - 1)
                        for h in range(8):
                            mm = nc.tensor.matmul(both(2 * (m % 2))[:, at_head(h), :], one(h), two(h), start=True, stop=True)
                        mm.then_inc(pair_mm.sem, 1)
                    for l in range(LEVELS):
                        for g in range(2):
                            n = (c * LEVELS + l) * 2 + g
                            pe.wait_ge(part_ready.sem, n + 1)
                            if l == 0:
                                pe.wait_ge(inverse_first.sem, c + 1)
                                pe.wait_ge(inverse_t_first.sem, c + 1)
                            else:
                                pe.wait_ge(stepped.sem, n - 1)
                            for h in range(g, 8, 2):
                                mm = nc.tensor.matmul(psum[:, 4 + g, (h // 2) * P:(h // 2 + 1) * P], part[:, at_head(h), :], inv[:, at_head(h), :],
                                                      start=True, stop=True)
                            mm.then_inc(times_l.sem, 1)
                        for g in range(2):
                            n = (c * LEVELS + l) * 2 + g
                            pe.wait_ge(prod_copied.sem, n + 1)
                            for h in range(g, 8, 2):
                                mm = nc.tensor.matmul(psum[:, 6 + g, (h // 2) * P:(h // 2 + 1) * P], prod[:, at_head(h), :], inv_t[:, at_head(h), :],
                                                      start=True, stop=True)
                            if l < LEVELS - 1:
                                for h in range(g, 8, 2):
                                    mm = nc.tensor.matmul(psum[:, 4 + g, (h // 2) * P:(h // 2 + 1) * P], inv_t[:, at_head(h), :], prod[:, at_head(h), :],
                                                          start=True, stop=True)
                            mm.then_inc(joined.sem, 1)
                    pe.wait_ge(pair_done.sem, PAIRS * (c + 1))
                    for h in range(8):
                        out = psum[:, h % 2, (h // 2) * 64:(h // 2 + 1) * 64]
                        if c:
                            nc.tensor.matmul(out, a_(h), state[rows(h), h // 2, :], start=True, stop=False)
                        mm = nc.tensor.matmul(out, lak[:, at_head(h), :], v_t[:, c, h * 64:(h + 1) * 64], start=not c, stop=True)
                    mm.then_inc(x0_mm.sem, 1)
                    pe.wait_ge(x0_copied.sem, c + 1)
                    pe.wait_ge(stepped.sem, 2 * LEVELS * (c + 1))
                    for h in range(8):
                        mm = nc.tensor.matmul(psum[:, 2, at_head(h) * 64:(at_head(h) + 1) * 64], inv_t[:, at_head(h), :], x0[:, at_head(h), :],
                                              start=True, stop=True)
                    mm.then_inc(sa_mm.sem, 1)
                    pe.wait_ge(sa_copied.sem, c + 1)
                    for h in range(8):
                        out = psum[rows(h), h % 2, (h // 2) * P:(h // 2 + 1) * P]
                        if c:
                            nc.tensor.matmul(out, state[rows(h), h // 2, :], r_(h), start=True, stop=False)
                        nc.tensor.matmul(out, sa[:, at_head(h), :], lrb[:, at_head(h), :], start=not c, stop=False)
                        mm = nc.tensor.matmul(out, v_t[:, c, h * 64:(h + 1) * 64], lrk[:, at_head(h), :], start=False, stop=True)
                    mm.then_inc(y_mm.sem, 1)
                    for h in range(8):
                        out = psum[rows(h), 2 + h % 2, (h // 2) * 64:(h // 2 + 1) * 64]
                        nc.tensor.matmul(out, b_t[:, c, h * 64:(h + 1) * 64], sa[:, at_head(h), :], start=True, stop=False)
                        mm = nc.tensor.matmul(out, k_t[:, c, h * 64:(h + 1) * 64], v_t[:, c, h * 64:(h + 1) * 64], start=False, stop=True)
                    mm.then_inc(state_mm.sem, 1)

            @block.scalar
            def _(act):
                for c in range(TT):
                    for l in range(LEVELS):
                        for g in range(2):
                            n = (c * LEVELS + l) * 2 + g
                            act.wait_ge(times_l.sem, n + 1)
                            nc.scalar.activation(half(prod, g), bank4(4 + g), ACT.Copy).then_inc(prod_copied.sem, 1)
                    act.wait_ge(x0_mm.sem, c + 1)
                    nc.scalar.activation(x0[:, :, :].rearrange("p (g h) v -> p g (h v)", g=2), psum[:, 0:2, 0:256], ACT.Copy).then_inc(x0_copied.sem, 1)
                    act.wait_ge(sa_mm.sem, c + 1)
                    nc.scalar.activation(sa[:, :, :].rearrange("p h v -> p (h v)"), psum[:, 2, :], ACT.Copy).then_inc(sa_copied.sem, 1)
                    act.wait_ge(y_mm.sem, c + 1)
                    for g in range(2):
                        part_rows = slice(64 * g, 64 * g + 64)
                        copied = nc.scalar.activation(y[part_rows, :, c * P:(c + 1) * P], bank4(g)[part_rows, :, :], ACT.Copy)
                    copied.then_inc(y_copied.sem, 1)

            @block.gpsimd
            def _(pool):
                pool.wait_ge(chunk_masks_loaded.sem, 16)
                for c in range(TT):
                    pool.wait_ge(pair_done.sem, PAIRS * c + 2)
                    nc.gpsimd.tensor_tensor(inv_t[:, :, :], low[:, :, :], mask(8, 8), ALU.mult).then_inc(unit_added.sem, 1)
                    pool.wait_ge(unit_added.sem, c + 1)
                    nc.gpsimd.tensor_tensor(inv_t[:, :, :], inv_t[:, :, :], mask(10, 8), ALU.add).then_inc(inverse_t_first.sem, 1)
                    for l in range(LEVELS):
                        for g in range(2):
                            n = (c * LEVELS + l) * 2 + g
                            if n >= 2:
                                pool.wait_ge(times_l.sem, n - 1)
                            nc.gpsimd.tensor_tensor(half(part, g), half(low, g), mask(2 + l, 4), ALU.mult).then_inc(part_ready.sem, 1)

            @block.vector
            def _(dve):
                dve.wait_ge(chunk_masks_loaded.sem, 16)
                for c in range(TT):
                    if c:
                        dve.wait_ge(part_ready.sem, 2 * LEVELS * c)
                    for n, (dst, m) in enumerate(((inv, 9), (low, 0), (lak, 0), (lrb, 1), (lrk, 1))):
                        dve.wait_ge(pair_mm.sem, PAIRS * c + n + 1)
                        nc.vector.tensor_tensor(dst[:, :, :], both(2 * ((PAIRS * c + n) % 2)), mask(m, 8), ALU.mult).then_inc(pair_done.sem, 1)
                        if n == 1:
                            dve.wait_ge(pair_done.sem, PAIRS * c + 1)
                            nc.vector.tensor_tensor(inv[:, :, :], inv[:, :, :], mask(10, 8), ALU.add).then_inc(inverse_first.sem, 1)
                    for l in range(LEVELS):
                        for g in range(2):
                            n = (c * LEVELS + l) * 2 + g
                            dve.wait_ge(joined.sem, n + 1)
                            last = nc.vector.tensor_tensor(half(inv_t, g), half(inv_t, g), bank4(6 + g), ALU.add)
                            if l < LEVELS - 1:
                                last = nc.vector.tensor_tensor(half(inv, g), half(inv, g), bank4(4 + g), ALU.add)
                            last.then_inc(stepped.sem, 1)
                    dve.wait_ge(state_mm.sem, c + 1)
                    if c < TT - 1:
                        for g in range(2):
                            part_rows = slice(64 * g, 64 * g + 64)
                            new = psum[part_rows, 2 + g, 0:256].rearrange("p (h v) -> p h v", v=64)
                            if c:
                                step = nc.vector.tensor_tensor(state[part_rows, :, :], state[part_rows, :, :], new, ALU.add)
                            else:
                                step = nc.vector.tensor_copy(state[part_rows, :, :], new)
                        step.then_inc(state_step.sem, 1)
                        dve.wait_ge(state_step.sem, 2 * c + 1)
                        nc.vector.tensor_tensor(state[:, :, :], state[:, :, :], mid_decay[:, 1, :, c].unsqueeze(2).to_broadcast([P, 4, 64]),
                                                ALU.mult).then_inc(state_step.sem, 1)
                        dve.wait_ge(state_step.sem, 2 * c + 2)
                        nc.vector.tensor_tensor(state[:, :, :], state[:, :, :], mid_decay[:, 0, :, c + 1].unsqueeze(2).to_broadcast([P, 4, 64]),
                                                ALU.mult).then_inc(state_done.sem, 1)

        head_norm(y, block_avg[:], ln_eps[:, 0:1], center=True)
        gate_product, out_step = sig("rwkv_gate_ready"), sig("rwkv_out_step")
        with nc.Block() as block:
            @block.tensor
            def _(pe):
                for j in range(4):
                    cols = slice(j * P, (j + 1) * P)
                    nc.tensor.matmul(psum[:, j, :], lora[:, 1, cols], R(G_), start=True, stop=False)
                    nc.tensor.matmul(psum[:, j, :], lora[0:32, 2, cols], rw[0:32, G_ + 1, 1:T + 1], start=False, stop=True).then_inc(gate_product.sem, 1)

            @block.vector
            def _(dve):
                for j in range(4):
                    nc.vector.tensor_scalar(y[:, j, :], y[:, j, :], lnw[:, j:j + 1], lnb[:, j:j + 1], ALU.mult, ALU.add).then_inc(out_step.sem, 1)
                for j in range(4):
                    dve.wait_ge(out_step.sem, j + 1)
                    nc.vector.tensor_tensor(y[:, j, :], y[:, j, :], bonus[:, j, :], ALU.add).then_inc(out_step.sem, 1)
                for j in range(4):
                    dve.wait_ge(out_step.sem, 4 + j + 1)
                    dve.wait_ge(gate_product.sem, j + 1)
                    nc.vector.tensor_tensor(y[:, j, :], y[:, j, :], psum[:, j, :], ALU.mult)
        rwkv_stack.close()
        if stop == 4:
            return

        branch_stack = ExitStack()
        ctx.enter_context(branch_stack)
        branch_hi = sb("branch_hi", [P, C, T], F32R, branch_stack)
        branch_lo = sb("branch_lo", [P, C, T], F32R, branch_stack)
        act_hi = sb("act_hi", [P, C, T], F32R, branch_stack)
        act_lo = sb("act_lo", [P, C, T], F32R, branch_stack)
        split([(y[:, j, :], 1.0) for j in range(4)], branch_hi, branch_lo)
        rms_norm(x, 3, out_split=(act_hi, act_lo))
        conv_u, conv_acc, conv_w_loaded = sig("conv_input_ready"), sig("conv_step"), sig("conv_weights_loaded")
        with ExitStack() as local:
            cv = sb("conv_projections", [P, 12, T], F32, local)
            acc = sb("conv_out", [P, 4, T], F32, local)
            taps = sb("conv_taps", [P, 4, 3], F32, local)
            linear(12, (act_hi, act_lo),
                   lambda loop, k, bank: nc.scalar.activation(cv[:, at(loop, k), :], bank, ACT.Copy), "scalar")
            with nc.Block() as block:
                @block.sync
                def _(sp):
                    sp.dma_start(taps[:, :, :], conv_taps).then_inc(conv_w_loaded.sem, 16)

                @block.gpsimd
                def _(pool):
                    for j in range(4):
                        nc.gpsimd.tensor_tensor(cv[:, 4 + j, :], cv[:, 4 + j, :], cv[:, 8 + j, :], ALU.mult).then_inc(conv_u.sem, 1)

                @block.vector
                def _(dve):
                    dve.wait_ge(conv_w_loaded.sem, 16)
                    for j in range(4):
                        dve.wait_ge(conv_u.sem, j + 1)
                        u, a = cv[:, 4 + j, :], acc[:, j, :]
                        nc.vector.tensor_scalar(a, u, taps[:, j, 2:3], None, ALU.mult).then_inc(conv_acc.sem, 1)
                        for back, tap in ((1, 1), (2, 0)):
                            dve.wait_ge(conv_acc.sem, 3 * j + back)
                            nc.vector.scalar_tensor_tensor(acc[:, j, back:T], cv[:, 4 + j, 0:T - back], taps[:, j, tap:tap + 1], acc[:, j, back:T],
                                                           ALU.mult, ALU.add).then_inc(conv_acc.sem, 1)
                        dve.wait_ge(conv_acc.sem, 3 * j + 3)
                        nc.vector.tensor_tensor(a, a, cv[:, j, :], ALU.mult)
            split([(acc[:, j, :], 1.0) for j in range(4)], branch_hi, branch_lo, 4)

        gate_sig, gate_a, merged_f, merged_hi_ready = sig("merge_gates_ready"), sig("merge_gated"), sig("merged_ready"), sig("merged_hi_ready")
        gate_bias_loaded = sig("gate_bias_loaded")
        inner_hi = sb("inner_hi", [P, C, T], F32R, branch_stack)
        inner_lo = sb("inner_lo", [P, C, T], F32R, branch_stack)
        with ExitStack() as local, nc.Block() as block:
            gate_bias = sb("gate_bias", [P, 2, C], F32, local)
            opened = sb("merge_gates", [P, 2, T], F32, local)
            gated_b = sb("merge_gated_branches", [P, 2, T], F32, local)
            merged = sb("merged", [P, 2, T], F32, local)
            w, u0, per, turn = weights, weights.u0, 12, 4

            @block.sync
            def _(sp):
                sp.dma_start(gate_bias[:, :, :], gate_bias_in).then_inc(gate_bias_loaded.sem, 16)
                w.load_stage(sp, 3 * C)

            @block.tensor
            def _(pe):
                pe.sem_inc(merged_f.sem, 2)
                with pe.Fori(0, C // turn) as i:
                    for q in range(turn):
                        b = 4 * (q % 2)
                        pe.wait_ge(merged_f.sem, i * turn + (q + 1))
                        w.multiply(pe, i, 3 * q, per, psum[:, b, :], (branch_hi[:, 0:4, :], branch_lo[:, 0:4, :]), chunks=range(4))
                        w.multiply(pe, i, 3 * q, per, psum[:, b + 1, :], (branch_hi[:, 4:8, :], branch_lo[:, 4:8, :]),
                                   chunks=range(4, 8)).then_inc(w.unit_done.sem, 1)
                        for g in range(2):
                            w.multiply(pe, i, 3 * q + 1 + g, per, psum[:, b + 2 + g, :], (act_hi, act_lo)).then_inc(w.unit_done.sem, 1)

            @block.scalar
            def _(act):
                act.wait_ge(gate_bias_loaded.sem, 16)
                act.sem_inc(gate_a.sem, 2)
                with act.Fori(0, C // turn) as i:
                    for q in range(turn):
                        for g in range(3):
                            w.hi_step(act, i, 3 * q + g + w.AHEAD, per)
                            if g:
                                act.wait_ge(w.unit_done.sem, i * per + w.done(3 * q + g))
                                act.wait_ge(gate_a.sem, i * (2 * turn) + (2 * q + g))
                                nc.scalar.activation(opened[:, g - 1, :], psum[:, 4 * (q % 2) + 1 + g, :], ACT.Sigmoid,
                                                     bias=gate_bias[:, g - 1, bass.ds(i * turn + q, 1)]).then_inc(gate_sig.sem, 1)
                        act.wait_ge(merged_f.sem, i * turn + (q + 3))
                        nc.scalar.activation(inner_hi[:, bass.ds(i * turn + q, 1), :], merged[:, q % 2, :].unsqueeze(1), ACT.Copy).then_inc(merged_hi_ready.sem, 1)

            @block.vector
            def _(dve):
                with dve.Fori(0, C // turn) as i:
                    for q in range(turn):
                        for g in range(3):
                            w.lo_step(dve, i, 3 * q + g + w.AHEAD, per)
                            if g:
                                dve.wait_ge(gate_sig.sem, i * (2 * turn) + (2 * q + g))
                                nc.vector.tensor_tensor(gated_b[:, g - 1, :], opened[:, g - 1, :],
                                                        psum[:, 4 * (q % 2) + g - 1, :], ALU.mult).then_inc(gate_a.sem, 1)
                        dve.wait_ge(gate_a.sem, i * (2 * turn) + (2 * q + 4))
                        nc.vector.tensor_tensor(merged[:, q % 2, :], gated_b[:, 0, :], gated_b[:, 1, :], ALU.add).then_inc(merged_f.sem, 1)
                        dve.wait_ge(merged_hi_ready.sem, i * turn + (q + 1))
                        nc.vector.tensor_tensor(inner_lo[:, bass.ds(i * turn + q, 1), :], merged[:, q % 2, :].unsqueeze(1),
                                                inner_hi[:, bass.ds(i * turn + q, 1), :].bitcast(F32), ALU.subtract)
            w.u0 += 3 * C

        def add_to_x(loop, k, bank):
            return nc.vector.tensor_tensor(x[:, at(loop, k), :], x[:, at(loop, k), :], bank, ALU.add)

        linear(C, (inner_hi, inner_lo), add_to_x, "vector")
        branch_stack.close()
        if stop == 5:
            return

        mem_stack = ExitStack()
        ctx.enter_context(mem_stack)
        kv = sb("memory_kv", [P, 2 * C, M], F32, mem_stack)
        v_m = sb("memory_v_by_token", [P, M // P, D], F32, mem_stack)
        queries = sb("memory_queries", [P, C, T], F32, mem_stack)
        mem_loaded = sig("memory_loaded")
        with ExitStack() as local:
            mem_sb = sb("memory", [P, C, M], F32, local)
            mem_hi = sb("memory_hi", [P, C, M], F32R, local)
            mem_lo = sb("memory_lo", [P, C, M], F32R, local)
            with nc.Block() as block:
                @block.sync
                def _(sp):
                    sp.dma_start(mem_sb[:, :, :], mem_t).then_inc(mem_loaded.sem, 16)
                    sp.wait_ge(mem_loaded.sem, 16)
            rms_norm(mem_sb, 5, out_split=(mem_hi, mem_lo), width=M)
            linear(2 * C, (mem_hi, mem_lo),
                   lambda loop, k, bank: nc.scalar.activation(kv[:, at(loop, k), :], bank, ACT.Copy), "scalar", tokens=M)
        with ExitStack() as local:
            act_hi = sb("act_hi", [P, C, T], F32R, local)
            act_lo = sb("act_lo", [P, C, T], F32R, local)
            rms_norm(x, 4, out_split=(act_hi, act_lo))
            linear(C, (act_hi, act_lo),
                   lambda loop, k, bank: nc.scalar.activation(queries[:, at(loop, k), :], bank, ACT.Copy), "scalar")
        x_scored, x_max, x_neg, x_exp, x_inv, x_prob = (sig(n) for n in (
            "memory_scores_ready", "memory_max_ready", "memory_neg_max_ready", "memory_exp_ready", "memory_inverse_sum_ready", "memory_probs_ready"))
        x_turned, x_copied, x_out, v_m_turned, v_m_copied = (sig(n) for n in (
            "memory_probs_transposed", "memory_probs_copied", "memory_out_ready", "memory_v_transposed", "memory_v_copied"))
        x_out_copied = sig("memory_out_copied")
        out_f = sb("memory_out", [P, C, T], F32, mem_stack)
        XH = 4
        MT = M // P
        with ExitStack() as local, nc.Block() as block:
            pr = sb("memory_probs", [P, 2, M], F32, local)
            pr_t = sb("memory_probs_t", [P, 2, MT, T], F32, local)
            st = sb("memory_stats", [P, XH * TT, 4], F32, local)
            x_scale = 256 ** -0.5

            @block.tensor
            def _(pe):
                for mt in range(MT):
                    for half_c in range(2):
                        n = 2 * mt + half_c
                        if n >= 2:
                            pe.wait_ge(v_m_copied.sem, n - 1)
                        for j in range(4):
                            mm = nc.tensor.transpose(psum[:, 4 + n % 2, j * P:(j + 1) * P], kv[:, C + 4 * half_c + j, mt * P:(mt + 1) * P], ident[:])
                        mm.then_inc(v_m_turned.sem, 1)

                def scores(it):
                    h, tile = divmod(it, TT)
                    if it >= 2:
                        pe.wait_ge(x_exp.sem, it - 1)
                    for e in range(2):
                        mm = nc.tensor.matmul(psum[:, it % 2, 0:M], queries[:, 2 * h + e, tile * P:(tile + 1) * P], kv[:, 2 * h + e, :],
                                              start=e == 0, stop=e == 1)
                    mm.then_inc(x_scored.sem, 1)
                scores(0)
                for it in range(XH * TT):
                    h, tile = divmod(it, TT)
                    if it + 1 < XH * TT:
                        scores(it + 1)
                    pe.wait_ge(x_prob.sem, it + 1)
                    if it >= 2:
                        pe.wait_ge(x_copied.sem, it - 1)
                    for mt in range(MT):
                        mm = nc.tensor.transpose(psum[:, 2 + it % 2, mt * P:(mt + 1) * P], pr[:, it % 2, mt * P:(mt + 1) * P], ident[:])
                    mm.then_inc(x_turned.sem, 1)
                    if tile == TT - 1:
                        pe.wait_ge(x_copied.sem, it + 1)
                        pe.wait_ge(v_m_copied.sem, 2 * MT)
                        if h >= 1:
                            pe.wait_ge(x_out_copied.sem, 2 * h)
                        for e in range(2):
                            for mt in range(MT):
                                mm = nc.tensor.matmul(psum[:, 6 + e, :], v_m[:, mt, (2 * h + e) * P:(2 * h + e + 1) * P], pr_t[:, h % 2, mt, :],
                                                      start=mt == 0, stop=mt == MT - 1)
                            mm.then_inc(x_out.sem, 1)

            @block.scalar
            def _(act):
                for n in range(2 * MT):
                    act.wait_ge(v_m_turned.sem, n + 1)
                    nc.scalar.activation(v_m[:, n // 2, (n % 2) * T:(n % 2 + 1) * T], psum[:, 4 + n % 2, :], ACT.Copy).then_inc(v_m_copied.sem, 1)

                def exps(it):
                    act.wait_ge(x_neg.sem, it + 1)
                    if it >= 2:
                        act.wait_ge(x_turned.sem, it - 1)
                    nc.scalar.activation(pr[:, it % 2, :], psum[:, it % 2, 0:M], ACT.Exp, bias=st[:, it, 1:2], scale=x_scale,
                                         accum_out=st[:, it, 2:3]).then_inc(x_exp.sem, 1)
                exps(0)
                for it in range(XH * TT):
                    h, tile = divmod(it, TT)
                    if it + 1 < XH * TT:
                        exps(it + 1)
                    act.wait_ge(x_turned.sem, it + 1)
                    if h >= 2:
                        act.wait_ge(x_out.sem, 2 * (h - 1))
                    nc.scalar.activation(pr_t[:, h % 2, :, tile * P:(tile + 1) * P], psum[:, 2 + it % 2, 0:M].rearrange("p (m t) -> p m t", m=MT),
                                         ACT.Copy).then_inc(x_copied.sem, 1)
                    if tile == TT - 1:
                        for e in range(2):
                            act.wait_ge(x_out.sem, 2 * h + e + 1)
                            nc.scalar.activation(out_f[:, 2 * h + e, :], psum[:, 6 + e, :], ACT.Copy).then_inc(x_out_copied.sem, 1)

            @block.vector
            def _(dve):
                def maxima(it):
                    dve.wait_ge(x_scored.sem, it + 1)
                    nc.vector.tensor_reduce(st[:, it, 0:1], psum[:, it % 2, 0:M], AX.X, ALU.max).then_inc(x_max.sem, 1)
                    dve.wait_ge(x_max.sem, it + 1)
                    nc.vector.tensor_scalar(st[:, it, 1:2], st[:, it, 0:1], -x_scale, None, ALU.mult).then_inc(x_neg.sem, 1)
                maxima(0)
                for it in range(XH * TT):
                    if it + 1 < XH * TT:
                        maxima(it + 1)
                    dve.wait_ge(x_exp.sem, it + 1)
                    nc.vector.reciprocal(st[:, it, 3:4], st[:, it, 2:3]).then_inc(x_inv.sem, 1)
                    dve.wait_ge(x_inv.sem, it + 1)
                    nc.vector.tensor_scalar(pr[:, it % 2, :], pr[:, it % 2, :], st[:, it, 3:4], None, ALU.mult).then_inc(x_prob.sem, 1)
        with ExitStack() as local:
            out_hi = sb("memory_out_hi", [P, C, T], F32R, local)
            out_lo = sb("memory_out_lo", [P, C, T], F32R, local)
            split([(out_f[:, j, :], 1.0) for j in range(C)], out_hi, out_lo)
            linear(C, (out_hi, out_lo), add_to_x, "vector")
        mem_stack.close()
        if stop == 6:
            return

        with ExitStack() as local:
            act_hi = sb("act_hi", [P, C, T], F32R, local)
            act_lo = sb("act_lo", [P, C, T], F32R, local)
            inner_hi = sb("inner_hi", [P, C, T], F32R, local)
            inner_lo = sb("inner_lo", [P, C, T], F32R, local)
            raw_act = sb("inner_activated", [P, 2, T], F32, local)
            raw_gated = sb("inner_gated", [P, 2, T], F32, local)
            rms_norm(x, 6, out_split=(act_hi, act_lo))
            feed_forward(MLP_GROUPS, (act_hi, act_lo), ACT.Relu, False, inner_hi, inner_lo, raw_act, raw_gated)
        rms_norm(x, 7, out_f32=x)
        stored = sig("output_stored")
        with nc.Block() as block:
            @block.sync
            def _(sp):
                sp.dma_start(out_t, x[:, :, :]).then_inc(stored.sem, 16)
                sp.wait_ge(stored.sem, 16)


def unit_layout(w):
    import numpy as np
    k, n = w.shape
    return np.ascontiguousarray(w.reshape(C, P, n // P, P).transpose(2, 1, 0, 3)).reshape(n // P, P, UNIT)


def constants():
    import numpy as np
    f = np.float32
    pos = np.arange(T, dtype=f)

    def rope(inv, dim, block):
        half = len(inv)
        ang = (pos[:, None] * inv[None, :]).astype(f)
        cos, sin = np.ones((block, T), f), np.zeros((block, T), f)
        swap = np.zeros((block, block), f)
        cos[:half] = cos[half:2 * half] = np.cos(ang).T
        sin[:half], sin[half:2 * half] = -np.sin(ang).T, np.sin(ang).T
        for i in range(half):
            swap[i, i + half] = swap[i + half, i] = 1
        n = P // block
        return np.tile(cos, (n, 1)), np.tile(sin, (n, 1)), np.kron(np.eye(n, dtype=f), swap)

    inv_d = np.power(f(500000.0), -np.arange(8, dtype=f) * f(2.0) / f(16)).astype(f)
    inv_r = (f(1.0) / np.power(f(10000.0), np.linspace(0.0, 1.0, 32, dtype=f))).astype(f)
    cd, sd, swd = rope(inv_d, 16, 64)
    cr, sr, swr = rope(inv_r, 64, 64)
    span = T + (TT - 1) * P
    ahead = (np.arange(span)[None, :] - (TT - 1) * P - np.arange(P)[:, None]).astype(f)
    n = np.arange(P)
    s, t = n[:, None], n[None, :]
    levels = [((s // m) % 2 == 0) & (t // m == s // m + 1) for m in (2, 4, 8, 16, 32, 64)]
    join0 = (s % 2 == 0) & (t == s + 1)
    blocks = np.kron(np.eye(2, dtype=f), np.ones((64, 64), f))
    return {
        "rwkv_sum_masks": np.ascontiguousarray(np.stack([(s <= t) * 1.0 - (s < 64), (s < t) * 1.0 - (s < 64)], 1).astype(f)),
        "rwkv_chunk_masks": np.ascontiguousarray(np.stack([s < t, s <= t, *levels, join0, join0.T, s == t], 1).astype(f)),
        "rwkv_block_ones": blocks,
        "rwkv_block_average": blocks / f(64),
        "rope_tables": np.ascontiguousarray(np.stack([cd, sd, cr, sr], 1)),
        "swap": np.ascontiguousarray(np.stack([swd, swr], 1)),
        "iota_in": np.tile(np.arange(P, dtype=f), (P, 1)),
        "ident_in": np.eye(P, dtype=f),
        "distance": np.ascontiguousarray(np.stack([np.maximum(ahead, 0), np.maximum(-ahead, 0)], 1)),
    }


def expert_units(u, v):
    import numpy as np
    up = u.reshape(P, EXPERT_GROUPS, C, C, P).transpose(1, 2, 4, 3, 0)
    down = v.reshape(P, EXPERT_GROUPS, C, C, P).transpose(1, 3, 0, 2, 4)
    return np.concatenate([up.reshape(-1, C, P, UNIT), down.reshape(-1, C, P, UNIT)], 1).reshape(-1, P, UNIT)


def mlp_units(up, down):
    import numpy as np
    groups = down.shape[0] // D
    ups = unit_layout(up).reshape(groups, C, P, UNIT)
    downs = down.reshape(groups, C, P, C, P).transpose(0, 3, 2, 1, 4).reshape(groups, C, P, UNIT)
    return np.concatenate([ups, downs], 1).reshape(-1, P, UNIT)


def host_layout(inputs):
    import numpy as np

    def by_feature(v):
        return np.ascontiguousarray(v.reshape(-1, P).T)

    def tokens_last(a):
        return np.ascontiguousarray(a.T.reshape(-1, P, a.shape[0]).transpose(1, 0, 2))

    g = {k: np.asarray(v) for k, v in inputs.items()}
    w2 = g["w_in_2"][0]
    rwkv_cols, conv_cols = 1824, 3 * 512
    w_rwkv = np.concatenate([w2[:, :rwkv_cols], np.zeros((D, RWKV_SLABS * P - rwkv_cols), w2.dtype)], 1)
    w_merge = np.stack([unit_layout(np.concatenate([g["w_proj_a_2"][0], g["w_proj_b_2"][0]], 0)),
                        unit_layout(w2[:, rwkv_cols + conv_cols:rwkv_cols + conv_cols + D]),
                        unit_layout(w2[:, rwkv_cols + conv_cols + D:])], 1).reshape(-1, P, UNIT)
    mu = np.concatenate([g["mu_shift_2"][0], np.zeros(RWKV_SLABS * P - rwkv_cols, w2.dtype)])
    vectors = np.concatenate([by_feature(mu), np.zeros((P, 1), w2.dtype)]
                             + [by_feature(g[n][0].reshape(-1)) for n in ("k_k_2", "k_a_2", "r_k_2", "a0_2", "ln_x_w_2", "ln_x_b_2")], 1)
    gains = [g[n].reshape(-1) for n in ("attn_norm_g", "ffn_norm_g", "final_norm_g", "norm_mix_2", "norm_xattn_2",
                                        "norm_mem_2", "norm_mlp_2", "norm_final_2")]
    arrays = {
        "x_t": tokens_last(g["x"][0]),
        "mem_t": tokens_last(g["mem_2"][0]),
        "norm_gains": np.ascontiguousarray(np.stack([by_feature(v) for v in gains], 1)),
        "lam_in": np.ascontiguousarray(np.tile(g["diff_lambda"], (P, 1, 1))),
        "diff_gain": np.ascontiguousarray(g["diff_norm_g"][0].reshape(P, 1)),
        "ret_decay": np.ascontiguousarray(np.tile(g["ret_log_decay"].reshape(1, -1), (P, 1))),
        "ret_gain": np.ascontiguousarray(g["ret_norm_g"][0].T),
        "keys_t": np.ascontiguousarray(g["peer_sub_keys"][0].reshape(LISTS, N_KEYS, P).transpose(2, 0, 1)),
        "rwkv_vectors": np.ascontiguousarray(vectors),
        "rwkv_lora_wa": np.ascontiguousarray(np.concatenate([g["w_lora_w_2"][0], g["w_lora_a_2"][0]], 0)),
        "rwkv_lora_g": np.ascontiguousarray(g["w_lora_g_2"][0]),
        "rwkv_w0": np.ascontiguousarray(g["w0_2"]),
        "conv_taps": np.ascontiguousarray(g["conv_w_2"][0, :, 0, :].T.reshape(4, P, 3).transpose(1, 0, 2)),
        "gate_bias_in": np.ascontiguousarray(g["b_gate_2"][0].reshape(2, C, P).transpose(2, 0, 1)),
        "u_in": unit_layout(g["w_in"][0]),
        "u_out": unit_layout(g["w_out"][0]),
        "u_query": unit_layout(g["peer_w_query"][0]),
        "u_experts": expert_units(g["peer_u"][0], g["peer_v"][0]),
        "u_rwkv": unit_layout(w_rwkv),
        "u_conv": unit_layout(w2[:, rwkv_cols:rwkv_cols + conv_cols]),
        "u_merge": w_merge,
        "u_out_mix": unit_layout(g["w_out_mix_2"][0]),
        "u_kv": unit_layout(g["w_kv_2"][0]),
        "u_q": unit_layout(g["w_q_2"][0]),
        "u_xo": unit_layout(g["w_xo_2"][0]),
        "u_mlp": mlp_units(g["w_up_2"][0], g["w_down_2"][0]),
    }
    arrays.update(constants())
    return arrays


def kernel(**inputs):
    import numpy as np
    import concourse.bacc as bacc
    from concourse.bass_utils import run_bass_kernel_spmd
    arrays = host_layout(inputs)
    nc = bacc.Bacc("TRN2", target_bir_lowering=False, num_devices=1)
    aps = {k: nc.dram_tensor("in_" + k, v.shape, mybir.dt.from_np(v.dtype), kind="ExternalInput").ap() for k, v in arrays.items()}
    out = nc.dram_tensor("out_0_dram", (P, C, T), mybir.dt.float32, kind="ExternalOutput").ap()
    build_program(nc, aps, out)
    r = run_bass_kernel_spmd(nc, [{"in_" + k: v for k, v in arrays.items()}], core_ids=[0])
    got = np.asarray(r.results[0]["out_0_dram"])
    return np.ascontiguousarray(got.transpose(2, 1, 0).reshape(1, T, D))
```

```python
import math

import concourse.bass as bass
from concourse import mybir
from contextlib import ExitStack

F32 = mybir.dt.float32
F32R = mybir.dt.float32r
U32 = mybir.dt.uint32
ALU = mybir.AluOpType
ACT = mybir.ActivationFunctionType
AX = mybir.AxisListType

P = 128
T = 512
TT = T // P
D = 1024
C = D // P
UNIT = C * P
RING = 4
EPS = 1e-6

IN_SLABS = 24
DQ, DK, DV, RQ, RK, RV, RG = 0, 4, 8, 12, 14, 16, 20
HEADS = 4
N_KEYS = 128
DIFF_QK = 64
RET_QK = 64
LAMBDA_INIT = 0.8 - 0.6
PEER_HEADS = 8
TOPK = 16
LOWEST = -3.0e38
LISTS = 2 * PEER_HEADS
PICKS = PEER_HEADS * TOPK
EXPERT_GROUPS = N_KEYS // C
MLP_GROUPS = 4
M = 256
RWKV_SLABS = 15
RWKV_LN_EPS = 64e-5
GT = 64
GBLOCKS = T // GT
UP_TILE = C + 2
UP_DENSE = 2 * C
UP_TAIL = C // 2
UP_FIRST = C // 2
GROUPS_AHEAD = (TT * UP_TILE + UP_DENSE + UP_TAIL + UP_FIRST) // C


class Signal:

    def __init__(self, ctx, nc, name):
        self.sem = ctx.enter_context(nc.semaphore(name))
        self.base = 0

    def at(self, n):
        return n + self.base


class Weights:

    AHEAD = 2

    def __init__(self, ctx, nc, sources):
        self.nc = nc
        self.raw = ctx.enter_context(nc.sbuf_tensor("weights_raw", [P, RING, UNIT], F32))
        self.hi = [ctx.enter_context(nc.sbuf_tensor(f"weights_hi{k}", [P, C, P], F32R)) for k in range(RING)]
        self.lo = [ctx.enter_context(nc.sbuf_tensor(f"weights_lo{k}", [P, C, P], F32R)) for k in range(RING)]
        self.loaded = [Signal(ctx, nc, f"weights_loaded{k}") for k in range(RING)]
        self.hi_ready = Signal(ctx, nc, "weights_hi_ready")
        self.lo_ready = Signal(ctx, nc, "weights_lo_ready")
        self.unit_done = Signal(ctx, nc, "unit_done")
        self.sources = sources
        self.total = sum(n for _, n in sources)
        self.u0 = 0

    def source(self, v):
        for dram, n in self.sources:
            if v < n:
                return dram, v
            v -= n
        raise IndexError

    def done(self, k):
        return k + (self.u0 + RING + 1)

    def load(self, sp, k, slot, dram, index, free=True):
        if free:
            sp.wait_ge(self.lo_ready.sem, k + (self.u0 + 1 - RING))
        sp.dma_start(self.raw[:, slot, :], dram[index]).then_inc(self.loaded[slot].sem, 16)

    def load_first(self, sp):
        for v in range(RING):
            dram, index = self.source(v)
            self.load(sp, v, v, dram, index, free=False)

    def load_stage(self, sp, n):
        first, last = self.u0 + RING, min(self.u0 + RING + n, self.total)
        v = first
        while v < last:
            dram, index = self.source(v)
            run = min(last - v, dram.shape[0] - index)
            if run >= 2 * RING:
                with sp.Fori(0, run // RING) as i:
                    for k in range(RING):
                        self.load(sp, i * RING + (v + k - self.u0), (v + k) % RING, dram, i * RING + (index + k))
                run -= run % RING
            else:
                for k in range(run):
                    self.load(sp, v + k - self.u0, (v + k) % RING, dram, index + k)
            v += run

    def hi_step(self, act, loop, k, per):
        slot = (self.u0 + k) % RING
        turn = (self.u0 + k - slot) // RING + 1
        act.wait_ge(self.loaded[slot].sem, 16 * turn if loop is None else loop * (16 * per // RING) + 16 * turn)
        act.wait_ge(self.unit_done.sem, self.u0 + k + 1 if loop is None else loop * per + (self.u0 + k + 1))
        self.nc.scalar.activation(self.hi[slot][:, :, :], self.raw[:, slot, :].rearrange("p (c n) -> p c n", c=C),
                                  ACT.Copy).then_inc(self.hi_ready.sem, 1)

    def lo_step(self, eng, loop, k, per):
        slot = (self.u0 + k) % RING
        eng.wait_ge(self.hi_ready.sem, self.u0 + k + 1 if loop is None else loop * per + (self.u0 + k + 1))
        eng.tensor_tensor(self.lo[slot][:, :, :], self.raw[:, slot, :].rearrange("p (c n) -> p c n", c=C),
                                     self.hi[slot][:, :, :].bitcast(F32), ALU.subtract).then_inc(self.lo_ready.sem, 1)

    def multiply_chunk(self, pe, loop, k, per, out, acts, c):
        slot = (self.u0 + k) % RING
        if c == 0:
            pe.wait_ge(self.lo_ready.sem, loop * per + (self.u0 + k + 1))
        for n, (w, a) in enumerate(((self.hi, acts[0]), (self.hi, acts[1]), (self.lo, acts[0]))):
            mm = self.nc.tensor.matmul(out, w[slot][:, c, :], a[:, c, :], start=c == 0 and n == 0, stop=c == C - 1 and n == 2)
        return mm

    def multiply(self, pe, loop, k, per, out, acts, first=True, last=True, chunks=range(C), tokens=T, before_chunk=None):
        slot = (self.u0 + k) % RING
        pe.wait_ge(self.lo_ready.sem, self.u0 + k + 1 if loop is None else loop * per + (self.u0 + k + 1))
        hi, lo = acts
        n = 0
        for j, c in enumerate(chunks):
            if before_chunk:
                before_chunk(c)
            for w, a in ((self.hi, hi), (self.hi, lo), (self.lo, hi)):
                n += 1
                mm = self.nc.tensor.matmul(out, w[slot][:, c, :], a[:, j, 0:tokens],
                                           start=first and n == 1, stop=last and n == 3 * len(chunks))
        return mm


def build_program(nc, aps, out_t, stop=99):
    (x_t, norm_gains, rope_tables, swap, ident_in, distance, lam_in, diff_gain, ret_decay, ret_gain, keys_t, iota_in,
     conv_taps, gate_bias_in, mem_t) = (aps[n] for n in (
         "x_t", "norm_gains", "rope_tables", "swap", "ident_in", "distance", "lam_in", "diff_gain", "ret_decay", "ret_gain",
         "keys_t", "iota_in", "conv_taps", "gate_bias_in", "mem_t"))
    rwkv = {k[5:]: v for k, v in aps.items() if k.startswith("rwkv_")}
    units = [(v, v.shape[0]) for k, v in aps.items() if k.startswith("u_")]
    ctx = ExitStack()
    with ctx:
        uses = {}

        def fresh(name):
            uses[name] = uses.get(name, 0) + 1
            return name if uses[name] == 1 else f"{name}_{uses[name]}"

        def sb(name, shape, dt=F32, c=None):
            name = fresh(name)
            return (c or ctx).enter_context(nc.sbuf_tensor(name, shape, dt))

        def sig(name):
            return Signal(ctx, nc, name)

        weights = Weights(ctx, nc, units)
        gates_dram = nc.dram_tensor("gates_dram", [GBLOCKS, P, N_KEYS * GT], F32).ap()
        x = sb("x", [P, C, T])
        gains = sb("gains", [P, 8, C])
        ident = sb("ident", [P, P])
        ones = sb("ones", [P, P])
        psum = ctx.enter_context(nc.psum_tensor("psum", [P, 8, T], F32))
        consts_loaded = sig("consts_loaded")
        norm_sq = sig("norm_squares_ready")
        norm_acc = sig("norm_partial_sums_ready")
        norm_sum = sig("norm_sum_ready")
        norm_root = sig("norm_root_ready")
        norm_rstd = sig("norm_rstd_ready")
        norm_y = sig("norm_scaled_ready")
        norm_hi = sig("norm_hi_ready")

        def rms_norm(src, gain, out_f32=None, out_split=None, width=T, before=None):
            with ExitStack() as local, nc.Block() as block:
                sq = sb("norm_squares", [P, 2, width], F32, local)
                acc = sb("norm_sums", [P, 2, width], F32, local)
                rstd = sb("norm_rstd", [P, width], F32, local)
                y = out_f32 if out_f32 is not None else sb("norm_scaled", [P, 2, width], F32, local)
                total = psum[:, 7, 0:width]

                @block.sync
                def _(sp):
                    if before:
                        before(sp)

                @block.scalar
                def _(act):
                    if before:
                        act.wait_ge(consts_loaded.sem, 16 * before.loads)
                    for c in range(C):
                        if c >= 2:
                            act.wait_ge(norm_acc.sem, norm_acc.at(c - 1))
                        nc.scalar.activation(sq[:, c % 2, :], src[:, c, 0:width], ACT.Square).then_inc(norm_sq.sem, 1)
                    act.wait_ge(norm_sum.sem, norm_sum.at(1))
                    nc.scalar.activation(rstd[:], total, ACT.Ln, bias=eps_ap[:, 0:1], scale=1.0 / D).then_inc(norm_root.sem, 1)
                    act.wait_ge(norm_root.sem, norm_root.at(1))
                    nc.scalar.activation(rstd[:], rstd[:], ACT.Exp, scale=-0.5).then_inc(norm_rstd.sem, 1)
                    if out_split:
                        for c in range(C):
                            act.wait_ge(norm_y.sem, norm_y.at(c + 1))
                            nc.scalar.activation(out_split[0][:, c, :], y[:, c % 2, :], ACT.Copy).then_inc(norm_hi.sem, 1)

                @block.tensor
                def _(pe):
                    pe.wait_ge(norm_acc.sem, norm_acc.at(C))
                    nc.tensor.matmul(total, ones[:], acc[:, 1, :], start=True, stop=True).then_inc(norm_sum.sem, 1)

                @block.vector
                def _(dve):
                    for c in range(C):
                        dve.wait_ge(norm_sq.sem, norm_sq.at(c + 1))
                        if c == 0:
                            nc.vector.tensor_copy(acc[:, 0, :], sq[:, 0, :]).then_inc(norm_acc.sem, 1)
                        else:
                            dve.wait_ge(norm_acc.sem, norm_acc.at(c))
                            nc.vector.tensor_tensor(acc[:, c % 2, :], acc[:, (c - 1) % 2, :], sq[:, c % 2, :],
                                                    ALU.add).then_inc(norm_acc.sem, 1)
                    dve.wait_ge(norm_rstd.sem, norm_rstd.at(1))
                    for c in range(C):
                        if out_split and c >= 2:
                            dve.wait_ge(norm_hi.sem, norm_hi.at(c - 1))
                        yc = y[:, c % 2, :] if out_split else y[:, c, 0:width]
                        nc.vector.scalar_tensor_tensor(yc, src[:, c, 0:width], gains[:, gain, c:c + 1], rstd[:],
                                                       ALU.mult, ALU.mult).then_inc(norm_y.sem, 1)
                        if out_split:
                            dve.wait_ge(norm_hi.sem, norm_hi.at(c + 1))
                            nc.vector.tensor_tensor(out_split[1][:, c, :], y[:, c % 2, :],
                                                    out_split[0][:, c, :].bitcast(F32), ALU.subtract)
            for s in (norm_sq, norm_acc, norm_y):
                s.base += C
            if out_split:
                norm_hi.base += C
            for s in (norm_sum, norm_root, norm_rstd):
                s.base += 1

        rstd = sb("rstd", [P, T])
        pre_hi, pre_lo, pre_sq, pre_acc = sig("operand_hi_ready"), sig("operand_lo_ready"), sig("operand_squares_ready"), sig("operand_squares_summed")
        pre_sum, pre_log, pre_rstd = sig("operand_sum_ready"), sig("operand_log_ready"), sig("rstd_ready")

        class Norm:

            def __init__(self, src, gain, hi, lo, width, local, loads=0):
                self.src, self.gain, self.hi, self.lo, self.width, self.loads = src, gain, hi, lo, width, loads
                self.sq = sb("operand_squares", [P, 2, width], F32, local)
                self.acc = sb("operand_sums", [P, 2, width], F32, local)

            def loaded(self, eng):
                if self.loads:
                    eng.wait_ge(consts_loaded.sem, 16 * self.loads)

            def scalar_hi(self, act):
                self.loaded(act)
                for c in range(C):
                    nc.scalar.activation(self.hi[:, c, :], self.src[:, c, 0:self.width], ACT.Copy,
                                         scale=gains[:, self.gain, c:c + 1]).then_inc(pre_hi.sem, 1)

            def scalar_rstd(self, act):
                act.wait_ge(pre_sum.sem, pre_sum.at(1))
                r = rstd[:, 0:self.width]
                nc.scalar.activation(r, psum[:, 7, 0:self.width], ACT.Ln, bias=eps_ap[:, 0:1], scale=1.0 / D).then_inc(pre_log.sem, 1)
                act.wait_ge(pre_log.sem, pre_log.at(1))
                nc.scalar.activation(r, r, ACT.Exp, scale=-0.5).then_inc(pre_rstd.sem, 1)

            def vector(self, dve):
                self.loaded(dve)
                for c in range(C):
                    dve.wait_ge(pre_hi.sem, pre_hi.at(c + 1))
                    nc.vector.scalar_tensor_tensor(self.lo[:, c, :], self.src[:, c, 0:self.width], gains[:, self.gain, c:c + 1],
                                                   self.hi[:, c, :].bitcast(F32), ALU.mult, ALU.subtract).then_inc(pre_lo.sem, 1)
                    dve.wait_ge(pre_sq.sem, pre_sq.at(c + 1))
                    if c == 0:
                        nc.vector.tensor_copy(self.acc[:, 0, :], self.sq[:, 0, :]).then_inc(pre_acc.sem, 1)
                    else:
                        dve.wait_ge(pre_acc.sem, pre_acc.at(c))
                        nc.vector.tensor_tensor(self.acc[:, c % 2, :], self.acc[:, (c - 1) % 2, :], self.sq[:, c % 2, :],
                                                ALU.add).then_inc(pre_acc.sem, 1)

            def gpsimd(self, pool):
                self.loaded(pool)
                for c in range(C):
                    if c >= 2:
                        pool.wait_ge(pre_acc.sem, pre_acc.at(c - 1))
                    part = self.src[:, c, 0:self.width]
                    nc.gpsimd.tensor_tensor(self.sq[:, c % 2, :], part, part, ALU.mult).then_inc(pre_sq.sem, 1)

            def tensor(self, pe):
                pe.wait_ge(pre_acc.sem, pre_acc.at(C))
                nc.tensor.matmul(psum[:, 7, 0:self.width], ones[:], self.acc[:, 1, :], start=True, stop=True).then_inc(pre_sum.sem, 1)

            def end(self):
                for s in (pre_hi, pre_lo, pre_sq, pre_acc):
                    s.base += C
                for s in (pre_sum, pre_log, pre_rstd):
                    s.base += 1

        def norm_alone(src, gain, hi, lo):
            with ExitStack() as local, nc.Block() as block:
                norm = Norm(src, gain, hi, lo, T, local)

                @block.scalar
                def _(act):
                    norm.scalar_hi(act)
                    norm.scalar_rstd(act)

                @block.vector
                def _(dve):
                    norm.vector(dve)

                @block.gpsimd
                def _(pool):
                    norm.gpsimd(pool)

                @block.tensor
                def _(pe):
                    norm.tensor(pe)
            norm.end()

        out_free = sig("product_read")

        def linear(n, acts, evacuate, engine, tokens=T, prologue=False, norm=None, before=None):
            w = weights
            head = RING if norm else 0
            loops = (n - head) // RING
            rest = range(head + loops * RING, n)
            u0, base = w.u0, out_free.base
            split_until = w.total - w.AHEAD - u0

            def bank(k):
                return (u0 + k) % 4

            with ExitStack() as local, nc.Block() as block:
                pre = Norm(norm[0], norm[1], acts[0], acts[1], tokens, local, before.loads if before else 0) if norm else None

                @block.sync
                def _(sp):
                    if before:
                        before(sp)
                    w.load_stage(sp, n)

                def evac(eng, loop, k):
                    eng.wait_ge(w.unit_done.sem, w.done(k) if loop is None else loop * RING + w.done(k))
                    evacuate(loop, k, psum[:, bank(k), 0:tokens]).then_inc(out_free.sem, 1)

                def run(eng, step, mine, make, ready):
                    if prologue:
                        for k in range(w.AHEAD):
                            step(eng, None, k, RING)
                    if pre:
                        make(eng)
                        step(eng, None, 2, RING)
                        step(eng, None, 3, RING)
                        ready(eng)
                        for k in range(RING):
                            if mine:
                                evac(eng, None, k)
                            if k >= 2:
                                step(eng, None, k + 2, RING)
                    if loops:
                        with eng.Fori(0, loops) as i:
                            for k in range(RING):
                                step(eng, i, head + k + w.AHEAD, RING)
                                if mine:
                                    evac(eng, i, head + k)
                    for k in rest:
                        if k < split_until:
                            step(eng, None, k + w.AHEAD, RING)
                        if mine:
                            evac(eng, None, k)

                @block.scalar
                def _(act):
                    run(act, w.hi_step, engine == "scalar", pre and pre.scalar_hi, pre and pre.scalar_rstd)

                @block.vector
                def _(dve):
                    def rstd_there(dve):
                        dve.wait_ge(pre_rstd.sem, pre_rstd.at(1))
                    run(dve, w.lo_step, engine == "vector", pre and pre.vector, rstd_there)

                if pre:
                    @block.gpsimd
                    def _(pool):
                        pre.gpsimd(pool)

                @block.tensor
                def _(pe):
                    def chunk_there(c):
                        pe.wait_ge(pre_lo.sem, pre_lo.at(c + 1))

                    def product(loop, k, before_chunk=None):
                        pe.wait_ge(out_free.sem, base + k + 1 if loop is None else loop * RING + (base + k + 1))
                        w.multiply(pe, loop, k, RING, psum[:, bank(k), 0:tokens], acts,
                                   tokens=tokens, before_chunk=before_chunk).then_inc(w.unit_done.sem, 1)
                    if prologue:
                        pe.sem_inc(w.unit_done.sem, RING)
                        pe.sem_inc(out_free.sem, RING)
                    if pre:
                        for k in range(RING):
                            product(None, k, chunk_there if k == 0 else None)
                            if k == 1:
                                pre.tensor(pe)
                    if loops:
                        with pe.Fori(0, loops) as i:
                            for k in range(RING):
                                product(i, head + k)
                    for k in rest:
                        product(None, k)
            w.u0 += n
            out_free.base += n
            if pre:
                pre.end()

        def scaled(dst, tokens=T):
            return lambda loop, k, bank: nc.vector.tensor_tensor(dst(at(loop, k)), bank, rstd[:, 0:tokens], ALU.mult)

        def at(loop, k):
            return k if loop is None else loop * RING + k

        eps_ap = sb("eps", [P, 1])

        def load_start(sp):
            sp.dma_start(x[:, :, :], x_t).then_inc(consts_loaded.sem, 16)
            sp.dma_start(gains[:, :, :], norm_gains).then_inc(consts_loaded.sem, 16)
            weights.load_first(sp)
            sp.dma_start(ident[:], ident_in).then_inc(consts_loaded.sem, 16)
        load_start.loads = 3

        ones_set = sig("ones_set")
        with nc.Block() as block:
            @block.gpsimd
            def _(pool):
                nc.gpsimd.memset(ones[:], 1.0).then_inc(ones_set.sem, 1)
                nc.gpsimd.memset(eps_ap[:], EPS).then_inc(ones_set.sem, 1)

        mix_stack = ExitStack()
        ctx.enter_context(mix_stack)
        proj = sb("projections", [P, IN_SLABS, T], F32, mix_stack)
        act_stack = ExitStack()
        act_hi = sb("act_hi_a", [P, C, T], F32R, act_stack)
        act_lo = sb("act_lo_a", [P, C, T], F32R, act_stack)
        linear(IN_SLABS, (act_hi, act_lo), scaled(lambda n: proj[:, n, :]), "vector", prologue=True, norm=(x, 0), before=load_start)
        act_stack.close()

        gn_mean = sig("head_mean_ready")
        gn_centred = sig("head_centred")
        gn_square = sig("head_square_ready")
        gn_var = sig("head_variance_ready")
        gn_floor = sig("head_variance_floored")
        gn_log = sig("head_log_ready")
        gn_rstd = sig("head_rstd_ready")
        gn_out = sig("head_scaled")

        def head_norm(src, average, eps, center, floor=None):
            with ExitStack() as local, nc.Block() as block:
                sq = sb("head_squares", [P, 2, T], F32, local)
                rstd = sb("head_rstd", [P, 2, T], F32, local)

                @block.tensor
                def _(pe):
                    if center:
                        for j in range(4):
                            nc.tensor.matmul(psum[:, j, :], average, src[:, j, :], start=True, stop=True).then_inc(gn_mean.sem, 1)
                    for j in range(4):
                        pe.wait_ge(gn_square.sem, gn_square.at(j + 1))
                        nc.tensor.matmul(psum[:, 4 + j, :], average, sq[:, j % 2, :], start=True, stop=True).then_inc(gn_var.sem, 1)

                @block.scalar
                def _(act):
                    def square(j):
                        if center:
                            act.wait_ge(gn_centred.sem, gn_centred.at(j + 1))
                        if j >= 2:
                            act.wait_ge(gn_var.sem, gn_var.at(j - 1))
                        nc.scalar.activation(sq[:, j % 2, :], src[:, j, :], ACT.Square).then_inc(gn_square.sem, 1)
                    square(0)
                    for j in range(4):
                        if j < 3:
                            square(j + 1)
                        if floor is not None:
                            act.wait_ge(gn_floor.sem, gn_floor.at(j + 1))
                        else:
                            act.wait_ge(gn_var.sem, gn_var.at(j + 1))
                            if j >= 2:
                                act.wait_ge(gn_out.sem, gn_out.at(j - 1))
                        source = rstd[:, j % 2, :] if floor is not None else psum[:, 4 + j, :]
                        nc.scalar.activation(rstd[:, j % 2, :], source, ACT.Ln, bias=eps, scale=1.0).then_inc(gn_log.sem, 1)
                        act.wait_ge(gn_log.sem, gn_log.at(j + 1))
                        nc.scalar.activation(rstd[:, j % 2, :], rstd[:, j % 2, :], ACT.Exp, scale=-0.5).then_inc(gn_rstd.sem, 1)

                @block.vector
                def _(dve):
                    if center:
                        for j in range(4):
                            dve.wait_ge(gn_mean.sem, gn_mean.at(j + 1))
                            nc.vector.tensor_tensor(src[:, j, :], src[:, j, :], psum[:, j, :], ALU.subtract).then_inc(gn_centred.sem, 1)

                    def floored(j):
                        dve.wait_ge(gn_var.sem, gn_var.at(j + 1))
                        if j >= 2:
                            dve.wait_ge(gn_out.sem, gn_out.at(j - 1))
                        nc.vector.tensor_scalar(rstd[:, j % 2, :], psum[:, 4 + j, :], floor, None, ALU.max).then_inc(gn_floor.sem, 1)
                    if floor is not None:
                        floored(0)
                    for j in range(4):
                        if floor is not None and j < 3:
                            floored(j + 1)
                        dve.wait_ge(gn_rstd.sem, gn_rstd.at(j + 1))
                        nc.vector.tensor_tensor(src[:, j, :], src[:, j, :], rstd[:, j % 2, :], ALU.mult).then_inc(gn_out.sem, 1)
            for s, used in ((gn_mean, center), (gn_centred, center), (gn_square, True), (gn_var, True), (gn_floor, floor is not None),
                            (gn_log, True), (gn_rstd, True), (gn_out, True)):
                s.base += 4 * used

        split_hi_ready = sig("split_hi_ready")

        def split(slabs, hi, lo, at_slab=0):
            with nc.Block() as block:
                @block.scalar
                def _(act):
                    for j, (src, gain) in enumerate(slabs):
                        nc.scalar.activation(hi[:, at_slab + j, :], src, ACT.Copy, scale=gain).then_inc(split_hi_ready.sem, 1)

                @block.vector
                def _(dve):
                    for j, (src, gain) in enumerate(slabs):
                        dve.wait_ge(split_hi_ready.sem, split_hi_ready.at(j + 1))
                        nc.vector.scalar_tensor_tensor(lo[:, at_slab + j, :], src, gain, hi[:, at_slab + j, :].bitcast(F32),
                                                       ALU.mult, ALU.subtract)
            split_hi_ready.base += len(slabs)

        mix_hi = sb("mix_hi", [P, C, T], F32R, mix_stack)
        mix_lo = sb("mix_lo", [P, C, T], F32R, mix_stack)
        v_tok = sb("values_by_token", [P, 2 * HEADS, T], F32, mix_stack)
        average128 = sb("average128", [P, P], F32, mix_stack)
        small = sb("attention_scalars", [P, 64], F32, mix_stack)
        neg_lam, gain_d, gain_r, lgf = small[:, 0:1], small[:, 4:5], small[:, 8:12], small[:, 16:24]
        lam_v = sb("lambda_vectors", [P, 4, 64], F32, mix_stack)
        lam_loaded = sig("attention_scalars_loaded")
        tables_loaded = sig("tables_loaded")
        rope_swapped, rope_cos, rope_sin, rope_done = (sig(n) for n in ("rope_swapped", "rope_cos", "rope_sin", "rope_done"))
        v_turned = sig("values_transposed")
        v_copied = sig("values_copied")
        lam_step = sig("lambda_step")
        lam_exp = sig("lambda_exp_ready")
        rotary = [(n, 0) for n in range(DQ, DV)] + [(n, 1) for n in range(RQ, RV)]
        values = list(range(DV, DV + HEADS)) + list(range(RV, RV + HEADS))
        with ExitStack() as local, nc.Block() as block:
            tables = sb("rope_tables_sb", [P, 4, T], F32, local)
            swaps = sb("rope_swaps", [P, 2, P], F32, local)
            by_cos = sb("rope_by_cos", [P, 2, T], F32, local)
            by_sin = sb("rope_by_sin", [P, 2, T], F32, local)

            @block.sync
            def _(sp):
                sp.dma_start(tables[:, :, :], rope_tables).then_inc(tables_loaded.sem, 16)
                sp.dma_start(swaps[:, :, :], swap).then_inc(tables_loaded.sem, 16)
                sp.dma_start(lam_v[:, :, :], lam_in).then_inc(lam_loaded.sem, 16)
                sp.dma_start(small[:, 4:5], diff_gain).then_inc(lam_loaded.sem, 16)
                sp.dma_start(small[:, 8:12], ret_gain).then_inc(lam_loaded.sem, 16)
                sp.dma_start(small[:, 16:24], ret_decay).then_inc(lam_loaded.sem, 16)

            @block.tensor
            def _(pe):
                for j, n in enumerate(values):
                    if j >= 2:
                        pe.wait_ge(v_copied.sem, j - 1)
                    for tile in range(TT):
                        mm = nc.tensor.transpose(psum[:, 4 + j % 2, tile * P:(tile + 1) * P], proj[:, n, tile * P:(tile + 1) * P], ident[:])
                    mm.then_inc(v_turned.sem, 1)
                pe.wait_ge(tables_loaded.sem, 32)
                for j, (n, kind) in enumerate(rotary):
                    if j >= 2:
                        pe.wait_ge(rope_sin.sem, j - 1)
                    nc.tensor.matmul(psum[:, j % 2, :], swaps[:, kind, :], proj[:, n, :], start=True, stop=True).then_inc(rope_swapped.sem, 1)

            @block.scalar
            def _(act):
                for j in range(len(values)):
                    act.wait_ge(v_turned.sem, j + 1)
                    nc.scalar.activation(v_tok[:, j, :], psum[:, 4 + j % 2, :], ACT.Copy).then_inc(v_copied.sem, 1)
                act.wait_ge(lam_loaded.sem, 64)
                act.wait_ge(lam_step.sem, 2)
                nc.scalar.activation(small[:, 2:4], small[:, 2:4], ACT.Exp).then_inc(lam_exp.sem, 1)
                nc.scalar.activation(lgf, lgf, ACT.Exp).then_inc(lam_exp.sem, 1)

            @block.gpsimd
            def _(pool):
                nc.gpsimd.memset(average128[:], 1.0 / P)
                pool.wait_ge(tables_loaded.sem, 32)
                for j, (n, kind) in enumerate(rotary):
                    if j >= 2:
                        pool.wait_ge(rope_done.sem, j - 1)
                    nc.gpsimd.tensor_tensor(by_cos[:, j % 2, :], proj[:, n, :], tables[:, 2 * kind, :], ALU.mult).then_inc(rope_cos.sem, 1)

            @block.vector
            def _(dve):
                for j, (n, kind) in enumerate(rotary):
                    dve.wait_ge(rope_swapped.sem, j + 1)
                    if j == 0:
                        dve.wait_ge(tables_loaded.sem, 32)
                    if j >= 2:
                        dve.wait_ge(rope_done.sem, j - 1)
                    nc.vector.tensor_tensor(by_sin[:, j % 2, :], psum[:, j % 2, :], tables[:, 2 * kind + 1, :], ALU.mult).then_inc(rope_sin.sem, 1)
                    dve.wait_ge(rope_cos.sem, j + 1)
                    dve.wait_ge(rope_sin.sem, j + 1)
                    nc.vector.tensor_tensor(proj[:, n, :], by_cos[:, j % 2, :], by_sin[:, j % 2, :], ALU.add).then_inc(rope_done.sem, 1)
                dve.wait_ge(lam_loaded.sem, 64)
                nc.vector.tensor_tensor(lam_v[:, 0::2, :], lam_v[:, 0::2, :], lam_v[:, 1::2, :], ALU.mult).then_inc(lam_step.sem, 1)
                dve.wait_ge(lam_step.sem, 1)
                nc.vector.tensor_reduce(small[:, 2:4], lam_v[:, 0::2, :], AX.X, ALU.add).then_inc(lam_step.sem, 1)
                dve.wait_ge(lam_exp.sem, 2)
                nc.vector.tensor_tensor(neg_lam, small[:, 3:4], small[:, 2:3], ALU.subtract).then_inc(lam_step.sem, 1)
                dve.wait_ge(lam_step.sem, 3)
                nc.vector.tensor_scalar(neg_lam, neg_lam, -LAMBDA_INIT, None, ALU.add)
                nc.vector.tensor_scalar(gain_d, gain_d, 1.0 - LAMBDA_INIT, None, ALU.mult)
                nc.vector.tensor_scalar(lgf, lgf, -1.0, None, ALU.mult)

        scored, maxed, neg_maxed, exped = (sig(n) for n in ("diff_scores_ready", "diff_max_ready", "diff_neg_max_ready", "diff_exp_ready"))
        inv_ready, scaled0, combined = (sig(n) for n in ("diff_inverse_sum_ready", "diff_first_map_scaled", "diff_maps_combined"))
        turned, turned_read, mixed, mixed_read = (sig(n) for n in ("diff_map_transposed", "diff_map_copied", "diff_out_ready", "diff_out_copied"))
        heads_out = sb("diff_heads_out", [P, HEADS, T], F32, mix_stack)
        scale = DIFF_QK ** -0.5
        steps = HEADS * TT
        with ExitStack() as local, nc.Block() as block:
            probs = sb("diff_probs", [P, 2, 2, T], F32, local)
            amap = sb("diff_map", [P, 2, T], F32, local)
            amap_t = sb("diff_map_t", [P, 2, TT, T], F32, local)
            stats = sb("diff_stats", [P, steps, 8], F32, local)

            @block.tensor
            def _(pe):
                def scores(it):
                    h, q = divmod(it, TT)
                    if it >= 3:
                        pe.wait_ge(exped.sem, 2 * (it - 2))
                    for m in range(2):
                        rows = slice(64 * m, 64 * m + 64)
                        nc.tensor.matmul(psum[:, 2 * (it % 3) + m, :], proj[rows, DQ + h, q * P:(q + 1) * P],
                                         proj[rows, DK + h, :], start=True, stop=True).then_inc(scored.sem, 1)
                scores(0)
                scores(1)
                for it in range(steps):
                    h, q = divmod(it, TT)
                    if it + 2 < steps:
                        scores(it + 2)
                    pe.wait_ge(combined.sem, it + 1)
                    if it >= 1:
                        pe.wait_ge(turned_read.sem, it)
                    for kt in range(TT):
                        mm = nc.tensor.transpose(psum[:, 6, kt * P:(kt + 1) * P], amap[:, it % 2, kt * P:(kt + 1) * P], ident[:])
                    mm.then_inc(turned.sem, 1)
                    if q == TT - 1:
                        pe.wait_ge(turned_read.sem, it + 1)
                        if h >= 1:
                            pe.wait_ge(mixed_read.sem, h)
                        for kt in range(TT):
                            mm = nc.tensor.matmul(psum[:, 7, :], v_tok[:, h, kt * P:(kt + 1) * P],
                                                  amap_t[:, h % 2, kt, :], start=kt == 0, stop=kt == TT - 1)
                        mm.then_inc(mixed.sem, 1)

            @block.scalar
            def _(act):
                def exps(it):
                    act.wait_ge(neg_maxed.sem, it + 1)
                    if it >= 2:
                        act.wait_ge(combined.sem, it - 1)
                    for m in range(2):
                        nc.scalar.activation(probs[:, it % 2, m, :], psum[:, 2 * (it % 3) + m, :], ACT.Exp, bias=stats[:, it, 2 + m:3 + m],
                                             scale=scale, accum_out=stats[:, it, 4 + m:5 + m]).then_inc(exped.sem, 1)
                exps(0)
                for it in range(steps):
                    h, q = divmod(it, TT)
                    if it + 1 < steps:
                        exps(it + 1)
                    act.wait_ge(turned.sem, it + 1)
                    if h >= 2:
                        act.wait_ge(mixed.sem, h - 1)
                    nc.scalar.activation(amap_t[:, h % 2, :, q * P:(q + 1) * P], psum[:, 6, :].rearrange("p (k q) -> p k q", k=TT),
                                         ACT.Copy).then_inc(turned_read.sem, 1)
                    if q == TT - 1:
                        act.wait_ge(mixed.sem, h + 1)
                        nc.scalar.activation(heads_out[:, h, :], psum[:, 7, :], ACT.Copy).then_inc(mixed_read.sem, 1)

            @block.vector
            def _(dve):
                def maxima(it):
                    dve.wait_ge(scored.sem, 2 * (it + 1))
                    nc.vector.tensor_reduce(stats[:, it, 0:2], psum[:, 2 * (it % 3):2 * (it % 3) + 2, :], AX.X, ALU.max).then_inc(maxed.sem, 1)
                    dve.wait_ge(maxed.sem, it + 1)
                    nc.vector.tensor_scalar(stats[:, it, 2:4], stats[:, it, 0:2], -scale, None, ALU.mult).then_inc(neg_maxed.sem, 1)
                maxima(0)
                maxima(1)
                for it in range(steps):
                    dve.wait_ge(exped.sem, 2 * (it + 1))
                    nc.vector.reciprocal(stats[:, it, 6:8], stats[:, it, 4:6]).then_inc(inv_ready.sem, 1)
                    dve.wait_ge(inv_ready.sem, 2 * it + 1)
                    nc.vector.tensor_tensor(stats[:, it, 7:8], stats[:, it, 7:8], neg_lam, ALU.mult).then_inc(inv_ready.sem, 1)
                    nc.vector.tensor_scalar(probs[:, it % 2, 0, :], probs[:, it % 2, 0, :], stats[:, it, 6:7], None, ALU.mult).then_inc(scaled0.sem, 1)
                    dve.wait_ge(inv_ready.sem, 2 * it + 2)
                    dve.wait_ge(scaled0.sem, it + 1)
                    if it >= 2:
                        dve.wait_ge(turned.sem, it - 1)
                    nc.vector.scalar_tensor_tensor(amap[:, it % 2, :], probs[:, it % 2, 1, :], stats[:, it, 7:8], probs[:, it % 2, 0, :],
                                                   ALU.mult, ALU.add).then_inc(combined.sem, 1)
                    if it + 2 < steps:
                        maxima(it + 2)

        head_norm(heads_out, average128[:], eps_ap[:, 0:1], center=False)
        split([(heads_out[:, h, :], gain_d) for h in range(HEADS)], mix_hi, mix_lo)

        dist_loaded, arg0_ready, arg_ready, decay_ready = (sig(n) for n in ("distances_loaded", "decay_half_ready", "decay_log_ready", "decay_ready"))
        ret_scored, ret_decayed, ret_mixed, ret_read = (sig(n) for n in ("ret_scores_ready", "ret_scores_decayed", "ret_out_ready", "ret_out_copied"))
        gate_ready = sig("ret_gate_ready")
        SPAN = T + (TT - 1) * P
        with ExitStack() as local, nc.Block() as block:
            dist = sb("ret_distances", [P, 2, SPAN], F32, local)
            args = sb("ret_decay_log", [P, 2, SPAN], F32, local)
            decay = sb("ret_decay", [P, 2, SPAN], F32, local)
            weighed = sb("ret_scores", [P, 4, T], F32, local)

            @block.sync
            def _(sp):
                sp.dma_start(dist[:, :, :], distance).then_inc(dist_loaded.sem, 16)

            @block.tensor
            def _(pe):
                def scores(it):
                    h, kt = divmod(it, TT)
                    rows = slice(64 * (h % 2), 64 * (h % 2) + 64)
                    if it >= 4:
                        pe.wait_ge(ret_decayed.sem, it - 3)
                    nc.tensor.matmul(psum[:, it % 4, :], proj[rows, RK + h // 2, kt * P:(kt + 1) * P], proj[rows, RQ + h // 2, :],
                                     start=True, stop=True).then_inc(ret_scored.sem, 1)
                scores(0)
                scores(1)
                for it in range(steps):
                    h, kt = divmod(it, TT)
                    if it + 2 < steps:
                        scores(it + 2)
                    pe.wait_ge(ret_decayed.sem, it + 1)
                    if kt == 0 and h >= 2:
                        pe.wait_ge(ret_read.sem, h - 1)
                    nc.tensor.matmul(psum[:, 4 + h % 2, :], v_tok[:, HEADS + h, kt * P:(kt + 1) * P], weighed[:, it % 4, :],
                                     start=kt == 0, stop=kt == TT - 1).then_inc(ret_mixed.sem, 1)

            @block.scalar
            def _(act):
                for h in range(HEADS):
                    act.wait_ge(arg_ready.sem, h + 1)
                    if h >= 2:
                        act.wait_ge(ret_decayed.sem, TT * (h - 1))
                    nc.scalar.activation(decay[:, h % 2, :], args[:, h % 2, :], ACT.Exp).then_inc(decay_ready.sem, 1)
                    if h >= 1:
                        act.wait_ge(ret_mixed.sem, TT * h)
                        nc.scalar.activation(heads_out[:, h - 1, :], psum[:, 4 + (h - 1) % 2, :], ACT.Copy).then_inc(ret_read.sem, 1)
                act.wait_ge(ret_mixed.sem, TT * HEADS)
                nc.scalar.activation(heads_out[:, HEADS - 1, :], psum[:, 4 + (HEADS - 1) % 2, :], ACT.Copy).then_inc(ret_read.sem, 1)
                for h in range(HEADS):
                    nc.scalar.activation(proj[:, RG + h, :], proj[:, RG + h, :], ACT.Silu)

            @block.vector
            def _(dve):
                dve.wait_ge(dist_loaded.sem, 16)

                def log_decay(h):
                    if h >= 2:
                        dve.wait_ge(decay_ready.sem, h - 1)
                    nc.vector.tensor_scalar(args[:, h % 2, :], dist[:, 0, :], lgf[:, h:h + 1], None, ALU.mult).then_inc(arg0_ready.sem, 1)
                    dve.wait_ge(arg0_ready.sem, h + 1)
                    nc.vector.scalar_tensor_tensor(args[:, h % 2, :], dist[:, 1, :], lgf[:, HEADS + h:HEADS + h + 1], args[:, h % 2, :],
                                                   ALU.mult, ALU.add).then_inc(arg_ready.sem, 1)
                log_decay(0)
                for it in range(steps):
                    h, kt = divmod(it, TT)
                    if kt == 0 and h + 1 < HEADS:
                        log_decay(h + 1)
                    dve.wait_ge(ret_scored.sem, it + 1)
                    dve.wait_ge(decay_ready.sem, h + 1)
                    if it >= 4:
                        dve.wait_ge(ret_mixed.sem, it - 3)
                    first = (TT - 1 - kt) * P
                    nc.vector.scalar_tensor_tensor(weighed[:, it % 4, :], psum[:, it % 4, :], RET_QK ** -0.5, decay[:, h % 2, first:first + T],
                                                   ALU.mult, ALU.mult).then_inc(ret_decayed.sem, 1)

        head_norm(heads_out, average128[:], eps_ap[:, 0:1], center=True)
        with nc.Block() as block:
            @block.vector
            def _(dve):
                for h in range(HEADS):
                    nc.vector.tensor_tensor(heads_out[:, h, :], heads_out[:, h, :], proj[:, RG + h, :], ALU.mult)
        split([(heads_out[:, h, :], gain_r[:, h:h + 1]) for h in range(HEADS)], mix_hi, mix_lo, HEADS)

        linear(C, (mix_hi, mix_lo),
               lambda loop, k, bank: nc.vector.tensor_tensor(x[:, at(loop, k), :], x[:, at(loop, k), :], bank, ALU.add), "vector")
        mix_stack.close()
        if stop == 1:
            return

        peer_stack = ExitStack()
        ctx.enter_context(peer_stack)
        act_hi = sb("act_hi", [P, C, T], F32R, peer_stack)
        act_lo = sb("act_lo", [P, C, T], F32R, peer_stack)
        picks_t = sb("picks_t", [P, 3, T], F32, peer_stack)
        iota = sb("iota", [P, P], F32, peer_stack)
        peer_local = ExitStack()
        queries = sb("queries", [P, LISTS, T], F32, peer_local)
        keys = sb("keys", [P, LISTS, P], F32, peer_local)
        keys_loaded = sig("keys_loaded")

        def load_keys(sp):
            sp.dma_start(keys[:, :, :], keys_t).then_inc(keys_loaded.sem, 16)
            sp.dma_start(iota[:, :], iota_in).then_inc(keys_loaded.sem, 16)
        load_keys.loads = 0
        linear(LISTS, (act_hi, act_lo), scaled(lambda n: queries[:, n, :]), "vector", norm=(x, 1), before=load_keys)

        up_copied = sig("up_product_copied")
        ups_stored = [sig(f"up_product_stored{k}") for k in range(2)]
        ups_dram = nc.dram_tensor("ups_dram", [GROUPS_AHEAD * C, P, T], F32).ap()

        class Ups:
            done = 0

            def __init__(self, count, bank, local):
                self.first, self.bank = Ups.done, bank
                Ups.done += count
                self.buffer = sb("up_products", [P, 2, T], F32, local)

            def number(self, loop, k, per):
                return self.first + k if loop is None else loop * per + (self.first + k)

            def free_bank(self, pe, loop, k, per):
                pe.wait_ge(up_copied.sem, self.number(loop, k, per) + 1)

            def product(self, pe, k):
                self.free_bank(pe, None, k, None)
                weights.multiply(pe, None, k, None, psum[:, self.bank + k % 2, :], (act_hi, act_lo)).then_inc(weights.unit_done.sem, 1)

            def copy(self, act, loop, k, per):
                turn = (self.first + k) // 2
                act.wait_ge(weights.unit_done.sem, weights.done(k) if loop is None else loop * per + weights.done(k))
                act.wait_ge(ups_stored[k % 2].sem, 16 * (turn + 1) if loop is None else loop * (16 * per // 2) + 16 * (turn + 1))
                nc.scalar.activation(self.buffer[:, k % 2, :], psum[:, self.bank + k % 2, :], ACT.Copy).then_inc(up_copied.sem, 1)

            def store(self, sp, loop, k, per):
                n = self.number(loop, k, per)
                sp.wait_ge(up_copied.sem, n + 3)
                sp.dma_start(ups_dram[n], self.buffer[:, k % 2, :]).then_inc(ups_stored[k % 2].sem, 16)

            def all_stored(self, sp):
                for k in range(2):
                    sp.wait_ge(ups_stored[k].sem, 16 * (Ups.done // 2 + 1))

        list_scored, list_copied = sig("peer_scores_ready"), sig("peer_scores_copied")
        top, choose, second, first_j = sig("top_step"), sig("choice_step"), sig("second_key_step"), sig("second_key_input")
        gate_inv = sig("gate_inverse_ready")
        gate_exp, picks_turned, picks_copied = sig("gate_exp_ready"), sig("picks_transposed"), sig("picks_copied")
        TOP_STEPS = 5 * LISTS + 5 * PEER_HEADS + 1
        CHOOSE_STEPS = 11
        UP_EXP = UP_TILE - 3
        with peer_local, nc.Block() as block:
            local = peer_local
            ups = Ups(TT * UP_TILE, 5, local)
            scores_sb = sb("peer_scores", [P, 2, LISTS, P], F32, local)
            rest_sb = sb("peer_scores_rest", [P, LISTS, P], F32, local)
            top_s = sb("top_scores", [P, LISTS, TOPK], F32, local)
            top_i = sb("top_keys", [P, LISTS, TOPK], U32, local)
            top_f = sb("top_keys_f32", [P, LISTS, TOPK], F32, local)
            cand = sb("candidates", [P, PEER_HEADS, TOPK * TOPK], F32, local)
            cand_rest = rest_sb[:, :, :].rearrange("p (h l) n -> p h (l n)", h=PEER_HEADS)
            best = sb("best_scores", [P, PEER_HEADS, TOPK], F32, local)
            place = sb("best_places", [P, PICKS], U32, local)
            place_a = sb("best_first", [P, PICKS], U32, local)
            place_b = sb("best_second", [P, PICKS], U32, local)
            places = sb("best_places_f32", [P, 2, PICKS], F32, local)
            hot = sb("place_one_hot", [P, 2, PICKS, TOPK], F32, local)
            picks = sb("picks", [P, 3, PICKS], F32, local)
            gate_sum = sb("gate_sum", [P, 2, PEER_HEADS], F32, local)

            @block.sync
            def _(sp):
                dram, index = weights.source(weights.u0)
                for k in range(TT * UP_TILE):
                    weights.load(sp, k + RING, (weights.u0 + k) % RING, dram, index + k + RING)
                    ups.store(sp, None, k, None)
                ups.all_stored(sp)

            @block.tensor
            def _(pe):
                pe.sem_inc(up_copied.sem, 2)
                pe.wait_ge(keys_loaded.sem, 32)

                def lists(tile):
                    if tile:
                        pe.wait_ge(list_copied.sem, tile)
                    for l in range(LISTS):
                        mm = nc.tensor.matmul(psum[:, l // 4, (l % 4) * P:(l % 4 + 1) * P], queries[:, l, tile * P:(tile + 1) * P],
                                              keys[:, l, :], start=True, stop=True)
                    mm.then_inc(list_scored.sem, 1)
                lists(0)
                for tile in range(TT):
                    if tile + 1 < TT:
                        lists(tile + 1)
                    for k in range(UP_TILE):
                        ups.product(pe, tile * UP_TILE + k)
                    pe.wait_ge(choose.sem, CHOOSE_STEPS * (tile + 1))
                    if tile:
                        pe.wait_ge(picks_copied.sem, tile)
                    for r in range(3):
                        mm = nc.tensor.transpose(psum[:, 4, r * P:(r + 1) * P], picks[:, r, :], ident[:])
                    mm.then_inc(picks_turned.sem, 1)

            @block.scalar
            def _(act):
                def copy_scores(tile):
                    act.wait_ge(list_scored.sem, tile + 1)
                    if tile >= 2:
                        act.wait_ge(top.sem, TOP_STEPS * (tile - 2) + 4 * LISTS)
                    nc.scalar.activation(scores_sb[:, tile % 2, :, :], psum[:, 0:4, :].rearrange("p b (l n) -> p (b l) n", n=P),
                                         ACT.Copy).then_inc(list_copied.sem, 1)
                def up_steps(units):
                    for k in units:
                        weights.hi_step(act, None, k + weights.AHEAD, None)
                        ups.copy(act, None, k, None)
                act.sem_inc(ups_stored[0].sem, 16)
                act.sem_inc(ups_stored[1].sem, 16)
                copy_scores(0)
                for tile in range(TT):
                    if tile + 1 < TT:
                        copy_scores(tile + 1)
                    up_steps(range(tile * UP_TILE, tile * UP_TILE + UP_EXP))
                    act.wait_ge(choose.sem, CHOOSE_STEPS * tile + 1)
                    nc.scalar.activation(picks[:, 2, :], picks[:, 2, :], ACT.Exp).then_inc(gate_exp.sem, 1)
                    up_steps(range(tile * UP_TILE + UP_EXP, (tile + 1) * UP_TILE))
                    act.wait_ge(picks_turned.sem, tile + 1)
                    nc.scalar.activation(picks_t[:, :, tile * P:(tile + 1) * P], psum[:, 4, 0:3 * P].rearrange("p (r t) -> p r t", r=3),
                                         ACT.Copy).then_inc(picks_copied.sem, 1)

            def by_keys(eng, side):
                hot_h = hot[:, side, :, :].rearrange("p (h k) a -> p h k a", h=PEER_HEADS)
                keys_h = top_f[:, side::2, :].unsqueeze(2).to_broadcast([P, PEER_HEADS, TOPK, TOPK])
                return eng.tensor_tensor(hot_h, hot_h, keys_h, ALU.mult)

            @block.gpsimd
            def _(pool):
                for tile in range(TT):
                    for k in range(tile * UP_TILE, (tile + 1) * UP_TILE):
                        if k == tile * UP_TILE + UP_EXP:
                            pool.wait_ge(first_j.sem, tile + 1)
                            by_keys(nc.gpsimd, 1).then_inc(second.sem, 1)
                        weights.lo_step(pool, None, k + weights.AHEAD, None)

            @block.vector
            def _(dve):
                dve.wait_ge(keys_loaded.sem, 32)
                for tile in range(TT):
                    n0 = TOP_STEPS * tile
                    dve.wait_ge(list_copied.sem, tile + 1)
                    s = scores_sb[:, tile % 2, :, :]
                    for l in range(LISTS):
                        nc.vector.max(top_s[:, l, 0:8], s[:, l, :]).then_inc(top.sem, 1)
                    for l in range(LISTS):
                        dve.wait_ge(top.sem, n0 + l + 1)
                        nc.vector.match_replace(rest_sb[:, l, :], top_s[:, l, 0:8], s[:, l, :], LOWEST).then_inc(top.sem, 1)
                    for l in range(LISTS):
                        nc.vector.max_index(top_i[:, l, 0:8], top_s[:, l, 0:8], s[:, l, :]).then_inc(top.sem, 1)
                    for l in range(LISTS):
                        dve.wait_ge(top.sem, n0 + LISTS + l + 1)
                        nc.vector.max(top_s[:, l, 8:16], rest_sb[:, l, :]).then_inc(top.sem, 1)
                    for l in range(LISTS):
                        dve.wait_ge(top.sem, n0 + 3 * LISTS + l + 1)
                        nc.vector.max_index(top_i[:, l, 8:16], top_s[:, l, 8:16], rest_sb[:, l, :]).then_inc(top.sem, 1)
                    n1 = n0 + 5 * LISTS
                    pairs = cand[:, :, :].rearrange("p h (a b) -> p h a b", a=TOPK)
                    nc.vector.tensor_tensor(pairs, top_s[:, 0::2, :].unsqueeze(3).to_broadcast([P, PEER_HEADS, TOPK, TOPK]),
                                            top_s[:, 1::2, :].unsqueeze(2).to_broadcast([P, PEER_HEADS, TOPK, TOPK]), ALU.add).then_inc(top.sem, 1)
                    dve.wait_ge(top.sem, n1 + 1)
                    for h in range(PEER_HEADS):
                        nc.vector.max(best[:, h, 0:8], cand[:, h, :]).then_inc(top.sem, 1)
                    for h in range(PEER_HEADS):
                        dve.wait_ge(top.sem, n1 + 1 + h + 1)
                        nc.vector.match_replace(cand_rest[:, h, :], best[:, h, 0:8], cand[:, h, :], LOWEST).then_inc(top.sem, 1)
                    for h in range(PEER_HEADS):
                        nc.vector.max_index(place[:, h * TOPK:h * TOPK + 8], best[:, h, 0:8], cand[:, h, :]).then_inc(top.sem, 1)
                    for h in range(PEER_HEADS):
                        dve.wait_ge(top.sem, n1 + 1 + PEER_HEADS + h + 1)
                        nc.vector.max(best[:, h, 8:16], cand_rest[:, h, :]).then_inc(top.sem, 1)
                    for h in range(PEER_HEADS):
                        dve.wait_ge(top.sem, n1 + 1 + 3 * PEER_HEADS + h + 1)
                        nc.vector.max_index(place[:, h * TOPK + 8:(h + 1) * TOPK], best[:, h, 8:16], cand_rest[:, h, :]).then_inc(top.sem, 1)
                    m0 = CHOOSE_STEPS * tile
                    gates = picks[:, 2, :].rearrange("p (h k) -> p h k", h=PEER_HEADS)
                    if tile:
                        dve.wait_ge(picks_turned.sem, tile)
                    nc.vector.tensor_tensor(gates, best[:, :, :], best[:, :, 0:1].to_broadcast([P, PEER_HEADS, TOPK]), ALU.subtract).then_inc(choose.sem, 1)
                    dve.wait_ge(top.sem, n0 + TOP_STEPS)
                    nc.vector.tensor_scalar(place_a[:], place[:], 4, None, ALU.logical_shift_right).then_inc(choose.sem, 1)
                    nc.vector.tensor_scalar(place_b[:], place[:], TOPK - 1, None, ALU.bitwise_and).then_inc(choose.sem, 1)
                    nc.vector.tensor_copy(top_f[:, :, :], top_i[:, :, :])
                    dve.wait_ge(choose.sem, m0 + 3)
                    nc.vector.tensor_copy(places[:, 0, :], place_a[:]).then_inc(choose.sem, 1)
                    nc.vector.tensor_copy(places[:, 1, :], place_b[:]).then_inc(choose.sem, 1)
                    dve.wait_ge(choose.sem, m0 + 5)
                    for side, one_hots in ((1, first_j), (0, choose)):
                        nc.vector.tensor_tensor(hot[:, side, :, :], iota[:, 0:TOPK].unsqueeze(1).to_broadcast([P, PICKS, TOPK]),
                                                places[:, side, :].unsqueeze(2).to_broadcast([P, PICKS, TOPK]), ALU.is_equal).then_inc(one_hots.sem, 1)
                    dve.wait_ge(choose.sem, m0 + 6)
                    by_keys(nc.vector, 0).then_inc(choose.sem, 1)
                    dve.wait_ge(choose.sem, m0 + 7)
                    nc.vector.tensor_reduce(picks[:, 0, :], hot[:, 0, :, :], AX.X, ALU.add).then_inc(choose.sem, 1)
                    dve.wait_ge(second.sem, tile + 1)
                    nc.vector.tensor_reduce(picks[:, 1, :], hot[:, 1, :, :], AX.X, ALU.add).then_inc(choose.sem, 1)
                    dve.wait_ge(gate_exp.sem, tile + 1)
                    nc.vector.tensor_reduce(gate_sum[:, 0, :], gates, AX.X, ALU.add).then_inc(choose.sem, 1)
                    dve.wait_ge(choose.sem, m0 + 10)
                    nc.vector.reciprocal(gate_sum[:, 1, :], gate_sum[:, 0, :]).then_inc(gate_inv.sem, 1)
                    dve.wait_ge(gate_inv.sem, tile + 1)
                    nc.vector.tensor_tensor(gates, gates, gate_sum[:, 1, :].unsqueeze(2).to_broadcast([P, PEER_HEADS, TOPK]), ALU.mult).then_inc(choose.sem, 1)
        weights.u0 += TT * UP_TILE
        if stop == 2:
            return

        hot1_ready, hot2_ready, dense_ready, dense_copied = (sig(n) for n in ("first_one_hots_ready", "gated_one_hots_ready", "dense_gates_ready", "dense_gates_copied"))
        hot2_raw, hot2_gated = sig("odd_second_one_hots_ready"), sig("odd_second_one_hots_gated")
        gates_stored = [sig(f"gates_stored{k}") for k in range(2)]
        ups_loaded = sig("up_group_loaded")
        group = sb("up_group", [P, C, T], F32, peer_stack)
        QUAD = 4
        HOTS = 4
        GSTEPS = GT // QUAD
        LOOP_TOKENS = 2 * GT
        LOOP_STEPS = LOOP_TOKENS // QUAD
        LOOP_UNITS = UP_DENSE * LOOP_TOKENS // T

        def load_ups(sp, g):
            sp.dma_start(group[:, :, :], ups_dram[bass.ds(g * C, C)].rearrange("c p t -> p c t")).then_inc(ups_loaded.sem, 16)
        with ExitStack() as local, nc.Block() as block:
            hot1 = [sb("hot1", [P, QUAD, P], F32, local) for _ in range(HOTS)]
            hot2 = [sb("hot2", [P, QUAD, P], F32, local) for _ in range(HOTS)]
            stage = sb("gates_stage", [P, 2, N_KEYS, GT], F32, local)
            ups = Ups(UP_DENSE + UP_TAIL, 5, local)
            tail = range(UP_DENSE, UP_DENSE + UP_TAIL)

            @block.vector
            def _(dve):
                def one_hots(hot, r, i, k):
                    return nc.vector.tensor_tensor(hot[:, :, :], iota[:, :].unsqueeze(1).to_broadcast([P, QUAD, P]),
                                                   picks_t[:, r, bass.ds(i * (HOTS * QUAD) + k * QUAD, QUAD)].unsqueeze(2).to_broadcast([P, QUAD, P]),
                                                   ALU.is_equal)
                with dve.Fori(0, T // QUAD // HOTS) as i:
                    for k in range(HOTS):
                        dve.wait_ge(dense_ready.sem, i * HOTS + (k + 1))
                        one_hots(hot1[k], 0, i, k).then_inc(hot1_ready.sem, 1)
                        if k % 2:
                            one_hots(hot2[k], 1, i, k).then_inc(hot2_raw.sem, 1)
                            continue
                        for t in range(QUAD):
                            token = i * (HOTS * QUAD) + (k * QUAD + t)
                            ins = nc.vector.tensor_scalar(hot2[k][:, t, :], iota[:, :], picks_t[:, 1, bass.ds(token, 1)], picks_t[:, 2, bass.ds(token, 1)],
                                                          ALU.is_equal, ALU.mult)
                        ins.then_inc(hot2_ready.sem, 1)

            @block.gpsimd
            def _(pool):
                with pool.Fori(0, T // LOOP_TOKENS) as i:
                    for u in range(LOOP_UNITS):
                        for n in range(u * C // 2, (u + 1) * C // 2):
                            if n == u * C // 2 + 1:
                                weights.lo_step(pool, i, u + weights.AHEAD, LOOP_UNITS)
                            pool.wait_ge(hot2_raw.sem, i * (LOOP_STEPS // 2) + (n + 1))
                            hot = hot2[(2 * n + 1) % HOTS]
                            nc.gpsimd.tensor_tensor(hot[:, :, :], hot[:, :, :],
                                                    picks_t[:, 2, bass.ds(i * LOOP_TOKENS + (2 * n + 1) * QUAD, QUAD)].unsqueeze(2).to_broadcast([P, QUAD, P]),
                                                    ALU.mult).then_inc(hot2_gated.sem, 1)
                for k in tail:
                    weights.lo_step(pool, None, k + weights.AHEAD, None)

            @block.tensor
            def _(pe):
                pe.sem_inc(dense_copied.sem, 2)
                pe.sem_inc(dense_ready.sem, HOTS)
                with pe.Fori(0, T // LOOP_TOKENS) as i:
                    for u in range(LOOP_UNITS):
                        ups.free_bank(pe, i, u, LOOP_UNITS)
                        for c in range(C):
                            n, k = u * C + c, c % 2
                            pe.wait_ge(hot1_ready.sem, i * LOOP_STEPS + (n + 1))
                            gated_hots = hot2_gated if k else hot2_ready
                            pe.wait_ge(gated_hots.sem, i * (LOOP_STEPS // 2) + (n // 2 + 1))
                            pe.wait_ge(dense_copied.sem, i * LOOP_STEPS + (n + 1))
                            for t in range(QUAD):
                                mm = nc.tensor.matmul(psum[:, k, t * P:(t + 1) * P], hot1[c % HOTS][:, t, :], hot2[c % HOTS][:, t, :], start=True, stop=True)
                            mm.then_inc(dense_ready.sem, 1)
                            mm = weights.multiply_chunk(pe, i, u, LOOP_UNITS, psum[:, ups.bank + u % 2, :], (act_hi, act_lo), c)
                        mm.then_inc(weights.unit_done.sem, 1)
                for k in tail:
                    ups.product(pe, k)

            @block.scalar
            def _(act):
                act.sem_inc(gates_stored[0].sem, 16)
                act.sem_inc(gates_stored[1].sem, 16)
                with act.Fori(0, T // LOOP_TOKENS) as i:
                    for u in range(LOOP_UNITS):
                        half = u * C // GSTEPS
                        if u * C % GSTEPS == 0:
                            act.wait_ge(gates_stored[half].sem, i * 16 + 16)
                        weights.hi_step(act, i, u + weights.AHEAD, LOOP_UNITS)
                        for c in range(C):
                            n = u * C + c
                            act.wait_ge(dense_ready.sem, i * LOOP_STEPS + (n + HOTS + 1))
                            nc.scalar.activation(stage[:, half, :, n % GSTEPS * QUAD:(n % GSTEPS + 1) * QUAD],
                                                 psum[:, c % 2, :].rearrange("p (t j) -> p j t", t=QUAD), ACT.Copy).then_inc(dense_copied.sem, 1)
                        ups.copy(act, i, u, LOOP_UNITS)
                for k in tail:
                    weights.hi_step(act, None, k + weights.AHEAD, None)
                    ups.copy(act, None, k, None)

            @block.sync
            def _(sp):
                load_ups(sp, 0)
                dram, index = weights.source(weights.u0)
                with sp.Fori(0, T // LOOP_TOKENS) as i:
                    for u in range(LOOP_UNITS):
                        weights.load(sp, i * LOOP_UNITS + (u + RING), (weights.u0 + u) % RING, dram, i * LOOP_UNITS + (index + u + RING))
                        ups.store(sp, i, u, LOOP_UNITS)
                        if (u + 1) * C % GSTEPS == 0:
                            half = u * C // GSTEPS
                            sp.wait_ge(dense_copied.sem, i * LOOP_STEPS + ((u + 1) * C + 2))
                            sp.dma_start(gates_dram[i * 2 + half], stage[:, half, :, :].rearrange("p j t -> p (j t)")).then_inc(gates_stored[half].sem, 16)
                for k in tail:
                    weights.load(sp, k + RING, (weights.u0 + k) % RING, dram, index + k + RING)
                    ups.store(sp, None, k, None)
                for half in range(2):
                    sp.wait_ge(gates_stored[half].sem, 16 * (GBLOCKS // 2 + 1))
                ups.all_stored(sp)
        weights.u0 += UP_DENSE + UP_TAIL

        activated = sig("ffn_activated")
        read = sig("ffn_up_scaled")
        gated, ffn_hi, ffn_lo = sig("ffn_gated"), sig("ffn_hi_ready"), sig("ffn_lo_ready")
        gates_loaded = sig("gates_loaded")
        started = [False]

        def gates_of(g):
            return gates_dram[:, :, bass.ds(g * (C * GT), C * GT)].rearrange("b i n -> i b n")

        def feed_forward(groups, acts, function, gates, h_hi, h_lo, raw_act, raw_gated, gate_tile=None, first_group=0):
            w = weights
            u0, base, per = w.u0, out_free.base, 2 * C
            a0, g0, h0, r0 = activated.base, gated.base, ffn_lo.base, read.base
            first = not started[0]
            started[0] = True
            with nc.Block() as block:
                @block.sync
                def _(sp):
                    if gates:
                        sp.dma_start(gate_tile[:, :, :], gates_of(first_group)).then_inc(gates_loaded.sem, 16)
                    dram, index = w.source(u0)
                    with sp.Fori(0, groups - 1) as i:
                        for k in range(per):
                            w.load(sp, i * per + (k + RING), (u0 + k) % RING, dram, i * per + (index + k + RING))
                            if gates and k == per - RING - 1:
                                sp.wait_ge(gated.sem, i * C + (g0 + C))
                                sp.dma_start(gate_tile[:, :, :], gates_of(i + (first_group + 1))).then_inc(gates_loaded.sem, 16)
                    for k in range(per):
                        v = u0 + (groups - 1) * per + k + RING
                        if v < w.total:
                            dram, index = w.source(v)
                            w.load(sp, (groups - 1) * per + k + RING, v % RING, dram, index)

                @block.tensor
                def _(pe):
                    if first:
                        pe.sem_inc(read.sem, RING)
                    with pe.Fori(0, groups) as i:
                        for k in range(C):
                            pe.wait_ge(read.sem, i * C + (r0 + k + 1))
                            w.multiply(pe, i, k, per, psum[:, k % RING, :], acts).then_inc(w.unit_done.sem, 1)
                        for d in range(C):
                            pe.wait_ge(out_free.sem, i * C + (base + d + 1))
                            bank = psum[:, 4 + d % RING, :]
                            for c in range(C):
                                if d == 0:
                                    pe.wait_ge(ffn_lo.sem, i * C + (h0 + c + 1))
                                mm = w.multiply_chunk(pe, i, C + d, per, bank, (h_hi, h_lo), c)
                            mm.then_inc(w.unit_done.sem, 1)

                @block.scalar
                def _(act):
                    def body(i, last):
                        for k in range(per):
                            if not (last and w.u0 + (groups - 1) * per + k + w.AHEAD >= w.total):
                                w.hi_step(act, i, k + w.AHEAD, per)
                            if k < C:
                                act.wait_ge(read.sem, i * C + (r0 + RING + k + 1))
                                nc.scalar.activation(raw_act[:, k % 2, :], raw_act[:, k % 2, :], function).then_inc(activated.sem, 1)
                                act.wait_ge(gated.sem, i * C + (g0 + k + 1))
                                nc.scalar.activation(h_hi[:, k, :], raw_gated[:, k % 2, :], ACT.Copy).then_inc(ffn_hi.sem, 1)
                    with act.Fori(0, groups - 1) as i:
                        body(i, False)
                    body(groups - 1, True)

                @block.vector
                def _(dve):
                    def body(i, last):
                        for k in range(per):
                            def lo_ahead():
                                if not (last and w.u0 + (groups - 1) * per + k + w.AHEAD >= w.total):
                                    w.lo_step(dve, i, k + w.AHEAD, per)
                            if k < C:
                                dve.wait_ge(w.unit_done.sem, i * per + w.done(k))
                                nc.vector.tensor_tensor(raw_act[:, k % 2, :], psum[:, k % RING, :], rstd[:], ALU.mult).then_inc(read.sem, 1)
                            if k != C - 1:
                                lo_ahead()
                            if k < C:
                                dve.wait_ge(activated.sem, i * C + (a0 + k + 1))
                                if gates and k == 0:
                                    dve.wait_ge(gates_loaded.sem, i * 16 + (gates_loaded.base + 16))
                                other = gate_tile[:, :, k * GT:(k + 1) * GT] if gates else raw_act[:, k % 2, :]
                                one = raw_act[:, k % 2, :]
                                out = raw_gated[:, k % 2, :]
                                if gates:
                                    one, out = (a.rearrange("p (b t) -> p b t", t=GT) for a in (one, out))
                                nc.vector.tensor_tensor(out, one, other, ALU.mult).then_inc(gated.sem, 1)
                                dve.wait_ge(ffn_hi.sem, i * C + (g0 + k + 1))
                                nc.vector.tensor_tensor(h_lo[:, k, :], raw_gated[:, k % 2, :], h_hi[:, k, :].bitcast(F32),
                                                        ALU.subtract).then_inc(ffn_lo.sem, 1)
                                if k == C - 1:
                                    lo_ahead()
                            else:
                                d = k - C
                                dve.wait_ge(w.unit_done.sem, i * per + w.done(k))
                                nc.vector.tensor_tensor(x[:, d, :], x[:, d, :], psum[:, 4 + d % RING, :], ALU.add).then_inc(out_free.sem, 1)
                    with dve.Fori(0, groups - 1) as i:
                        body(i, False)
                    body(groups - 1, True)
            w.u0 += groups * per
            for s in (activated, read, gated, ffn_hi, ffn_lo, out_free):
                s.base += groups * C

        ups_scaled, ups_gelu = sig("up_group_scaled"), sig("up_group_activated")
        inner_free = sig("inner_chunk_free")

        def stored_groups(local):
            w = weights
            ups = Ups(UP_FIRST, 0, local)
            base, first = out_free.base, UP_FIRST
            last_group = range(first + (GROUPS_AHEAD - 1) * C, first + GROUPS_AHEAD * C)
            with nc.Block() as block:
                def load_gates(sp, g):
                    sp.dma_start(gate_tile[:, :, :], gates_of(g)).then_inc(gates_loaded.sem, 16)

                @block.sync
                def _(sp):
                    load_gates(sp, 0)
                    dram, index = w.source(w.u0)
                    for k in range(first):
                        w.load(sp, k + RING, (w.u0 + k) % RING, dram, index + k + RING)
                        ups.store(sp, None, k, None)
                    ups.all_stored(sp)
                    with sp.Fori(0, GROUPS_AHEAD - 1) as i:
                        for k in range(first, first + C):
                            w.load(sp, i * C + (k + RING), (w.u0 + k) % RING, dram, i * C + (index + k + RING))
                            if k == first:
                                sp.wait_ge(gated.sem, i * C + C)
                                load_ups(sp, i + 1)
                                load_gates(sp, i + 1)
                    for k in last_group:
                        w.load(sp, k + RING, (w.u0 + k) % RING, dram, index + k + RING)

                @block.tensor
                def _(pe):
                    for k in range(first):
                        ups.product(pe, k)
                    with pe.Fori(0, GROUPS_AHEAD) as i:
                        for d in range(C):
                            pe.wait_ge(out_free.sem, i * C + (base + d + 1))
                            for c in range(C):
                                if d == 0:
                                    pe.wait_ge(ffn_lo.sem, i * C + (c + 1))
                                mm = w.multiply_chunk(pe, i, first + d, C, psum[:, 4 + d % RING, :], (inner_hi, inner_lo), c)
                                if d == C - 1 and c < C - 1:
                                    mm.then_inc(inner_free.sem, 1)
                            mm.then_inc(w.unit_done.sem, 1)

                def next_group(i):
                    return 0 if i is None else i * C + C

                @block.gpsimd
                def _(pool):
                    def scale(i):
                        pool.wait_ge(ups_loaded.sem, 16 if i is None else i * 16 + 32)
                        for c in range(C):
                            nc.gpsimd.tensor_tensor(group[:, c, :], group[:, c, :], rstd[:], ALU.mult).then_inc(ups_scaled.sem, 1)
                    scale(None)
                    with pool.Fori(0, GROUPS_AHEAD - 1) as i:
                        scale(i)

                @block.scalar
                def _(act):
                    def gelu(i, c):
                        act.wait_ge(ups_scaled.sem, next_group(i) + (c + 1))
                        nc.scalar.activation(group[:, c, :], group[:, c, :], ACT.Gelu).then_inc(ups_gelu.sem, 1)

                    def inner(i, c):
                        act.wait_ge(gated.sem, next_group(i) + (c + 1))
                        if i is not None and c < C - 1:
                            act.wait_ge(inner_free.sem, i * (C - 1) + (c + 1))
                        elif i is not None:
                            act.wait_ge(w.unit_done.sem, i * C + w.done(first + C - 1))
                        nc.scalar.activation(inner_hi[:, c, :], raw_gated[:, c % 2, :], ACT.Copy).then_inc(ffn_hi.sem, 1)
                    for k in range(first):
                        w.hi_step(act, None, k + w.AHEAD, None)
                        if k == first - 2:
                            for c in range(C):
                                gelu(None, c)
                        if k == first - 1:
                            for c in range(C):
                                inner(None, c)
                        ups.copy(act, None, k, None)
                    with act.Fori(0, GROUPS_AHEAD - 1) as i:
                        for d in range(C):
                            w.hi_step(act, i, first + d + w.AHEAD, C)
                            if d in (3, 4, 5, 6):
                                gelu(i, 2 * d - 6)
                                gelu(i, 2 * d - 5)
                        for c in range(C):
                            inner(i, c)
                    for k in last_group:
                        w.hi_step(act, None, k + w.AHEAD, None)

                @block.vector
                def _(dve):
                    def inner(i, c):
                        if c == 0:
                            dve.wait_ge(gates_loaded.sem, 16 if i is None else i * 16 + 32)
                        dve.wait_ge(ups_gelu.sem, next_group(i) + (c + 1))
                        if c >= 2:
                            dve.wait_ge(ffn_lo.sem, next_group(i) + (c - 1))
                        nc.vector.tensor_tensor(raw_gated[:, c % 2, :].rearrange("p (b t) -> p b t", t=GT),
                                                group[:, c, :].rearrange("p (b t) -> p b t", t=GT),
                                                gate_tile[:, :, c * GT:(c + 1) * GT], ALU.mult).then_inc(gated.sem, 1)

                    def inner_lo_step(i, c):
                        dve.wait_ge(ffn_hi.sem, next_group(i) + (c + 1))
                        nc.vector.tensor_tensor(inner_lo[:, c, :], raw_gated[:, c % 2, :], inner_hi[:, c, :].bitcast(F32),
                                                ALU.subtract).then_inc(ffn_lo.sem, 1)

                    def add(i, d):
                        dve.wait_ge(w.unit_done.sem, w.done(last_group[d]) if i is None else i * C + w.done(first + d))
                        nc.vector.tensor_tensor(x[:, d, :], x[:, d, :], psum[:, 4 + d % RING, :], ALU.add).then_inc(out_free.sem, 1)

                    def inner_chunks(i):
                        inner(i, 0)
                        for c in range(C):
                            if c + 1 < C:
                                inner(i, c + 1)
                            inner_lo_step(i, c)
                    for k in range(first):
                        w.lo_step(dve, None, k + w.AHEAD, None)
                    inner_chunks(None)
                    with dve.Fori(0, GROUPS_AHEAD - 1) as i:
                        for d in range(C - 1):
                            w.lo_step(dve, i, first + d + w.AHEAD, C)
                            add(i, d)
                        inner_chunks(i)
                        w.lo_step(dve, i, first + C - 1 + w.AHEAD, C)
                        add(i, C - 1)
                    for d in range(C):
                        w.lo_step(dve, None, last_group[d] + w.AHEAD, None)
                        add(None, d)
            w.u0 += first + GROUPS_AHEAD * C
            for s in (gated, ffn_hi, ffn_lo, out_free):
                s.base += GROUPS_AHEAD * C
            gates_loaded.base += 16 * GROUPS_AHEAD

        with ExitStack() as local:
            inner_hi = sb("inner_hi", [P, C, T], F32R, local)
            inner_lo = sb("inner_lo", [P, C, T], F32R, local)
            raw_act = sb("inner_activated", [P, 2, T], F32, local)
            raw_gated = sb("inner_gated", [P, 2, T], F32, local)
            gate_tile = sb("gates_of_group", [P, GBLOCKS, C * GT], F32, local)
            with ExitStack() as ahead:
                stored_groups(ahead)
            feed_forward(EXPERT_GROUPS - GROUPS_AHEAD, (act_hi, act_lo), ACT.Gelu, True, inner_hi, inner_lo, raw_act, raw_gated,
                         gate_tile, GROUPS_AHEAD)
        peer_stack.close()
        rms_norm(x, 2, out_f32=x)
        if stop == 3:
            return

        y = sb("rwkv_out", [P, 4, T], F32)
        rwkv_stack = ExitStack()
        ctx.enter_context(rwkv_stack)
        rw = sb("rwkv_projections", [P, RWKV_SLABS, T + 1], F32, rwkv_stack)
        vecs = sb("rwkv_vectors_sb", [P, 64], F32, rwkv_stack)
        mu, kkv, kav, rkv, a0v, lnw, lnb = vecs[:, 0:15], vecs[:, 16:20], vecs[:, 20:24], vecs[:, 24:28], vecs[:, 28:32], vecs[:, 32:36], vecs[:, 36:40]
        block_ones = sb("block_ones", [P, P], F32, rwkv_stack)
        block_avg = sb("block_average", [P, P], F32, rwkv_stack)
        lora = sb("rwkv_lora", [P, 3, T], F32, rwkv_stack)
        w0_row = sb("rwkv_w0", [1, T], F32, rwkv_stack)
        ln_eps = sb("rwkv_eps", [P, 1], F32, rwkv_stack)
        mid_decay = sb("mid_decay", [P, 2, 4, TT], F32, rwkv_stack)
        sum_masks = sb("decay_sum_masks", [P, 2, P], F32, rwkv_stack)
        rwkv_loaded = sig("rwkv_loaded")

        def load_rwkv(sp):
            for dst, src in ((vecs[:, 0:40], rwkv["vectors"]), (block_ones[:], rwkv["block_ones"]), (block_avg[:], rwkv["block_average"]),
                             (lora[:, 0, :], rwkv["lora_wa"]), (lora[:, 1, :], rwkv["lora_g"][0:P, :]),
                             (lora[0:32, 2, :], rwkv["lora_g"][P:P + 32, :]), (w0_row[:, :], rwkv["w0"]), (sum_masks[:, :, :], rwkv["sum_masks"])):
                sp.dma_start(dst, src).then_inc(rwkv_loaded.sem, 16)
        load_rwkv.loads = 0
        with ExitStack() as local:
            act_hi = sb("act_hi", [P, C, T], F32R, local)
            act_lo = sb("act_lo", [P, C, T], F32R, local)
            linear(RWKV_SLABS, (act_hi, act_lo), scaled(lambda n: rw[:, n, 1:T + 1]), "vector", norm=(x, 3), before=load_rwkv)

        def R(n):
            return rw[:, n, 1:T + 1]

        R_, K_, V_, WA_, G_ = 0, 4, 8, 12, 13
        kk = sb("rwkv_kk", [P, 4, T], F32, rwkv_stack)
        bb = sb("rwkv_b", [P, 4, T], F32, rwkv_stack)
        bonus = sb("rwkv_bonus", [P, 4, T], F32, rwkv_stack)
        turned_stack = ExitStack()
        rwkv_stack.enter_context(turned_stack)
        decay_in = sb("decay_gate", [P, TT, T], F32, turned_stack)

        shift_diff, shifted = sig("shift_difference_ready"), sig("token_shifted")
        lora_in, decay_product, decay_gate = sig("lora_inputs_ready"), sig("decay_product_ready"), sig("decay_gate_ready")
        a_product, a_ready = sig("a_product_ready"), sig("a_ready")
        with ExitStack() as local, nc.Block() as block:
            diff = sb("shift_difference", [P, 2, T], F32, local)

            order = [WA_, G_, G_ + 1] + list(range(12))

            @block.gpsimd
            def _(pool):
                nc.gpsimd.memset(rw[:, :, 0:1], 0.0).then_inc(shift_diff.sem, 1)
                nc.gpsimd.memset(ln_eps[:], RWKV_LN_EPS)
                pool.wait_ge(shift_diff.sem, 1)
                for j, n in enumerate(order):
                    if j >= 2:
                        pool.wait_ge(shifted.sem, j - 1)
                    nc.gpsimd.tensor_tensor(diff[:, j % 2, :], rw[:, n, 0:T], rw[:, n, 1:T + 1], ALU.subtract).then_inc(shift_diff.sem, 1)

            @block.vector
            def _(dve):
                dve.wait_ge(rwkv_loaded.sem, 8 * 16)
                for j, n in enumerate(order):
                    dve.wait_ge(shift_diff.sem, j + 2)
                    nc.vector.scalar_tensor_tensor(R(n), diff[:, j % 2, :], mu[:, n:n + 1], R(n), ALU.mult, ALU.add).then_inc(shifted.sem, 1)
                for j in range(4):
                    dve.wait_ge(shifted.sem, len(order))
                    nc.vector.tensor_scalar(kk[:, j, :], R(K_ + j), kkv[:, j:j + 1], None, ALU.mult)

            @block.tensor
            def _(pe):
                pe.wait_ge(rwkv_loaded.sem, 8 * 16)
                pe.wait_ge(lora_in.sem, 1)
                for tile in range(TT):
                    tokens = slice(1 + tile * P, 1 + (tile + 1) * P)
                    nc.tensor.matmul(psum[:, tile, :], rw[0:64, WA_, tokens], lora[0:64, 0, :], start=True, stop=False)
                    nc.tensor.matmul(psum[:, tile, :], ones[0:1, :], w0_row[0:1, :], start=False, stop=True).then_inc(decay_product.sem, 1)
                for j in range(4):
                    nc.tensor.matmul(psum[:, 4 + j, :], lora[64:128, 0, j * P:(j + 1) * P], rw[64:128, WA_, 1:T + 1],
                                     start=True, stop=True).then_inc(a_product.sem, 1)

            @block.scalar
            def _(act):
                act.wait_ge(shifted.sem, 3)
                nc.scalar.activation(rw[0:64, WA_, 1:T + 1], rw[0:64, WA_, 1:T + 1], ACT.Tanh).then_inc(lora_in.sem, 1)
                nc.scalar.activation(R(G_), R(G_), ACT.Sigmoid)
                nc.scalar.activation(rw[0:32, G_ + 1, 1:T + 1], rw[0:32, G_ + 1, 1:T + 1], ACT.Sigmoid)
                for tile in range(TT):
                    act.wait_ge(decay_product.sem, tile + 1)
                    nc.scalar.activation(decay_in[:, tile, :], psum[:, tile, :], ACT.Sigmoid)
                act.wait_ge(rwkv_loaded.sem, 8 * 16)
                for j in range(4):
                    act.wait_ge(a_product.sem, j + 1)
                    nc.scalar.activation(bb[:, j, :], psum[:, 4 + j, :], ACT.Sigmoid, bias=a0v[:, j:j + 1])

        head_norm(kk, block_ones[:], 0.0, center=False, floor=1e-24)

        KAPPA = math.exp(-0.5)
        sums_ready, sums_read = sig("decay_sums_ready"), sig("decay_sums_read")
        ops, bonus_sum, k_step = sig("rwkv_operand_ready"), sig("bonus_sum_ready"), sig("k_factor_ready")
        with ExitStack() as local, nc.Block() as block:
            till = sb("decay_till", [P, 4, T], F32, local)
            before = sb("decay_before", [P, 4, T], F32, local)
            back = sb("decay_inverse", [P, 4, T], F32, local)
            factor = sb("k_factor", [P, 4, T], F32, local)

            @block.tensor
            def _(pe):
                for j in range(4):
                    for pair in range(2):
                        n = 2 * j + pair
                        if n >= 4:
                            pe.wait_ge(sums_read.sem, n - 3)
                        for half in range(2):
                            tile = 2 * pair + half
                            mm = nc.tensor.matmul(psum[:, n % 4, half * 2 * P:(half + 1) * 2 * P], decay_in[:, tile, j * P:(j + 1) * P],
                                                  sum_masks[:, :, :], start=True, stop=True)
                        mm.then_inc(sums_ready.sem, 1)
                for j in range(4):
                    pe.wait_ge(ops.sem, j + 1)
                    nc.tensor.matmul(psum[:, 4 + j, :], block_ones[:], bonus[:, j, :], start=True, stop=True).then_inc(bonus_sum.sem, 1)

            @block.scalar
            def _(act):
                for j in range(4):
                    for pair in range(2):
                        n = 2 * j + pair
                        act.wait_ge(sums_ready.sem, n + 1)
                        sums = psum[:, n % 4, :].rearrange("p (h m t) -> p h m t", h=2, m=2)
                        span = slice(2 * pair * P, 2 * (pair + 1) * P)

                        def two(buf):
                            return buf[:, j, span].rearrange("p (h t) -> p h t", h=2)
                        nc.scalar.activation(two(till), sums[:, :, 0, :], ACT.Exp, scale=-KAPPA)
                        nc.scalar.activation(two(back), sums[:, :, 0, :], ACT.Exp, scale=KAPPA)
                        nc.scalar.activation(two(before), sums[:, :, 1, :], ACT.Exp, scale=-KAPPA)
                        nc.scalar.activation(mid_decay[:, 1, j, 2 * pair:2 * pair + 2], sums[:, :, 0, P - 1], ACT.Exp, scale=-KAPPA)
                        nc.scalar.activation(mid_decay[:, 0, j, 2 * pair:2 * pair + 2], sums[:, :, 1, 0], ACT.Exp, scale=KAPPA).then_inc(sums_read.sem, 1)

            @block.vector
            def _(dve):
                for j in range(4):
                    nc.vector.tensor_scalar(factor[:, j, :], bb[:, j, :], 1.0, kav[:, j:j + 1], ALU.subtract, ALU.mult).then_inc(k_step.sem, 1)
                for j in range(4):
                    dve.wait_ge(k_step.sem, j + 1)
                    nc.vector.scalar_tensor_tensor(R(K_ + j), factor[:, j, :], 1.0, R(K_ + j), ALU.add, ALU.mult).then_inc(k_step.sem, 1)
                for j in range(4):
                    dve.wait_ge(k_step.sem, 4 + j + 1)
                    nc.vector.scalar_tensor_tensor(bonus[:, j, :], R(R_ + j), rkv[:, j:j + 1], R(K_ + j), ALU.mult, ALU.mult).then_inc(ops.sem, 1)
                for j in range(4):
                    nc.vector.tensor_tensor(bb[:, j, :], bb[:, j, :], kk[:, j, :], ALU.mult).then_inc(k_step.sem, 1)
                for j in range(4):
                    dve.wait_ge(bonus_sum.sem, j + 1)
                    nc.vector.tensor_tensor(bonus[:, j, :], R(V_ + j), psum[:, 4 + j, :], ALU.mult)
                for j in range(4):
                    dve.wait_ge(sums_read.sem, 2 * (j + 1))
                    dve.wait_ge(k_step.sem, 8 + j + 1)
                    nc.vector.tensor_tensor(bb[:, j, :], bb[:, j, :], back[:, j, :], ALU.mult)
                    nc.vector.scalar_tensor_tensor(kk[:, j, :], kk[:, j, :], -1.0, before[:, j, :], ALU.mult, ALU.mult)
                    nc.vector.tensor_tensor(R(K_ + j), R(K_ + j), back[:, j, :], ALU.mult)
                    nc.vector.tensor_tensor(R(R_ + j), R(R_ + j), till[:, j, :], ALU.mult)
        turned_stack.close()

        tok_turned, tok_copied = sig("operand_transposed"), sig("operand_copied")
        v_t = sb("rwkv_v_by_token", [P, TT, T], F32, rwkv_stack)
        k_t = sb("rwkv_k_by_token", [P, TT, T], F32, rwkv_stack)
        b_t = sb("rwkv_b_by_token", [P, TT, T], F32, rwkv_stack)
        with nc.Block() as block:
            turns = [(dst, get, tile) for dst, get in ((v_t, lambda j: R(V_ + j)), (k_t, lambda j: R(K_ + j)), (b_t, lambda j: bb[:, j, :]))
                     for tile in range(TT)]

            @block.tensor
            def _(pe):
                for n, (dst, get, tile) in enumerate(turns):
                    if n >= 4:
                        pe.wait_ge(tok_copied.sem, n - 3)
                    for j in range(4):
                        mm = nc.tensor.transpose(psum[:, n % 4, j * P:(j + 1) * P], get(j)[:, tile * P:(tile + 1) * P], ident[:])
                    mm.then_inc(tok_turned.sem, 1)

            @block.scalar
            def _(act):
                for n, (dst, get, tile) in enumerate(turns):
                    act.wait_ge(tok_turned.sem, n + 1)
                    nc.scalar.activation(dst[:, tile, :], psum[:, n % 4, :], ACT.Copy).then_inc(tok_copied.sem, 1)

        LEVELS = 6
        PAIRS = 5
        pair_mm, pair_done = sig("pair_products_ready"), sig("pair_products_masked")
        inverse_first, inverse_t_first = sig("first_inverse_ready"), sig("first_inverse_t_ready")
        part_ready, times_l, prod_copied = sig("joining_blocks_ready"), sig("l_times_inverse_ready"), sig("l_times_inverse_copied")
        joined, inverse_stepped, stepped = sig("joined_blocks_ready"), sig("inverse_stepped"), sig("inverse_t_stepped")
        unit_added = sig("inverse_t_first_step")
        x0_mm, x0_copied, sa_mm, sa_copied = sig("x0_ready"), sig("x0_copied"), sig("sa_ready"), sig("sa_copied")
        y_mm, y_copied, state_mm, state_done, state_step = sig("y_ready"), sig("y_copied"), sig("state_product_ready"), sig("state_updated"), sig("state_step")
        chunk_masks_loaded = sig("chunk_masks_loaded")
        with ExitStack() as local, nc.Block() as block:
            masks = sb("chunk_masks", [P, 11, P], F32, local)
            lak, lrb, lrk, low, inv, inv_t, prod, part = (sb(n, [P, 8, P], F32, local) for n in (
                "chunk_lak", "chunk_lrb", "chunk_lrk", "chunk_l_t", "chunk_inverse", "chunk_inverse_t", "chunk_l_inverse", "chunk_l_part"))
            state = sb("state", [P, 4, 64], F32, local)
            x0 = sb("chunk_x0", [P, 8, 64], F32, local)
            sa = sb("chunk_sa", [P, 8, 64], F32, local)

            def at_head(h):
                return (h % 2) * 4 + h // 2

            def rows(h):
                return slice(64 * (h % 2), 64 * (h % 2) + 64)

            def both(b):
                return psum[:, b:b + 2, :].rearrange("p b (h t) -> p (b h) t", t=P)

            def half(buf, g):
                return buf[:, 4 * g:4 * g + 4, :]

            def bank4(b):
                return psum[:, b, :].rearrange("p (h t) -> p h t", t=P)

            def mask(m, n):
                return masks[:, m, :].unsqueeze(1).to_broadcast([P, n, P])

            @block.sync
            def _(sp):
                sp.dma_start(masks[:, :, :], rwkv["chunk_masks"]).then_inc(chunk_masks_loaded.sem, 16)

            @block.tensor
            def _(pe):
                for c in range(TT):
                    tok, tok1 = slice(c * P, (c + 1) * P), slice(1 + c * P, 1 + (c + 1) * P)

                    def a_(h): return kk[rows(h), h // 2, tok]
                    def b_(h): return bb[rows(h), h // 2, tok]
                    def k_(h): return rw[rows(h), K_ + h // 2, tok1]
                    def r_(h): return rw[rows(h), R_ + h // 2, tok1]
                    if c:
                        pe.wait_ge(y_copied.sem, c)
                        pe.wait_ge(state_done.sem, c)
                    for n, (one, two) in enumerate(((a_, b_), (b_, a_), (k_, a_), (b_, r_), (k_, r_))):
                        m = c * PAIRS + n
                        if m >= 2:
                            pe.wait_ge(pair_done.sem, m - 1)
                        for h in range(8):
                            mm = nc.tensor.matmul(both(2 * (m % 2))[:, at_head(h), :], one(h), two(h), start=True, stop=True)
                        mm.then_inc(pair_mm.sem, 1)
                    for l in range(LEVELS):
                        for g in range(2):
                            n = (c * LEVELS + l) * 2 + g
                            pe.wait_ge(part_ready.sem, n + 1)
                            if l == 0:
                                pe.wait_ge(inverse_first.sem, c + 1)
                            else:
                                pe.wait_ge(inverse_stepped.sem, (c * (LEVELS - 1) + l - 1) * 2 + g + 1)
                            for h in range(g, 8, 2):
                                mm = nc.tensor.matmul(psum[:, 4 + g, (h // 2) * P:(h // 2 + 1) * P], part[:, at_head(h), :], inv[:, at_head(h), :],
                                                      start=True, stop=True)
                            mm.then_inc(times_l.sem, 1)
                        for g in range(2):
                            n = (c * LEVELS + l) * 2 + g
                            pe.wait_ge(prod_copied.sem, n + 1)
                            if l == 0:
                                pe.wait_ge(inverse_t_first.sem, c + 1)
                            else:
                                pe.wait_ge(stepped.sem, n - 1)
                            for h in range(g, 8, 2):
                                mm = nc.tensor.matmul(psum[:, 6 + g, (h // 2) * P:(h // 2 + 1) * P], prod[:, at_head(h), :], inv_t[:, at_head(h), :],
                                                      start=True, stop=True)
                            if l < LEVELS - 1:
                                for h in range(g, 8, 2):
                                    mm = nc.tensor.matmul(psum[:, 4 + g, (h // 2) * P:(h // 2 + 1) * P], inv_t[:, at_head(h), :], prod[:, at_head(h), :],
                                                          start=True, stop=True)
                            mm.then_inc(joined.sem, 1)
                    pe.wait_ge(pair_done.sem, PAIRS * (c + 1))
                    for h in range(8):
                        out = psum[:, h % 2, (h // 2) * 64:(h // 2 + 1) * 64]
                        if c:
                            nc.tensor.matmul(out, a_(h), state[rows(h), h // 2, :], start=True, stop=False)
                        mm = nc.tensor.matmul(out, lak[:, at_head(h), :], v_t[:, c, h * 64:(h + 1) * 64], start=not c, stop=True)
                    mm.then_inc(x0_mm.sem, 1)
                    pe.wait_ge(x0_copied.sem, c + 1)
                    pe.wait_ge(stepped.sem, 2 * LEVELS * (c + 1))
                    for h in range(8):
                        mm = nc.tensor.matmul(psum[:, 2, at_head(h) * 64:(at_head(h) + 1) * 64], inv_t[:, at_head(h), :], x0[:, at_head(h), :],
                                              start=True, stop=True)
                    mm.then_inc(sa_mm.sem, 1)
                    pe.wait_ge(sa_copied.sem, c + 1)
                    for h in range(8):
                        out = psum[rows(h), h % 2, (h // 2) * P:(h // 2 + 1) * P]
                        if c:
                            nc.tensor.matmul(out, state[rows(h), h // 2, :], r_(h), start=True, stop=False)
                        nc.tensor.matmul(out, sa[:, at_head(h), :], lrb[:, at_head(h), :], start=not c, stop=False)
                        mm = nc.tensor.matmul(out, v_t[:, c, h * 64:(h + 1) * 64], lrk[:, at_head(h), :], start=False, stop=True)
                    mm.then_inc(y_mm.sem, 1)
                    for h in range(8):
                        out = psum[rows(h), 2 + h % 2, (h // 2) * 64:(h // 2 + 1) * 64]
                        nc.tensor.matmul(out, b_t[:, c, h * 64:(h + 1) * 64], sa[:, at_head(h), :], start=True, stop=False)
                        mm = nc.tensor.matmul(out, k_t[:, c, h * 64:(h + 1) * 64], v_t[:, c, h * 64:(h + 1) * 64], start=False, stop=True)
                    mm.then_inc(state_mm.sem, 1)

            @block.scalar
            def _(act):
                for c in range(TT):
                    for l in range(LEVELS):
                        for g in range(2):
                            n = (c * LEVELS + l) * 2 + g
                            act.wait_ge(times_l.sem, n + 1)
                            nc.scalar.activation(half(prod, g), bank4(4 + g), ACT.Copy).then_inc(prod_copied.sem, 1)
                    act.wait_ge(x0_mm.sem, c + 1)
                    nc.scalar.activation(x0[:, :, :].rearrange("p (g h) v -> p g (h v)", g=2), psum[:, 0:2, 0:256], ACT.Copy).then_inc(x0_copied.sem, 1)
                    act.wait_ge(sa_mm.sem, c + 1)
                    nc.scalar.activation(sa[:, :, :].rearrange("p h v -> p (h v)"), psum[:, 2, :], ACT.Copy).then_inc(sa_copied.sem, 1)
                    act.wait_ge(y_mm.sem, c + 1)
                    for g in range(2):
                        part_rows = slice(64 * g, 64 * g + 64)
                        copied = nc.scalar.activation(y[part_rows, :, c * P:(c + 1) * P], bank4(g)[part_rows, :, :], ACT.Copy)
                    copied.then_inc(y_copied.sem, 1)

            @block.gpsimd
            def _(pool):
                pool.wait_ge(chunk_masks_loaded.sem, 16)
                for c in range(TT):
                    pool.wait_ge(pair_done.sem, PAIRS * c + 2)
                    nc.gpsimd.tensor_tensor(inv_t[:, :, :], low[:, :, :], mask(8, 8), ALU.mult).then_inc(unit_added.sem, 1)
                    pool.wait_ge(unit_added.sem, c + 1)
                    nc.gpsimd.tensor_tensor(inv_t[:, :, :], inv_t[:, :, :], mask(10, 8), ALU.add).then_inc(inverse_t_first.sem, 1)
                    for l in range(LEVELS):
                        for g in range(2):
                            n = (c * LEVELS + l) * 2 + g
                            if n >= 2:
                                pool.wait_ge(times_l.sem, n - 1)
                            nc.gpsimd.tensor_tensor(half(part, g), half(low, g), mask(2 + l, 4), ALU.mult).then_inc(part_ready.sem, 1)

            @block.vector
            def _(dve):
                dve.wait_ge(chunk_masks_loaded.sem, 16)
                for c in range(TT):
                    if c:
                        dve.wait_ge(part_ready.sem, 2 * LEVELS * c)
                    for n, (dst, m) in enumerate(((inv, 9), (low, 0), (lak, 0), (lrb, 1), (lrk, 1))):
                        dve.wait_ge(pair_mm.sem, PAIRS * c + n + 1)
                        nc.vector.tensor_tensor(dst[:, :, :], both(2 * ((PAIRS * c + n) % 2)), mask(m, 8), ALU.mult).then_inc(pair_done.sem, 1)
                        if n == 1:
                            dve.wait_ge(pair_done.sem, PAIRS * c + 1)
                            nc.vector.tensor_tensor(inv[:, :, :], inv[:, :, :], mask(10, 8), ALU.add).then_inc(inverse_first.sem, 1)
                    for l in range(LEVELS):
                        for g in range(2):
                            n = (c * LEVELS + l) * 2 + g
                            dve.wait_ge(joined.sem, n + 1)
                            if l < LEVELS - 1:
                                nc.vector.tensor_tensor(half(inv, g), half(inv, g), bank4(4 + g), ALU.add).then_inc(inverse_stepped.sem, 1)
                            nc.vector.tensor_tensor(half(inv_t, g), half(inv_t, g), bank4(6 + g), ALU.add).then_inc(stepped.sem, 1)
                    dve.wait_ge(state_mm.sem, c + 1)
                    if c < TT - 1:
                        for g in range(2):
                            part_rows = slice(64 * g, 64 * g + 64)
                            new = psum[part_rows, 2 + g, 0:256].rearrange("p (h v) -> p h v", v=64)
                            if c:
                                step = nc.vector.tensor_tensor(state[part_rows, :, :], state[part_rows, :, :], new, ALU.add)
                            else:
                                step = nc.vector.tensor_copy(state[part_rows, :, :], new)
                        step.then_inc(state_step.sem, 1)
                        dve.wait_ge(state_step.sem, 2 * c + 1)
                        nc.vector.tensor_tensor(state[:, :, :], state[:, :, :], mid_decay[:, 1, :, c].unsqueeze(2).to_broadcast([P, 4, 64]),
                                                ALU.mult).then_inc(state_step.sem, 1)
                        dve.wait_ge(state_step.sem, 2 * c + 2)
                        nc.vector.tensor_tensor(state[:, :, :], state[:, :, :], mid_decay[:, 0, :, c + 1].unsqueeze(2).to_broadcast([P, 4, 64]),
                                                ALU.mult).then_inc(state_done.sem, 1)

        head_norm(y, block_avg[:], ln_eps[:, 0:1], center=True)
        gate_product, out_step = sig("rwkv_gate_ready"), sig("rwkv_out_step")
        with nc.Block() as block:
            @block.tensor
            def _(pe):
                for j in range(4):
                    cols = slice(j * P, (j + 1) * P)
                    nc.tensor.matmul(psum[:, j, :], lora[:, 1, cols], R(G_), start=True, stop=False)
                    nc.tensor.matmul(psum[:, j, :], lora[0:32, 2, cols], rw[0:32, G_ + 1, 1:T + 1], start=False, stop=True).then_inc(gate_product.sem, 1)

            @block.vector
            def _(dve):
                for j in range(4):
                    nc.vector.tensor_scalar(y[:, j, :], y[:, j, :], lnw[:, j:j + 1], lnb[:, j:j + 1], ALU.mult, ALU.add).then_inc(out_step.sem, 1)
                for j in range(4):
                    dve.wait_ge(out_step.sem, j + 1)
                    nc.vector.tensor_tensor(y[:, j, :], y[:, j, :], bonus[:, j, :], ALU.add).then_inc(out_step.sem, 1)
                for j in range(4):
                    dve.wait_ge(out_step.sem, 4 + j + 1)
                    dve.wait_ge(gate_product.sem, j + 1)
                    nc.vector.tensor_tensor(y[:, j, :], y[:, j, :], psum[:, j, :], ALU.mult)
        rwkv_stack.close()
        if stop == 4:
            return

        branch_stack = ExitStack()
        ctx.enter_context(branch_stack)
        branch_hi = sb("branch_hi", [P, C, T], F32R, branch_stack)
        branch_lo = sb("branch_lo", [P, C, T], F32R, branch_stack)
        act_hi = sb("act_hi", [P, C, T], F32R, branch_stack)
        act_lo = sb("act_lo", [P, C, T], F32R, branch_stack)
        split([(y[:, j, :], 1.0) for j in range(4)], branch_hi, branch_lo)
        split([(x[:, c, :], gains[:, 3, c:c + 1]) for c in range(C)], act_hi, act_lo)
        conv_u, conv_acc, conv_w_loaded = sig("conv_input_ready"), sig("conv_step"), sig("conv_weights_loaded")
        with ExitStack() as local:
            cv = sb("conv_projections", [P, 12, T], F32, local)
            acc = sb("conv_out", [P, 4, T], F32, local)
            taps = sb("conv_taps", [P, 4, 3], F32, local)
            linear(12, (act_hi, act_lo), scaled(lambda n: cv[:, n, :]), "vector")
            with nc.Block() as block:
                @block.sync
                def _(sp):
                    sp.dma_start(taps[:, :, :], conv_taps).then_inc(conv_w_loaded.sem, 16)

                @block.gpsimd
                def _(pool):
                    for j in range(4):
                        nc.gpsimd.tensor_tensor(cv[:, 4 + j, :], cv[:, 4 + j, :], cv[:, 8 + j, :], ALU.mult).then_inc(conv_u.sem, 1)

                @block.vector
                def _(dve):
                    dve.wait_ge(conv_w_loaded.sem, 16)
                    for j in range(4):
                        dve.wait_ge(conv_u.sem, j + 1)
                        u, a = cv[:, 4 + j, :], acc[:, j, :]
                        nc.vector.tensor_scalar(a, u, taps[:, j, 2:3], None, ALU.mult).then_inc(conv_acc.sem, 1)
                        for back, tap in ((1, 1), (2, 0)):
                            dve.wait_ge(conv_acc.sem, 3 * j + back)
                            nc.vector.scalar_tensor_tensor(acc[:, j, back:T], cv[:, 4 + j, 0:T - back], taps[:, j, tap:tap + 1], acc[:, j, back:T],
                                                           ALU.mult, ALU.add).then_inc(conv_acc.sem, 1)
                        dve.wait_ge(conv_acc.sem, 3 * j + 3)
                        nc.vector.tensor_tensor(a, a, cv[:, j, :], ALU.mult)
            split([(acc[:, j, :], 1.0) for j in range(4)], branch_hi, branch_lo, 4)

        gate_sig, gate_a, merged_f, merged_hi_ready = sig("merge_gates_ready"), sig("merge_gated"), sig("merged_ready"), sig("merged_hi_ready")
        gate_bias_loaded, gate_in = sig("gate_bias_loaded"), sig("merge_gates_scaled")
        inner_hi = sb("inner_hi", [P, C, T], F32R, branch_stack)
        inner_lo = sb("inner_lo", [P, C, T], F32R, branch_stack)
        with ExitStack() as local, nc.Block() as block:
            gate_bias = sb("gate_bias", [P, 2, C], F32, local)
            opened = sb("merge_gates", [P, 2, T], F32, local)
            gate_raw = sb("merge_gates_raw", [P, 2, T], F32, local)
            gated_b = sb("merge_gated_branches", [P, 2, T], F32, local)
            merged = sb("merged", [P, 2, T], F32, local)
            w, u0, per, turn = weights, weights.u0, 12, 4

            @block.sync
            def _(sp):
                sp.dma_start(gate_bias[:, :, :], gate_bias_in).then_inc(gate_bias_loaded.sem, 16)
                w.load_stage(sp, 3 * C)

            @block.tensor
            def _(pe):
                pe.sem_inc(merged_f.sem, 2)
                with pe.Fori(0, C // turn) as i:
                    for q in range(turn):
                        b = 4 * (q % 2)
                        pe.wait_ge(merged_f.sem, i * turn + (q + 1))
                        w.multiply(pe, i, 3 * q, per, psum[:, b, :], (branch_hi[:, 0:4, :], branch_lo[:, 0:4, :]), chunks=range(4))
                        w.multiply(pe, i, 3 * q, per, psum[:, b + 1, :], (branch_hi[:, 4:8, :], branch_lo[:, 4:8, :]),
                                   chunks=range(4, 8)).then_inc(w.unit_done.sem, 1)
                        for g in range(2):
                            w.multiply(pe, i, 3 * q + 1 + g, per, psum[:, b + 2 + g, :], (act_hi, act_lo)).then_inc(w.unit_done.sem, 1)

            @block.scalar
            def _(act):
                act.wait_ge(gate_bias_loaded.sem, 16)
                act.sem_inc(gate_a.sem, 2)
                with act.Fori(0, C // turn) as i:
                    for q in range(turn):
                        for g in range(3):
                            w.hi_step(act, i, 3 * q + g + w.AHEAD, per)
                            if g:
                                act.wait_ge(gate_in.sem, i * (2 * turn) + (2 * q + g))
                                act.wait_ge(gate_a.sem, i * (2 * turn) + (2 * q + g))
                                nc.scalar.activation(opened[:, g - 1, :], gate_raw[:, g - 1, :], ACT.Sigmoid,
                                                     bias=gate_bias[:, g - 1, bass.ds(i * turn + q, 1)]).then_inc(gate_sig.sem, 1)
                        act.wait_ge(merged_f.sem, i * turn + (q + 3))
                        nc.scalar.activation(inner_hi[:, bass.ds(i * turn + q, 1), :], merged[:, q % 2, :].unsqueeze(1), ACT.Copy).then_inc(merged_hi_ready.sem, 1)

            @block.vector
            def _(dve):
                with dve.Fori(0, C // turn) as i:
                    for q in range(turn):
                        for g in range(3):
                            w.lo_step(dve, i, 3 * q + g + w.AHEAD, per)
                            if g:
                                dve.wait_ge(w.unit_done.sem, i * per + w.done(3 * q + g))
                                nc.vector.tensor_tensor(gate_raw[:, g - 1, :], psum[:, 4 * (q % 2) + 1 + g, :], rstd[:], ALU.mult).then_inc(gate_in.sem, 1)
                                dve.wait_ge(gate_sig.sem, i * (2 * turn) + (2 * q + g))
                                nc.vector.tensor_tensor(gated_b[:, g - 1, :], opened[:, g - 1, :],
                                                        psum[:, 4 * (q % 2) + g - 1, :], ALU.mult).then_inc(gate_a.sem, 1)
                        dve.wait_ge(gate_a.sem, i * (2 * turn) + (2 * q + 4))
                        nc.vector.tensor_tensor(merged[:, q % 2, :], gated_b[:, 0, :], gated_b[:, 1, :], ALU.add).then_inc(merged_f.sem, 1)
                        dve.wait_ge(merged_hi_ready.sem, i * turn + (q + 1))
                        nc.vector.tensor_tensor(inner_lo[:, bass.ds(i * turn + q, 1), :], merged[:, q % 2, :].unsqueeze(1),
                                                inner_hi[:, bass.ds(i * turn + q, 1), :].bitcast(F32), ALU.subtract)
            w.u0 += 3 * C

        def add_to_x(loop, k, bank):
            return nc.vector.tensor_tensor(x[:, at(loop, k), :], x[:, at(loop, k), :], bank, ALU.add)

        linear(C, (inner_hi, inner_lo), add_to_x, "vector")
        branch_stack.close()
        if stop == 5:
            return

        mem_stack = ExitStack()
        ctx.enter_context(mem_stack)
        kv = sb("memory_kv", [P, 2 * C, M], F32, mem_stack)
        v_m = sb("memory_v_by_token", [P, M // P, D], F32, mem_stack)
        queries = sb("memory_queries", [P, C, T], F32, mem_stack)
        mem_loaded = sig("memory_loaded")
        with ExitStack() as local:
            mem_sb = sb("memory", [P, C, M], F32, local)
            mem_hi = sb("memory_hi", [P, C, M], F32R, local)
            mem_lo = sb("memory_lo", [P, C, M], F32R, local)
            with nc.Block() as block:
                @block.sync
                def _(sp):
                    sp.dma_start(mem_sb[:, :, :], mem_t).then_inc(mem_loaded.sem, 16)
                    sp.wait_ge(mem_loaded.sem, 16)
            linear(2 * C, (mem_hi, mem_lo), scaled(lambda n: kv[:, n, :], M), "vector", tokens=M, norm=(mem_sb, 5))
        with ExitStack() as local:
            act_hi = sb("act_hi", [P, C, T], F32R, local)
            act_lo = sb("act_lo", [P, C, T], F32R, local)
            linear(C, (act_hi, act_lo), scaled(lambda n: queries[:, n, :]), "vector", norm=(x, 4))
        x_scored, x_max, x_neg, x_exp, x_inv, x_prob = (sig(n) for n in (
            "memory_scores_ready", "memory_max_ready", "memory_neg_max_ready", "memory_exp_ready", "memory_inverse_sum_ready", "memory_probs_ready"))
        x_turned, x_copied, x_out, v_m_turned, v_m_copied = (sig(n) for n in (
            "memory_probs_transposed", "memory_probs_copied", "memory_out_ready", "memory_v_transposed", "memory_v_copied"))
        x_out_copied = sig("memory_out_copied")
        out_f = sb("memory_out", [P, C, T], F32, mem_stack)
        XH = 4
        MT = M // P
        with ExitStack() as local, nc.Block() as block:
            pr = sb("memory_probs", [P, 2, M], F32, local)
            pr_t = sb("memory_probs_t", [P, 2, MT, T], F32, local)
            st = sb("memory_stats", [P, XH * TT, 4], F32, local)
            x_scale = 256 ** -0.5

            @block.tensor
            def _(pe):
                for mt in range(MT):
                    for half_c in range(2):
                        n = 2 * mt + half_c
                        if n >= 2:
                            pe.wait_ge(v_m_copied.sem, n - 1)
                        for j in range(4):
                            mm = nc.tensor.transpose(psum[:, 4 + n % 2, j * P:(j + 1) * P], kv[:, C + 4 * half_c + j, mt * P:(mt + 1) * P], ident[:])
                        mm.then_inc(v_m_turned.sem, 1)

                def scores(it):
                    h, tile = divmod(it, TT)
                    if it >= 3:
                        pe.wait_ge(x_exp.sem, it - 2)
                    for e in range(2):
                        mm = nc.tensor.matmul(psum[:, it % 3, 0:M], queries[:, 2 * h + e, tile * P:(tile + 1) * P], kv[:, 2 * h + e, :],
                                              start=e == 0, stop=e == 1)
                    mm.then_inc(x_scored.sem, 1)
                scores(0)
                scores(1)
                for it in range(XH * TT):
                    h, tile = divmod(it, TT)
                    if it + 2 < XH * TT:
                        scores(it + 2)
                    pe.wait_ge(x_prob.sem, it + 1)
                    if it >= 1:
                        pe.wait_ge(x_copied.sem, it)
                    for mt in range(MT):
                        mm = nc.tensor.transpose(psum[:, 3, mt * P:(mt + 1) * P], pr[:, it % 2, mt * P:(mt + 1) * P], ident[:])
                    mm.then_inc(x_turned.sem, 1)
                    if tile == TT - 1:
                        pe.wait_ge(x_copied.sem, it + 1)
                        pe.wait_ge(v_m_copied.sem, 2 * MT)
                        if h >= 1:
                            pe.wait_ge(x_out_copied.sem, 2 * h)
                        for e in range(2):
                            for mt in range(MT):
                                mm = nc.tensor.matmul(psum[:, 6 + e, :], v_m[:, mt, (2 * h + e) * P:(2 * h + e + 1) * P], pr_t[:, h % 2, mt, :],
                                                      start=mt == 0, stop=mt == MT - 1)
                            mm.then_inc(x_out.sem, 1)

            @block.scalar
            def _(act):
                for n in range(2 * MT):
                    act.wait_ge(v_m_turned.sem, n + 1)
                    nc.scalar.activation(v_m[:, n // 2, (n % 2) * T:(n % 2 + 1) * T], psum[:, 4 + n % 2, :], ACT.Copy).then_inc(v_m_copied.sem, 1)

                def exps(it):
                    act.wait_ge(x_neg.sem, it + 1)
                    if it >= 2:
                        act.wait_ge(x_turned.sem, it - 1)
                    nc.scalar.activation(pr[:, it % 2, :], psum[:, it % 3, 0:M], ACT.Exp, bias=st[:, it, 1:2], scale=x_scale,
                                         accum_out=st[:, it, 2:3]).then_inc(x_exp.sem, 1)
                exps(0)
                for it in range(XH * TT):
                    h, tile = divmod(it, TT)
                    if it + 1 < XH * TT:
                        exps(it + 1)
                    act.wait_ge(x_turned.sem, it + 1)
                    if h >= 2:
                        act.wait_ge(x_out.sem, 2 * (h - 1))
                    nc.scalar.activation(pr_t[:, h % 2, :, tile * P:(tile + 1) * P], psum[:, 3, 0:M].rearrange("p (m t) -> p m t", m=MT),
                                         ACT.Copy).then_inc(x_copied.sem, 1)
                    if tile == TT - 1:
                        for e in range(2):
                            act.wait_ge(x_out.sem, 2 * h + e + 1)
                            nc.scalar.activation(out_f[:, 2 * h + e, :], psum[:, 6 + e, :], ACT.Copy).then_inc(x_out_copied.sem, 1)

            @block.vector
            def _(dve):
                def maxima(it):
                    dve.wait_ge(x_scored.sem, it + 1)
                    nc.vector.tensor_reduce(st[:, it, 0:1], psum[:, it % 3, 0:M], AX.X, ALU.max).then_inc(x_max.sem, 1)
                    dve.wait_ge(x_max.sem, it + 1)
                    nc.vector.tensor_scalar(st[:, it, 1:2], st[:, it, 0:1], -x_scale, None, ALU.mult).then_inc(x_neg.sem, 1)
                maxima(0)
                maxima(1)
                for it in range(XH * TT):
                    dve.wait_ge(x_exp.sem, it + 1)
                    nc.vector.reciprocal(st[:, it, 3:4], st[:, it, 2:3]).then_inc(x_inv.sem, 1)
                    dve.wait_ge(x_inv.sem, it + 1)
                    nc.vector.tensor_scalar(pr[:, it % 2, :], pr[:, it % 2, :], st[:, it, 3:4], None, ALU.mult).then_inc(x_prob.sem, 1)
                    if it + 2 < XH * TT:
                        maxima(it + 2)
        with ExitStack() as local:
            out_hi = sb("memory_out_hi", [P, C, T], F32R, local)
            out_lo = sb("memory_out_lo", [P, C, T], F32R, local)
            split([(out_f[:, j, :], 1.0) for j in range(C)], out_hi, out_lo)
            linear(C, (out_hi, out_lo), add_to_x, "vector")
        mem_stack.close()
        if stop == 6:
            return

        with ExitStack() as local:
            act_hi = sb("act_hi", [P, C, T], F32R, local)
            act_lo = sb("act_lo", [P, C, T], F32R, local)
            inner_hi = sb("inner_hi", [P, C, T], F32R, local)
            inner_lo = sb("inner_lo", [P, C, T], F32R, local)
            raw_act = sb("inner_activated", [P, 2, T], F32, local)
            raw_gated = sb("inner_gated", [P, 2, T], F32, local)
            norm_alone(x, 6, act_hi, act_lo)
            feed_forward(MLP_GROUPS, (act_hi, act_lo), ACT.Relu, False, inner_hi, inner_lo, raw_act, raw_gated)
        rms_norm(x, 7, out_f32=x)
        stored = sig("output_stored")
        with nc.Block() as block:
            @block.sync
            def _(sp):
                sp.dma_start(out_t, x[:, :, :]).then_inc(stored.sem, 16)
                sp.wait_ge(stored.sem, 16)


def unit_layout(w):
    import numpy as np
    k, n = w.shape
    return np.ascontiguousarray(w.reshape(C, P, n // P, P).transpose(2, 1, 0, 3)).reshape(n // P, P, UNIT)


def constants():
    import numpy as np
    f = np.float32
    pos = np.arange(T, dtype=f)

    def rope(inv, dim, block):
        half = len(inv)
        ang = (pos[:, None] * inv[None, :]).astype(f)
        cos, sin = np.ones((block, T), f), np.zeros((block, T), f)
        swap = np.zeros((block, block), f)
        cos[:half] = cos[half:2 * half] = np.cos(ang).T
        sin[:half], sin[half:2 * half] = -np.sin(ang).T, np.sin(ang).T
        for i in range(half):
            swap[i, i + half] = swap[i + half, i] = 1
        n = P // block
        return np.tile(cos, (n, 1)), np.tile(sin, (n, 1)), np.kron(np.eye(n, dtype=f), swap)

    inv_d = np.power(f(500000.0), -np.arange(8, dtype=f) * f(2.0) / f(16)).astype(f)
    inv_r = (f(1.0) / np.power(f(10000.0), np.linspace(0.0, 1.0, 32, dtype=f))).astype(f)
    cd, sd, swd = rope(inv_d, 16, 64)
    cr, sr, swr = rope(inv_r, 64, 64)
    span = T + (TT - 1) * P
    ahead = (np.arange(span)[None, :] - (TT - 1) * P - np.arange(P)[:, None]).astype(f)
    n = np.arange(P)
    s, t = n[:, None], n[None, :]
    levels = [((s // m) % 2 == 0) & (t // m == s // m + 1) for m in (2, 4, 8, 16, 32, 64)]
    join0 = (s % 2 == 0) & (t == s + 1)
    blocks = np.kron(np.eye(2, dtype=f), np.ones((64, 64), f))
    return {
        "rwkv_sum_masks": np.ascontiguousarray(np.stack([(s <= t) * 1.0 - (s < 64), (s < t) * 1.0 - (s < 64)], 1).astype(f)),
        "rwkv_chunk_masks": np.ascontiguousarray(np.stack([s < t, s <= t, *levels, join0, join0.T, s == t], 1).astype(f)),
        "rwkv_block_ones": blocks,
        "rwkv_block_average": blocks / f(64),
        "rope_tables": np.ascontiguousarray(np.stack([cd, sd, cr, sr], 1)),
        "swap": np.ascontiguousarray(np.stack([swd, swr], 1)),
        "iota_in": np.tile(np.arange(P, dtype=f), (P, 1)),
        "ident_in": np.eye(P, dtype=f),
        "distance": np.ascontiguousarray(np.stack([np.maximum(ahead, 0), np.maximum(-ahead, 0)], 1)),
    }


def expert_units(u, v):
    import numpy as np
    up = u.reshape(P, EXPERT_GROUPS, C, C, P).transpose(1, 2, 4, 3, 0)
    down = v.reshape(P, EXPERT_GROUPS, C, C, P).transpose(1, 3, 0, 2, 4)
    up, down, n = up.reshape(-1, C, P, UNIT), down.reshape(-1, C, P, UNIT), GROUPS_AHEAD
    rest = np.concatenate([up[n:], down[n:]], 1)
    return np.concatenate([part.reshape(-1, P, UNIT) for part in (up[:n], down[:n], rest)])


def mlp_units(up, down):
    import numpy as np
    groups = down.shape[0] // D
    ups = unit_layout(up).reshape(groups, C, P, UNIT)
    downs = down.reshape(groups, C, P, C, P).transpose(0, 3, 2, 1, 4).reshape(groups, C, P, UNIT)
    return np.concatenate([ups, downs], 1).reshape(-1, P, UNIT)


def host_layout(inputs):
    import numpy as np

    def by_feature(v):
        return np.ascontiguousarray(v.reshape(-1, P).T)

    def tokens_last(a):
        return np.ascontiguousarray(a.T.reshape(-1, P, a.shape[0]).transpose(1, 0, 2))

    g = {k: np.asarray(v) for k, v in inputs.items()}
    w2 = g["w_in_2"][0]
    rwkv_cols, conv_cols = 1824, 3 * 512
    w_rwkv = np.concatenate([w2[:, :rwkv_cols], np.zeros((D, RWKV_SLABS * P - rwkv_cols), w2.dtype)], 1)
    w_merge = np.stack([unit_layout(np.concatenate([g["w_proj_a_2"][0], g["w_proj_b_2"][0]], 0)),
                        unit_layout(w2[:, rwkv_cols + conv_cols:rwkv_cols + conv_cols + D]),
                        unit_layout(w2[:, rwkv_cols + conv_cols + D:])], 1).reshape(-1, P, UNIT)
    mu = np.concatenate([g["mu_shift_2"][0], np.zeros(RWKV_SLABS * P - rwkv_cols, w2.dtype)])
    vectors = np.concatenate([by_feature(mu), np.zeros((P, 1), w2.dtype)]
                             + [by_feature(g[n][0].reshape(-1)) for n in ("k_k_2", "k_a_2", "r_k_2", "a0_2", "ln_x_w_2", "ln_x_b_2")], 1)
    gains = [g[n].reshape(-1) for n in ("attn_norm_g", "ffn_norm_g", "final_norm_g", "norm_mix_2", "norm_xattn_2",
                                        "norm_mem_2", "norm_mlp_2", "norm_final_2")]
    arrays = {
        "x_t": tokens_last(g["x"][0]),
        "mem_t": tokens_last(g["mem_2"][0]),
        "norm_gains": np.ascontiguousarray(np.stack([by_feature(v) for v in gains], 1)),
        "lam_in": np.ascontiguousarray(np.tile(g["diff_lambda"], (P, 1, 1))),
        "diff_gain": np.ascontiguousarray(g["diff_norm_g"][0].reshape(P, 1)),
        "ret_decay": np.ascontiguousarray(np.tile(g["ret_log_decay"].reshape(1, -1), (P, 1))),
        "ret_gain": np.ascontiguousarray(g["ret_norm_g"][0].T),
        "keys_t": np.ascontiguousarray(g["peer_sub_keys"][0].reshape(LISTS, N_KEYS, P).transpose(2, 0, 1)),
        "rwkv_vectors": np.ascontiguousarray(vectors),
        "rwkv_lora_wa": np.ascontiguousarray(np.concatenate([g["w_lora_w_2"][0], g["w_lora_a_2"][0]], 0)),
        "rwkv_lora_g": np.ascontiguousarray(g["w_lora_g_2"][0]),
        "rwkv_w0": np.ascontiguousarray(g["w0_2"]),
        "conv_taps": np.ascontiguousarray(g["conv_w_2"][0, :, 0, :].T.reshape(4, P, 3).transpose(1, 0, 2)),
        "gate_bias_in": np.ascontiguousarray(g["b_gate_2"][0].reshape(2, C, P).transpose(2, 0, 1)),
        "u_in": unit_layout(g["w_in"][0]),
        "u_out": unit_layout(g["w_out"][0]),
        "u_query": unit_layout(g["peer_w_query"][0]),
        "u_experts": expert_units(g["peer_u"][0], g["peer_v"][0]),
        "u_rwkv": unit_layout(w_rwkv),
        "u_conv": unit_layout(w2[:, rwkv_cols:rwkv_cols + conv_cols]),
        "u_merge": w_merge,
        "u_out_mix": unit_layout(g["w_out_mix_2"][0]),
        "u_kv": unit_layout(g["w_kv_2"][0]),
        "u_q": unit_layout(g["w_q_2"][0]),
        "u_xo": unit_layout(g["w_xo_2"][0]),
        "u_mlp": mlp_units(g["w_up_2"][0], g["w_down_2"][0]),
    }
    arrays.update(constants())
    return arrays


def kernel(**inputs):
    import numpy as np
    import concourse.bacc as bacc
    from concourse.bass_utils import run_bass_kernel_spmd
    arrays = host_layout(inputs)
    nc = bacc.Bacc("TRN2", target_bir_lowering=False, num_devices=1)
    aps = {k: nc.dram_tensor("in_" + k, v.shape, mybir.dt.from_np(v.dtype), kind="ExternalInput").ap() for k, v in arrays.items()}
    out = nc.dram_tensor("out_0_dram", (P, C, T), mybir.dt.float32, kind="ExternalOutput").ap()
    build_program(nc, aps, out)
    r = run_bass_kernel_spmd(nc, [{"in_" + k: v for k, v in arrays.items()}], core_ids=[0])
    got = np.asarray(r.results[0]["out_0_dram"])
    return np.ascontiguousarray(got.transpose(2, 1, 0).reshape(1, T, D))
```

```python
import math

import concourse.bass as bass
from concourse import mybir
from contextlib import ExitStack

F32 = mybir.dt.float32
F32R = mybir.dt.float32r
U32 = mybir.dt.uint32
ALU = mybir.AluOpType
ACT = mybir.ActivationFunctionType
AX = mybir.AxisListType

P = 128
T = 512
TT = T // P
D = 1024
C = D // P
UNIT = C * P
RING = 4
EPS = 1e-6

IN_SLABS = 24
DQ, DK, DV, RQ, RK, RV, RG = 0, 4, 8, 12, 14, 16, 20
HEADS = 4
N_KEYS = 128
DIFF_QK = 64
RET_QK = 64
LAMBDA_INIT = 0.8 - 0.6
PEER_HEADS = 8
TOPK = 16
LOWEST = -3.0e38
LISTS = 2 * PEER_HEADS
PICKS = PEER_HEADS * TOPK
EXPERT_GROUPS = N_KEYS // C
MLP_GROUPS = 4
M = 256
RWKV_SLABS = 15
RWKV_LN_EPS = 64e-5
GT = 64
GBLOCKS = T // GT
UP_TILE = C + 2
UP_DENSE = 2 * C
UP_TAIL = C // 2
UP_FIRST = C // 2
GROUPS_AHEAD = (TT * UP_TILE + UP_DENSE + UP_TAIL + UP_FIRST) // C


class Signal:

    def __init__(self, ctx, nc, name):
        self.sem = ctx.enter_context(nc.semaphore(name))
        self.base = 0

    def at(self, n):
        return n + self.base


class Weights:

    AHEAD = 2

    def __init__(self, ctx, nc, sources):
        self.nc = nc
        self.raw = ctx.enter_context(nc.sbuf_tensor("weights_raw", [P, RING, UNIT], F32))
        self.hi = [ctx.enter_context(nc.sbuf_tensor(f"weights_hi{k}", [P, C, P], F32R)) for k in range(RING)]
        self.lo = [ctx.enter_context(nc.sbuf_tensor(f"weights_lo{k}", [P, C, P], F32R)) for k in range(RING)]
        self.loaded = [Signal(ctx, nc, f"weights_loaded{k}") for k in range(RING)]
        self.hi_ready = Signal(ctx, nc, "weights_hi_ready")
        self.lo_ready = Signal(ctx, nc, "weights_lo_ready")
        self.unit_done = Signal(ctx, nc, "unit_done")
        self.sources = sources
        self.total = sum(n for _, n in sources)
        self.u0 = 0

    def source(self, v):
        for dram, n in self.sources:
            if v < n:
                return dram, v
            v -= n
        raise IndexError

    def done(self, k):
        return k + (self.u0 + RING + 1)

    def load(self, sp, k, slot, dram, index, free=True):
        if free:
            sp.wait_ge(self.lo_ready.sem, k + (self.u0 + 1 - RING))
        sp.dma_start(self.raw[:, slot, :], dram[index]).then_inc(self.loaded[slot].sem, 16)

    def load_first(self, sp, units):
        for v in units:
            dram, index = self.source(v)
            self.load(sp, v, v, dram, index, free=False)

    def load_stage(self, sp, n):
        first, last = self.u0 + RING, min(self.u0 + RING + n, self.total)
        v = first
        while v < last:
            dram, index = self.source(v)
            run = min(last - v, dram.shape[0] - index)
            if run >= 2 * RING:
                with sp.Fori(0, run // RING) as i:
                    for k in range(RING):
                        self.load(sp, i * RING + (v + k - self.u0), (v + k) % RING, dram, i * RING + (index + k))
                run -= run % RING
            else:
                for k in range(run):
                    self.load(sp, v + k - self.u0, (v + k) % RING, dram, index + k)
            v += run

    def hi_step(self, act, loop, k, per):
        slot = (self.u0 + k) % RING
        turn = (self.u0 + k - slot) // RING + 1
        act.wait_ge(self.loaded[slot].sem, 16 * turn if loop is None else loop * (16 * per // RING) + 16 * turn)
        act.wait_ge(self.unit_done.sem, self.u0 + k + 1 if loop is None else loop * per + (self.u0 + k + 1))
        self.nc.scalar.activation(self.hi[slot][:, :, :], self.raw[:, slot, :].rearrange("p (c n) -> p c n", c=C),
                                  ACT.Copy).then_inc(self.hi_ready.sem, 1)

    def lo_step(self, eng, loop, k, per):
        slot = (self.u0 + k) % RING
        eng.wait_ge(self.hi_ready.sem, self.u0 + k + 1 if loop is None else loop * per + (self.u0 + k + 1))
        eng.tensor_tensor(self.lo[slot][:, :, :], self.raw[:, slot, :].rearrange("p (c n) -> p c n", c=C),
                                     self.hi[slot][:, :, :].bitcast(F32), ALU.subtract).then_inc(self.lo_ready.sem, 1)

    def multiply_chunk(self, pe, loop, k, per, out, acts, c):
        slot = (self.u0 + k) % RING
        if c == 0:
            pe.wait_ge(self.lo_ready.sem, loop * per + (self.u0 + k + 1))
        for n, (w, a) in enumerate(((self.hi, acts[0]), (self.hi, acts[1]), (self.lo, acts[0]))):
            mm = self.nc.tensor.matmul(out, w[slot][:, c, :], a[:, c, :], start=c == 0 and n == 0, stop=c == C - 1 and n == 2)
        return mm

    def multiply(self, pe, loop, k, per, out, acts, first=True, last=True, chunks=range(C), tokens=T, before_chunk=None):
        slot = (self.u0 + k) % RING
        pe.wait_ge(self.lo_ready.sem, self.u0 + k + 1 if loop is None else loop * per + (self.u0 + k + 1))
        hi, lo = acts
        n = 0
        for j, c in enumerate(chunks):
            if before_chunk:
                before_chunk(c)
            for w, a in ((self.hi, hi), (self.hi, lo), (self.lo, hi)):
                n += 1
                mm = self.nc.tensor.matmul(out, w[slot][:, c, :], a[:, j, 0:tokens],
                                           start=first and n == 1, stop=last and n == 3 * len(chunks))
        return mm


def build_program(nc, aps, out_t, stop=99):
    (x_t, norm_gains, rope_tables, swap, ident_in, distance, lam_in, diff_gain, ret_decay, ret_gain, keys_t, iota_in,
     conv_taps, gate_bias_in, mem_t) = (aps[n] for n in (
         "x_t", "norm_gains", "rope_tables", "swap", "ident_in", "distance", "lam_in", "diff_gain", "ret_decay", "ret_gain",
         "keys_t", "iota_in", "conv_taps", "gate_bias_in", "mem_t"))
    rwkv = {k[5:]: v for k, v in aps.items() if k.startswith("rwkv_")}
    units = [(v, v.shape[0]) for k, v in aps.items() if k.startswith("u_")]
    ctx = ExitStack()
    with ctx:
        uses = {}

        def fresh(name):
            uses[name] = uses.get(name, 0) + 1
            return name if uses[name] == 1 else f"{name}_{uses[name]}"

        def sb(name, shape, dt=F32, c=None):
            name = fresh(name)
            return (c or ctx).enter_context(nc.sbuf_tensor(name, shape, dt))

        def sig(name):
            return Signal(ctx, nc, name)

        weights = Weights(ctx, nc, units)
        gates_dram = nc.dram_tensor("gates_dram", [GBLOCKS, P, N_KEYS * GT], F32).ap()
        x = sb("x", [P, C, T])
        gains = sb("gains", [P, 8, C])
        ident = sb("ident", [P, P])
        ones = sb("ones", [P, P])
        psum = ctx.enter_context(nc.psum_tensor("psum", [P, 8, T], F32))
        consts_loaded = sig("consts_loaded")
        norm_sq, norm_acc, norm_sum, norm_log, norm_rstd, norm_y = (sig(n) for n in (
            "norm_squares_ready", "norm_squares_summed", "norm_sum_ready", "norm_log_ready", "norm_rstd_ready", "norm_scaled_ready"))
        rstd = sb("rstd", [P, T])

        def add_squares(sq, acc, c, buffers):
            nc.vector.wait_ge(norm_sq.sem, norm_sq.at(c + 1))
            if c == 0:
                return nc.vector.tensor_copy(acc[:, 0, :], sq[:, 0, :]).then_inc(norm_acc.sem, 1)
            nc.vector.wait_ge(norm_acc.sem, norm_acc.at(c))
            return nc.vector.tensor_tensor(acc[:, c % 2, :], acc[:, (c - 1) % 2, :], sq[:, c % buffers, :], ALU.add).then_inc(norm_acc.sem, 1)

        def sum_squares(pe, acc, width=T):
            pe.wait_ge(norm_acc.sem, norm_acc.at(C))
            nc.tensor.matmul(psum[:, 7, 0:width], ones[:], acc[:, 1, :], start=True, stop=True).then_inc(norm_sum.sem, 1)

        def root(act, width=T):
            act.wait_ge(norm_sum.sem, norm_sum.at(1))
            r = rstd[:, 0:width]
            nc.scalar.activation(r, psum[:, 7, 0:width], ACT.Ln, bias=eps_ap[:, 0:1], scale=1.0 / D).then_inc(norm_log.sem, 1)
            act.wait_ge(norm_log.sem, norm_log.at(1))
            nc.scalar.activation(r, r, ACT.Exp, scale=-0.5).then_inc(norm_rstd.sem, 1)

        def norm_done():
            for s in (norm_sq, norm_acc):
                s.base += C
            for s in (norm_sum, norm_log, norm_rstd):
                s.base += 1

        def scale_x(gain, store=None):
            with nc.Block() as block:
                if store:
                    @block.sync
                    def _(sp):
                        for c in range(0, C, 2):
                            sp.wait_ge(norm_y.sem, norm_y.at(c + 2))
                            sp.dma_start(store[:, c:c + 2, :], x[:, c:c + 2, :]).then_inc(output_stored.sem, 16)
                        sp.wait_ge(output_stored.sem, 16 * C // 2)

                @block.vector
                def _(dve):
                    for c in range(C):
                        nc.vector.scalar_tensor_tensor(x[:, c, :], x[:, c, :], gains[:, gain, c:c + 1], rstd[:],
                                                       ALU.mult, ALU.mult).then_inc(norm_y.sem, 1)
            norm_y.base += C

        pre_hi, pre_lo, part_product = sig("operand_hi_ready"), sig("operand_lo_ready"), sig("operand_product_ready")
        output_stored = sig("output_stored")

        class Norm:

            def __init__(self, src, gain, hi, lo, width, local, arrived=None, parts_before=0, scale_first=None):
                self.parts_before = parts_before
                self.scale_first = scale_first
                self.src, self.gain, self.hi, self.lo, self.width, self.arrived = src, gain, hi, lo, width, arrived
                self.sq = sb("operand_squares", [P, 4, width], F32, local)
                self.acc = sb("operand_sums", [P, 2, width], F32, local)

            def there(self, eng, c):
                if self.arrived:
                    self.arrived(eng, c)
                if self.scale_first is not None:
                    eng.wait_ge(norm_y.sem, norm_y.at(c + 1))

            def hi_step(self, act, c):
                self.there(act, c)
                nc.scalar.activation(self.hi[:, c, :], self.src[:, c, 0:self.width], ACT.Copy,
                                     scale=gains[:, self.gain, c:c + 1]).then_inc(pre_hi.sem, 1)

            def square(self, act, c):
                if c >= 4:
                    act.wait_ge(norm_acc.sem, norm_acc.at(c - 3))
                nc.scalar.activation(self.sq[:, c % 4, :], self.src[:, c, 0:self.width], ACT.Square).then_inc(norm_sq.sem, 1)

            def lo_step(self, dve, c):
                self.there(dve, c)
                dve.wait_ge(pre_hi.sem, pre_hi.at(self.parts_before + c + 1))
                nc.vector.scalar_tensor_tensor(self.lo[:, c, :], self.src[:, c, 0:self.width], gains[:, self.gain, c:c + 1],
                                               self.hi[:, c, :].bitcast(F32), ALU.mult, ALU.subtract).then_inc(pre_lo.sem, 1)

            def scalar_hi(self, act):
                for c in range(C):
                    self.hi_step(act, c)

            def scalar_rstd(self, act):
                for c in range(C):
                    self.square(act, c)
                root(act, self.width)

            def vector(self, dve):
                def scale(c):
                    nc.vector.scalar_tensor_tensor(self.src[:, c, :], self.src[:, c, :], gains[:, self.scale_first, c:c + 1], rstd[:],
                                                   ALU.mult, ALU.mult).then_inc(norm_y.sem, 1)
                if self.scale_first is not None:
                    scale(0)
                for c in range(C):
                    if self.scale_first is not None and c + 1 < C:
                        scale(c + 1)
                    self.lo_step(dve, c)

            def vector_rstd(self, dve):
                for c in range(C):
                    add_squares(self.sq, self.acc, c, 4)
                dve.wait_ge(norm_rstd.sem, norm_rstd.at(1))

            def tensor(self, pe):
                sum_squares(pe, self.acc, self.width)

            def chunk_there(self, pe, c):
                pe.wait_ge(pre_lo.sem, pre_lo.at(c + 1))

            def end(self):
                for s in (pre_hi, pre_lo):
                    s.base += C
                if self.scale_first is not None:
                    norm_y.base += C
                norm_done()

        class Parts:

            def __init__(self, parts, hi, lo, more=()):
                self.parts, self.hi, self.lo, self.more = parts, hi, lo, more
                self.times = [part for part in parts if part[3] is not None]
                self.place = {part[0]: n for n, part in enumerate(parts)}

            def scalar_hi(self, act):
                for c, src, gain, other in self.parts:
                    if other is not None:
                        act.wait_ge(part_product.sem, part_product.at([part[0] for part in self.times].index(c) + 1))
                    nc.scalar.activation(self.hi[:, c, :], src, ACT.Copy, scale=gain).then_inc(pre_hi.sem, 1)
                for hi, lo, src in self.more:
                    nc.scalar.activation(hi, src, ACT.Copy).then_inc(pre_hi.sem, 1)

            def scalar_rstd(self, act):
                pass

            def vector(self, dve):
                for c, src, gain, other in self.times:
                    nc.vector.tensor_tensor(src, src, other, ALU.mult).then_inc(part_product.sem, 1)
                for n, (c, src, gain, other) in enumerate(self.parts):
                    dve.wait_ge(pre_hi.sem, pre_hi.at(n + 1))
                    nc.vector.scalar_tensor_tensor(self.lo[:, c, :], src, gain, self.hi[:, c, :].bitcast(F32),
                                                   ALU.mult, ALU.subtract).then_inc(pre_lo.sem, 1)
                for n, (hi, lo, src) in enumerate(self.more):
                    dve.wait_ge(pre_hi.sem, pre_hi.at(len(self.parts) + n + 1))
                    nc.vector.tensor_tensor(lo, src, hi.bitcast(F32), ALU.subtract).then_inc(pre_lo.sem, 1)

            def vector_rstd(self, dve):
                pass

            def tensor(self, pe):
                pass

            def chunk_there(self, pe, c):
                if c in self.place:
                    pe.wait_ge(pre_lo.sem, pre_lo.at(self.place[c] + 1))

            def end(self):
                pre_hi.base += len(self.parts) + len(self.more)
                pre_lo.base += len(self.parts) + len(self.more)
                part_product.base += len(self.times)

        out_free = sig("product_read")

        def linear(n, acts, evacuate, engine, tokens=T, prologue=False, norm=None, parts=None, more=(), before=None, then=None, along=None):
            w = weights
            head = RING if norm or parts else 0
            loops = 0 if then or along else (n - head) // RING
            rest = range(head + loops * RING, n)
            u0, base = w.u0, out_free.base
            split_until = w.total - w.AHEAD - u0

            def bank(k):
                return (u0 + k) % 4

            with ExitStack() as local, nc.Block() as block:
                pre = None
                if norm:
                    pre = Norm(norm[0], norm[1], acts[0], acts[1], tokens, local, before and before.arrived,
                               scale_first=norm[2] if len(norm) > 2 else None)
                post = Norm(x, then[0], then[1], then[2], T, local, parts_before=len(parts or ())) if then else None
                if parts:
                    pre = Parts(parts, acts[0], acts[1], more)

                @block.sync
                def _(sp):
                    if before:
                        before(sp)
                    w.load_stage(sp, n)

                def evac(eng, loop, k):
                    eng.wait_ge(w.unit_done.sem, w.done(k) if loop is None else loop * RING + w.done(k))
                    evacuate(loop, k, psum[:, bank(k), 0:tokens]).then_inc(out_free.sem, 1)

                def scalar_post(k):
                    nc.scalar.wait_ge(out_free.sem, base + RING + k + 1)
                    post.hi_step(nc.scalar, k)
                    post.square(nc.scalar, k)

                def vector_post(k):
                    post.lo_step(nc.vector, k)
                    add_squares(post.sq, post.acc, k, 4)

                def run(eng, step, mine, make, ready, after=None):
                    if prologue:
                        step(eng, None, 0, RING)
                    if pre:
                        make(eng)
                        if prologue:
                            step(eng, None, 1, RING)
                        step(eng, None, 2, RING)
                        step(eng, None, 3, RING)
                        ready(eng)
                        for k in range(RING):
                            if mine:
                                evac(eng, None, k)
                            if k >= 2:
                                step(eng, None, k + 2, RING)
                            if after and k:
                                after(k - 1)
                            if along:
                                along[eng is nc.vector](k)
                    if loops:
                        with eng.Fori(0, loops) as i:
                            for k in range(RING):
                                step(eng, i, head + k + w.AHEAD, RING)
                                if mine:
                                    evac(eng, i, head + k)
                    for k in rest:
                        if k < split_until:
                            step(eng, None, k + w.AHEAD, RING)
                        if mine:
                            evac(eng, None, k)
                        if after and k:
                            after(k - 1)
                        if along:
                            along[eng is nc.vector](k)
                    if after:
                        after(n - 1)

                @block.scalar
                def _(act):
                    run(act, w.hi_step, engine == "scalar", pre and pre.scalar_hi, pre and pre.scalar_rstd, then and scalar_post)
                    if then:
                        root(act)

                @block.vector
                def _(dve):
                    run(dve, w.lo_step, engine == "vector", pre and pre.vector, pre and pre.vector_rstd, then and vector_post)

                if along:
                    @block.gpsimd
                    def _(pool):
                        along[2](pool, base + RING)

                if before and before.arrived:
                    @block.gpsimd
                    def _(pool):
                        before.arrived(pool, None)

                @block.tensor
                def _(pe):
                    def chunk_there(c):
                        pre.chunk_there(pe, c)

                    def product(loop, k, before_chunk=None):
                        pe.wait_ge(out_free.sem, base + k + 1 if loop is None else loop * RING + (base + k + 1))
                        w.multiply(pe, loop, k, RING, psum[:, bank(k), 0:tokens], acts,
                                   tokens=tokens, before_chunk=before_chunk).then_inc(w.unit_done.sem, 1)
                    if prologue:
                        pe.sem_inc(w.unit_done.sem, RING)
                        pe.sem_inc(out_free.sem, RING)
                    if pre:
                        for k in range(RING):
                            product(None, k, chunk_there if k == 0 else None)
                            if k == 2:
                                pre.tensor(pe)
                    if loops:
                        with pe.Fori(0, loops) as i:
                            for k in range(RING):
                                product(i, head + k)
                    for k in rest:
                        product(None, k)
                    if then:
                        post.tensor(pe)
            w.u0 += n
            out_free.base += n
            if pre:
                pre.end()
            if then:
                post.end()

        def scaled(dst, tokens=T):
            return lambda loop, k, bank: nc.vector.tensor_tensor(dst(at(loop, k)), bank, rstd[:, 0:tokens], ALU.mult)

        def at(loop, k):
            return k if loop is None else loop * RING + k

        eps_ap = sb("eps", [P, 1])

        X_PIECES = (0, 2, 4)
        x_loaded = [sig(f"x_loaded{k}") for k in range(len(X_PIECES))]
        gains_loaded = sig("gains_loaded")

        def load_start(sp):
            sp.dma_start(gains[:, :, :], norm_gains).then_inc(gains_loaded.sem, 16)
            for k, c in enumerate(X_PIECES):
                end = (X_PIECES + (C,))[k + 1]
                sp.dma_start(x[:, c:end, :], x_t[:, c:end, :]).then_inc(x_loaded[k].sem, 16)
                if k == 0:
                    weights.load_first(sp, [0])
            weights.load_first(sp, range(1, RING))
            sp.dma_start(ident[:], ident_in).then_inc(consts_loaded.sem, 16)

        def start_arrived(eng, c):
            if c is None:
                eng.wait_ge(consts_loaded.sem, 16)
                return
            if c == 0:
                eng.wait_ge(gains_loaded.sem, 16)
            if c in X_PIECES:
                eng.wait_ge(x_loaded[X_PIECES.index(c)].sem, 16)
        load_start.arrived = start_arrived

        ones_set = sig("ones_set")
        with nc.Block() as block:
            @block.gpsimd
            def _(pool):
                nc.gpsimd.memset(ones[:], 1.0).then_inc(ones_set.sem, 1)
                nc.gpsimd.memset(eps_ap[:], EPS).then_inc(ones_set.sem, 1)

        mix_stack = ExitStack()
        ctx.enter_context(mix_stack)
        proj = sb("projections", [P, IN_SLABS, T], F32, mix_stack)
        act_stack = ExitStack()
        act_hi = sb("act_hi_a", [P, C, T], F32R, act_stack)
        act_lo = sb("act_lo_a", [P, C, T], F32R, act_stack)
        linear(IN_SLABS, (act_hi, act_lo), scaled(lambda n: proj[:, n, :]), "vector", prologue=True, norm=(x, 0), before=load_start)
        act_stack.close()

        split_hi_ready = sig("split_hi_ready")
        gn_mean = sig("head_mean_ready")
        gn_centred = sig("head_centred")
        gn_square = sig("head_square_ready")
        gn_var = sig("head_variance_ready")
        gn_floor = sig("head_variance_floored")
        gn_log = sig("head_log_ready")
        gn_rstd = sig("head_rstd_ready")

        gn_out = sig("head_scaled")

        def head_norm(src, average, eps, center, floor=None, products=None, finish=None, split_to=None):
            with ExitStack() as local, nc.Block() as block:
                sq = sb("head_squares", [P, 2, T], F32, local)
                rstd = sb("head_rstd", [P, 4, T], F32, local)

                @block.tensor
                def _(pe):
                    if center:
                        for j in range(4):
                            nc.tensor.matmul(psum[:, j, :], average, src[:, j, :], start=True, stop=True).then_inc(gn_mean.sem, 1)
                    if products:
                        products(pe)
                    for j in range(4):
                        pe.wait_ge(gn_square.sem, gn_square.at(j + 1))
                        nc.tensor.matmul(psum[:, j, :], average, sq[:, j % 2, :], start=True, stop=True).then_inc(gn_var.sem, 1)

                @block.scalar
                def _(act):
                    for j in range(4):
                        if center:
                            act.wait_ge(gn_centred.sem, gn_centred.at(j + 1))
                        if j >= 2:
                            act.wait_ge(gn_var.sem, gn_var.at(j - 1))
                        nc.scalar.activation(sq[:, j % 2, :], src[:, j, :], ACT.Square).then_inc(gn_square.sem, 1)
                    for j in range(4):
                        if floor is not None:
                            act.wait_ge(gn_floor.sem, gn_floor.at(j + 1))
                        else:
                            act.wait_ge(gn_var.sem, gn_var.at(j + 1))
                        source = rstd[:, j, :] if floor is not None else psum[:, j, :]
                        nc.scalar.activation(rstd[:, j, :], source, ACT.Ln, bias=eps, scale=1.0).then_inc(gn_log.sem, 1)
                    for j in range(4):
                        act.wait_ge(gn_log.sem, gn_log.at(j + 1))
                        nc.scalar.activation(rstd[:, j, :], rstd[:, j, :], ACT.Exp, scale=-0.5).then_inc(gn_rstd.sem, 1)
                    if split_to:
                        for j in range(4):
                            act.wait_ge(gn_out.sem, gn_out.at(j + 1))
                            nc.scalar.activation(split_to[1][:, j, :], src[:, j, :], ACT.Copy, scale=split_to[0]).then_inc(split_hi_ready.sem, 1)

                @block.vector
                def _(dve):
                    if center:
                        for j in range(4):
                            dve.wait_ge(gn_mean.sem, gn_mean.at(j + 1))
                            nc.vector.tensor_tensor(src[:, j, :], src[:, j, :], psum[:, j, :], ALU.subtract).then_inc(gn_centred.sem, 1)
                    if floor is not None:
                        for j in range(4):
                            dve.wait_ge(gn_var.sem, gn_var.at(j + 1))
                            nc.vector.tensor_scalar(rstd[:, j, :], psum[:, j, :], floor, None, ALU.max).then_inc(gn_floor.sem, 1)
                    for j in range(4):
                        dve.wait_ge(gn_rstd.sem, gn_rstd.at(j + 1))
                        nc.vector.tensor_tensor(src[:, j, :], src[:, j, :], rstd[:, j, :], ALU.mult).then_inc(gn_out.sem, 1)
                    if finish:
                        finish(dve)
                    if split_to:
                        for j in range(4):
                            dve.wait_ge(split_hi_ready.sem, split_hi_ready.at(j + 1))
                            nc.vector.scalar_tensor_tensor(split_to[2][:, j, :], src[:, j, :], split_to[0], split_to[1][:, j, :].bitcast(F32),
                                                           ALU.mult, ALU.subtract)
            if split_to:
                split_hi_ready.base += 4
            for s, used in ((gn_mean, center), (gn_centred, center), (gn_square, True), (gn_var, True), (gn_floor, floor is not None),
                            (gn_log, True), (gn_rstd, True), (gn_out, True)):
                s.base += 4 * used

        mix_hi = sb("mix_hi", [P, C, T], F32R, mix_stack)
        mix_lo = sb("mix_lo", [P, C, T], F32R, mix_stack)
        v_tok = sb("values_by_token", [P, 2 * HEADS, T], F32, mix_stack)
        average128 = sb("average128", [P, P], F32, mix_stack)
        small = sb("attention_scalars", [P, 64], F32, mix_stack)
        neg_lam, gain_d, gain_r, lgf = small[:, 0:1], small[:, 4:5], small[:, 8:12], small[:, 16:24]
        lam_v = sb("lambda_vectors", [P, 4, 64], F32, mix_stack)
        lam_loaded = sig("attention_scalars_loaded")
        tables_loaded = sig("tables_loaded")
        rope_swapped, rope_cos, rope_sin, rope_done = (sig(n) for n in ("rope_swapped", "rope_cos", "rope_sin", "rope_done"))
        v_turned = sig("values_transposed")
        v_copied = sig("values_copied")
        lam_step = sig("lambda_step")
        lam_exp = sig("lambda_exp_ready")
        rotary = [(n, 0) for n in range(DQ, DV)] + [(n, 1) for n in range(RQ, RV)]
        values = list(range(DV, DV + HEADS)) + list(range(RV, RV + HEADS))
        with ExitStack() as local, nc.Block() as block:
            tables = sb("rope_tables_sb", [P, 4, T], F32, local)
            swaps = sb("rope_swaps", [P, 2, P], F32, local)
            by_cos = sb("rope_by_cos", [P, 2, T], F32, local)
            by_sin = sb("rope_by_sin", [P, 2, T], F32, local)

            @block.sync
            def _(sp):
                sp.dma_start(tables[:, :, :], rope_tables).then_inc(tables_loaded.sem, 16)
                sp.dma_start(swaps[:, :, :], swap).then_inc(tables_loaded.sem, 16)
                sp.dma_start(lam_v[:, :, :], lam_in).then_inc(lam_loaded.sem, 16)
                sp.dma_start(small[:, 4:5], diff_gain).then_inc(lam_loaded.sem, 16)
                sp.dma_start(small[:, 8:12], ret_gain).then_inc(lam_loaded.sem, 16)
                sp.dma_start(small[:, 16:24], ret_decay).then_inc(lam_loaded.sem, 16)

            @block.tensor
            def _(pe):
                for j, n in enumerate(values):
                    if j >= 2:
                        pe.wait_ge(v_copied.sem, j - 1)
                    for tile in range(TT):
                        mm = nc.tensor.transpose(psum[:, 4 + j % 2, tile * P:(tile + 1) * P], proj[:, n, tile * P:(tile + 1) * P], ident[:])
                    mm.then_inc(v_turned.sem, 1)
                pe.wait_ge(tables_loaded.sem, 32)
                for j, (n, kind) in enumerate(rotary):
                    if j >= 2:
                        pe.wait_ge(rope_sin.sem, j - 1)
                    nc.tensor.matmul(psum[:, j % 2, :], swaps[:, kind, :], proj[:, n, :], start=True, stop=True).then_inc(rope_swapped.sem, 1)

            @block.scalar
            def _(act):
                for j in range(len(values)):
                    act.wait_ge(v_turned.sem, j + 1)
                    nc.scalar.activation(v_tok[:, j, :], psum[:, 4 + j % 2, :], ACT.Copy).then_inc(v_copied.sem, 1)
                act.wait_ge(lam_loaded.sem, 64)
                act.wait_ge(lam_step.sem, 2)
                nc.scalar.activation(small[:, 2:4], small[:, 2:4], ACT.Exp).then_inc(lam_exp.sem, 1)
                nc.scalar.activation(lgf, lgf, ACT.Exp).then_inc(lam_exp.sem, 1)

            @block.gpsimd
            def _(pool):
                nc.gpsimd.memset(average128[:], 1.0 / P)
                pool.wait_ge(tables_loaded.sem, 32)
                for j, (n, kind) in enumerate(rotary):
                    if j >= 2:
                        pool.wait_ge(rope_done.sem, j - 1)
                    nc.gpsimd.tensor_tensor(by_cos[:, j % 2, :], proj[:, n, :], tables[:, 2 * kind, :], ALU.mult).then_inc(rope_cos.sem, 1)

            @block.vector
            def _(dve):
                for j, (n, kind) in enumerate(rotary):
                    dve.wait_ge(rope_swapped.sem, j + 1)
                    if j == 0:
                        dve.wait_ge(tables_loaded.sem, 32)
                    if j >= 2:
                        dve.wait_ge(rope_done.sem, j - 1)
                    nc.vector.tensor_tensor(by_sin[:, j % 2, :], psum[:, j % 2, :], tables[:, 2 * kind + 1, :], ALU.mult).then_inc(rope_sin.sem, 1)
                    dve.wait_ge(rope_cos.sem, j + 1)
                    dve.wait_ge(rope_sin.sem, j + 1)
                    nc.vector.tensor_tensor(proj[:, n, :], by_cos[:, j % 2, :], by_sin[:, j % 2, :], ALU.add).then_inc(rope_done.sem, 1)
                dve.wait_ge(lam_loaded.sem, 64)
                nc.vector.tensor_tensor(lam_v[:, 0::2, :], lam_v[:, 0::2, :], lam_v[:, 1::2, :], ALU.mult).then_inc(lam_step.sem, 1)
                dve.wait_ge(lam_step.sem, 1)
                nc.vector.tensor_reduce(small[:, 2:4], lam_v[:, 0::2, :], AX.X, ALU.add).then_inc(lam_step.sem, 1)
                dve.wait_ge(lam_exp.sem, 2)
                nc.vector.tensor_tensor(neg_lam, small[:, 3:4], small[:, 2:3], ALU.subtract).then_inc(lam_step.sem, 1)
                dve.wait_ge(lam_step.sem, 3)
                nc.vector.tensor_scalar(neg_lam, neg_lam, -LAMBDA_INIT, None, ALU.add)
                nc.vector.tensor_scalar(gain_d, gain_d, 1.0 - LAMBDA_INIT, None, ALU.mult)
                nc.vector.tensor_scalar(lgf, lgf, -1.0, None, ALU.mult)

        scored, maxed, neg_maxed, exped = (sig(n) for n in ("diff_scores_ready", "diff_max_ready", "diff_neg_max_ready", "diff_exp_ready"))
        inv_ready, scaled0, combined = (sig(n) for n in ("diff_inverse_sum_ready", "diff_first_map_scaled", "diff_maps_combined"))
        turned, turned_read, mixed, mixed_read = (sig(n) for n in ("diff_map_transposed", "diff_map_copied", "diff_out_ready", "diff_out_copied"))
        heads_out = sb("diff_heads_out", [P, HEADS, T], F32, mix_stack)
        scale = DIFF_QK ** -0.5
        steps = HEADS * TT
        with ExitStack() as local, nc.Block() as block:
            probs = sb("diff_probs", [P, 2, 2, T], F32, local)
            amap = sb("diff_map", [P, 2, T], F32, local)
            amap_t = sb("diff_map_t", [P, 2, TT, T], F32, local)
            stats = sb("diff_stats", [P, steps, 8], F32, local)

            @block.tensor
            def _(pe):
                def scores(it):
                    h, q = divmod(it, TT)
                    if it >= 3:
                        pe.wait_ge(exped.sem, 2 * (it - 2))
                    for m in range(2):
                        rows = slice(64 * m, 64 * m + 64)
                        nc.tensor.matmul(psum[:, 2 * (it % 3) + m, :], proj[rows, DQ + h, q * P:(q + 1) * P],
                                         proj[rows, DK + h, :], start=True, stop=True).then_inc(scored.sem, 1)
                scores(0)
                scores(1)
                for it in range(steps):
                    h, q = divmod(it, TT)
                    if it + 2 < steps:
                        scores(it + 2)
                    pe.wait_ge(combined.sem, it + 1)
                    if it >= 1:
                        pe.wait_ge(turned_read.sem, it)
                    for kt in range(TT):
                        mm = nc.tensor.transpose(psum[:, 6, kt * P:(kt + 1) * P], amap[:, it % 2, kt * P:(kt + 1) * P], ident[:])
                    mm.then_inc(turned.sem, 1)
                    if q == TT - 1:
                        pe.wait_ge(turned_read.sem, it + 1)
                        if h >= 1:
                            pe.wait_ge(mixed_read.sem, h)
                        for kt in range(TT):
                            mm = nc.tensor.matmul(psum[:, 7, :], v_tok[:, h, kt * P:(kt + 1) * P],
                                                  amap_t[:, h % 2, kt, :], start=kt == 0, stop=kt == TT - 1)
                        mm.then_inc(mixed.sem, 1)

            @block.scalar
            def _(act):
                def exps(it):
                    act.wait_ge(neg_maxed.sem, it + 1)
                    if it >= 2:
                        act.wait_ge(combined.sem, it - 1)
                    for m in range(2):
                        nc.scalar.activation(probs[:, it % 2, m, :], psum[:, 2 * (it % 3) + m, :], ACT.Exp, bias=stats[:, it, 2 + m:3 + m],
                                             scale=scale, accum_out=stats[:, it, 4 + m:5 + m]).then_inc(exped.sem, 1)
                exps(0)
                for it in range(steps):
                    h, q = divmod(it, TT)
                    if it + 1 < steps:
                        exps(it + 1)
                    act.wait_ge(turned.sem, it + 1)
                    if h >= 2:
                        act.wait_ge(mixed.sem, h - 1)
                    nc.scalar.activation(amap_t[:, h % 2, :, q * P:(q + 1) * P], psum[:, 6, :].rearrange("p (k q) -> p k q", k=TT),
                                         ACT.Copy).then_inc(turned_read.sem, 1)
                    if q == TT - 1:
                        act.wait_ge(mixed.sem, h + 1)
                        nc.scalar.activation(heads_out[:, h, :], psum[:, 7, :], ACT.Copy).then_inc(mixed_read.sem, 1)

            @block.vector
            def _(dve):
                def maxima(it):
                    dve.wait_ge(scored.sem, 2 * (it + 1))
                    nc.vector.tensor_reduce(stats[:, it, 0:2], psum[:, 2 * (it % 3):2 * (it % 3) + 2, :], AX.X, ALU.max).then_inc(maxed.sem, 1)
                    dve.wait_ge(maxed.sem, it + 1)
                    nc.vector.tensor_scalar(stats[:, it, 2:4], stats[:, it, 0:2], -scale, None, ALU.mult).then_inc(neg_maxed.sem, 1)
                maxima(0)
                maxima(1)
                for it in range(steps):
                    dve.wait_ge(exped.sem, 2 * (it + 1))
                    nc.vector.reciprocal(stats[:, it, 6:8], stats[:, it, 4:6]).then_inc(inv_ready.sem, 1)
                    dve.wait_ge(inv_ready.sem, 2 * it + 1)
                    nc.vector.tensor_tensor(stats[:, it, 7:8], stats[:, it, 7:8], neg_lam, ALU.mult).then_inc(inv_ready.sem, 1)
                    nc.vector.tensor_scalar(probs[:, it % 2, 0, :], probs[:, it % 2, 0, :], stats[:, it, 6:7], None, ALU.mult).then_inc(scaled0.sem, 1)
                    dve.wait_ge(inv_ready.sem, 2 * it + 2)
                    dve.wait_ge(scaled0.sem, it + 1)
                    if it >= 2:
                        dve.wait_ge(turned.sem, it - 1)
                    nc.vector.scalar_tensor_tensor(amap[:, it % 2, :], probs[:, it % 2, 1, :], stats[:, it, 7:8], probs[:, it % 2, 0, :],
                                                   ALU.mult, ALU.add).then_inc(combined.sem, 1)
                    if it + 2 < steps:
                        maxima(it + 2)

        head_norm(heads_out, average128[:], eps_ap[:, 0:1], center=False, split_to=(gain_d, mix_hi, mix_lo))

        dist_loaded, arg0_ready, arg_ready, decay_ready = (sig(n) for n in ("distances_loaded", "decay_half_ready", "decay_log_ready", "decay_ready"))
        ret_scored, ret_decayed, ret_mixed, ret_read = (sig(n) for n in ("ret_scores_ready", "ret_scores_decayed", "ret_out_ready", "ret_out_copied"))
        SPAN = T + (TT - 1) * P
        with ExitStack() as local, nc.Block() as block:
            dist = sb("ret_distances", [P, 2, SPAN], F32, local)
            args = sb("ret_decay_log", [P, 2, SPAN], F32, local)
            decay = sb("ret_decay", [P, 2, SPAN], F32, local)
            weighed = sb("ret_scores", [P, 4, T], F32, local)

            @block.sync
            def _(sp):
                sp.dma_start(dist[:, :, :], distance).then_inc(dist_loaded.sem, 16)

            @block.tensor
            def _(pe):
                def scores(it):
                    h, kt = divmod(it, TT)
                    rows = slice(64 * (h % 2), 64 * (h % 2) + 64)
                    if it >= 4:
                        pe.wait_ge(ret_decayed.sem, it - 3)
                    nc.tensor.matmul(psum[:, it % 4, :], proj[rows, RK + h // 2, kt * P:(kt + 1) * P], proj[rows, RQ + h // 2, :],
                                     start=True, stop=True).then_inc(ret_scored.sem, 1)
                scores(0)
                scores(1)
                for it in range(steps):
                    h, kt = divmod(it, TT)
                    if it + 2 < steps:
                        scores(it + 2)
                    pe.wait_ge(ret_decayed.sem, it + 1)
                    if kt == 0 and h >= 2:
                        pe.wait_ge(ret_read.sem, h - 1)
                    nc.tensor.matmul(psum[:, 4 + h % 2, :], v_tok[:, HEADS + h, kt * P:(kt + 1) * P], weighed[:, it % 4, :],
                                     start=kt == 0, stop=kt == TT - 1).then_inc(ret_mixed.sem, 1)

            @block.scalar
            def _(act):
                for h in range(HEADS):
                    act.wait_ge(arg_ready.sem, h + 1)
                    if h >= 2:
                        act.wait_ge(ret_decayed.sem, TT * (h - 1))
                    nc.scalar.activation(decay[:, h % 2, :], args[:, h % 2, :], ACT.Exp).then_inc(decay_ready.sem, 1)
                    if h >= 1:
                        act.wait_ge(ret_mixed.sem, TT * h)
                        nc.scalar.activation(heads_out[:, h - 1, :], psum[:, 4 + (h - 1) % 2, :], ACT.Copy).then_inc(ret_read.sem, 1)
                act.wait_ge(ret_mixed.sem, TT * HEADS)
                nc.scalar.activation(heads_out[:, HEADS - 1, :], psum[:, 4 + (HEADS - 1) % 2, :], ACT.Copy).then_inc(ret_read.sem, 1)
                for h in range(HEADS):
                    nc.scalar.activation(proj[:, RG + h, :], proj[:, RG + h, :], ACT.Silu)

            @block.vector
            def _(dve):
                dve.wait_ge(dist_loaded.sem, 16)

                def log_decay(h):
                    if h >= 2:
                        dve.wait_ge(decay_ready.sem, h - 1)
                    nc.vector.tensor_scalar(args[:, h % 2, :], dist[:, 0, :], lgf[:, h:h + 1], None, ALU.mult).then_inc(arg0_ready.sem, 1)
                    dve.wait_ge(arg0_ready.sem, h + 1)
                    nc.vector.scalar_tensor_tensor(args[:, h % 2, :], dist[:, 1, :], lgf[:, HEADS + h:HEADS + h + 1], args[:, h % 2, :],
                                                   ALU.mult, ALU.add).then_inc(arg_ready.sem, 1)
                log_decay(0)
                for it in range(steps):
                    h, kt = divmod(it, TT)
                    if kt == 0 and h + 1 < HEADS:
                        log_decay(h + 1)
                    dve.wait_ge(ret_scored.sem, it + 1)
                    dve.wait_ge(decay_ready.sem, h + 1)
                    if it >= 4:
                        dve.wait_ge(ret_mixed.sem, it - 3)
                    first = (TT - 1 - kt) * P
                    nc.vector.scalar_tensor_tensor(weighed[:, it % 4, :], psum[:, it % 4, :], RET_QK ** -0.5, decay[:, h % 2, first:first + T],
                                                   ALU.mult, ALU.mult).then_inc(ret_decayed.sem, 1)

        head_norm(heads_out, average128[:], eps_ap[:, 0:1], center=True)
        linear(C, (mix_hi, mix_lo), lambda loop, k, bank: nc.vector.tensor_tensor(x[:, at(loop, k), :], x[:, at(loop, k), :], bank, ALU.add),
               "vector", parts=[(HEADS + h, heads_out[:, h, :], gain_r[:, h:h + 1], proj[:, RG + h, :]) for h in range(HEADS)])
        mix_stack.close()
        if stop == 1:
            return

        peer_stack = ExitStack()
        ctx.enter_context(peer_stack)
        act_hi = sb("act_hi", [P, C, T], F32R, peer_stack)
        act_lo = sb("act_lo", [P, C, T], F32R, peer_stack)
        picks_t = sb("picks_t", [P, 3, T], F32, peer_stack)
        iota = sb("iota", [P, P], F32, peer_stack)
        peer_local = ExitStack()
        queries = sb("queries", [P, LISTS, T], F32, peer_local)
        keys = sb("keys", [P, LISTS, P], F32, peer_local)
        keys_loaded = sig("keys_loaded")

        def load_keys(sp):
            sp.dma_start(keys[:, :, :], keys_t).then_inc(keys_loaded.sem, 16)
            sp.dma_start(iota[:, :], iota_in).then_inc(keys_loaded.sem, 16)
        load_keys.arrived = None
        linear(LISTS, (act_hi, act_lo), scaled(lambda n: queries[:, n, :]), "vector", norm=(x, 1), before=load_keys)

        up_copied = sig("up_product_copied")
        ups_stored = [sig(f"up_product_stored{k}") for k in range(2)]
        ups_dram = nc.dram_tensor("ups_dram", [GROUPS_AHEAD * C, P, T], F32).ap()

        class Ups:
            done = 0

            def __init__(self, count, bank, local):
                self.first, self.bank = Ups.done, bank
                Ups.done += count
                self.buffer = sb("up_products", [P, 2, T], F32, local)

            def number(self, loop, k, per):
                return self.first + k if loop is None else loop * per + (self.first + k)

            def free_bank(self, pe, loop, k, per):
                pe.wait_ge(up_copied.sem, self.number(loop, k, per) + 1)

            def product(self, pe, k):
                self.free_bank(pe, None, k, None)
                weights.multiply(pe, None, k, None, psum[:, self.bank + k % 2, :], (act_hi, act_lo)).then_inc(weights.unit_done.sem, 1)

            def copy(self, act, loop, k, per):
                turn = (self.first + k) // 2
                act.wait_ge(weights.unit_done.sem, weights.done(k) if loop is None else loop * per + weights.done(k))
                act.wait_ge(ups_stored[k % 2].sem, 16 * (turn + 1) if loop is None else loop * (16 * per // 2) + 16 * (turn + 1))
                nc.scalar.activation(self.buffer[:, k % 2, :], psum[:, self.bank + k % 2, :], ACT.Copy).then_inc(up_copied.sem, 1)

            def store(self, sp, loop, k, per):
                n = self.number(loop, k, per)
                sp.wait_ge(up_copied.sem, n + 3)
                sp.dma_start(ups_dram[n], self.buffer[:, k % 2, :]).then_inc(ups_stored[k % 2].sem, 16)

            def all_stored(self, sp):
                for k in range(2):
                    sp.wait_ge(ups_stored[k].sem, 16 * (Ups.done // 2 + 1))

        list_scored, list_copied = sig("peer_scores_ready"), sig("peer_scores_copied")
        top, choose, second, first_j = sig("top_step"), sig("choice_step"), sig("second_key_step"), sig("second_key_input")
        gate_inv = sig("gate_inverse_ready")
        gate_exp, picks_turned, picks_copied = sig("gate_exp_ready"), sig("picks_transposed"), sig("picks_copied")
        TOP_STEPS = 5 * LISTS + 5 * PEER_HEADS + 1
        CHOOSE_STEPS = 11
        UP_EXP = UP_TILE - 3
        with peer_local, nc.Block() as block:
            local = peer_local
            ups = Ups(TT * UP_TILE, 5, local)
            scores_sb = sb("peer_scores", [P, 2, LISTS, P], F32, local)
            rest_sb = sb("peer_scores_rest", [P, LISTS, P], F32, local)
            top_s = sb("top_scores", [P, LISTS, TOPK], F32, local)
            top_i = sb("top_keys", [P, LISTS, TOPK], U32, local)
            top_f = sb("top_keys_f32", [P, LISTS, TOPK], F32, local)
            cand = sb("candidates", [P, PEER_HEADS, TOPK * TOPK], F32, local)
            cand_rest = rest_sb[:, :, :].rearrange("p (h l) n -> p h (l n)", h=PEER_HEADS)
            best = sb("best_scores", [P, PEER_HEADS, TOPK], F32, local)
            place = sb("best_places", [P, PICKS], U32, local)
            place_a = sb("best_first", [P, PICKS], U32, local)
            place_b = sb("best_second", [P, PICKS], U32, local)
            places = sb("best_places_f32", [P, 2, PICKS], F32, local)
            hot = sb("place_one_hot", [P, 2, PICKS, TOPK], F32, local)
            picks = sb("picks", [P, 3, PICKS], F32, local)
            gate_sum = sb("gate_sum", [P, 2, PEER_HEADS], F32, local)

            @block.sync
            def _(sp):
                dram, index = weights.source(weights.u0)
                for k in range(TT * UP_TILE):
                    weights.load(sp, k + RING, (weights.u0 + k) % RING, dram, index + k + RING)
                    ups.store(sp, None, k, None)
                ups.all_stored(sp)

            @block.tensor
            def _(pe):
                pe.sem_inc(up_copied.sem, 2)
                pe.wait_ge(keys_loaded.sem, 32)

                def lists(tile):
                    if tile:
                        pe.wait_ge(list_copied.sem, tile)
                    for l in range(LISTS):
                        mm = nc.tensor.matmul(psum[:, l // 4, (l % 4) * P:(l % 4 + 1) * P], queries[:, l, tile * P:(tile + 1) * P],
                                              keys[:, l, :], start=True, stop=True)
                    mm.then_inc(list_scored.sem, 1)
                lists(0)
                for tile in range(TT):
                    if tile + 1 < TT:
                        lists(tile + 1)
                    for k in range(UP_TILE):
                        ups.product(pe, tile * UP_TILE + k)
                    pe.wait_ge(choose.sem, CHOOSE_STEPS * (tile + 1))
                    if tile:
                        pe.wait_ge(picks_copied.sem, tile)
                    for r in range(3):
                        mm = nc.tensor.transpose(psum[:, 4, r * P:(r + 1) * P], picks[:, r, :], ident[:])
                    mm.then_inc(picks_turned.sem, 1)

            @block.scalar
            def _(act):
                def copy_scores(tile):
                    act.wait_ge(list_scored.sem, tile + 1)
                    if tile >= 2:
                        act.wait_ge(top.sem, TOP_STEPS * (tile - 2) + 4 * LISTS)
                    nc.scalar.activation(scores_sb[:, tile % 2, :, :], psum[:, 0:4, :].rearrange("p b (l n) -> p (b l) n", n=P),
                                         ACT.Copy).then_inc(list_copied.sem, 1)
                def up_steps(units):
                    for k in units:
                        weights.hi_step(act, None, k + weights.AHEAD, None)
                        ups.copy(act, None, k, None)
                act.sem_inc(ups_stored[0].sem, 16)
                act.sem_inc(ups_stored[1].sem, 16)
                copy_scores(0)
                for tile in range(TT):
                    if tile + 1 < TT:
                        copy_scores(tile + 1)
                    up_steps(range(tile * UP_TILE, tile * UP_TILE + UP_EXP))
                    act.wait_ge(choose.sem, CHOOSE_STEPS * tile + 1)
                    nc.scalar.activation(picks[:, 2, :], picks[:, 2, :], ACT.Exp).then_inc(gate_exp.sem, 1)
                    up_steps(range(tile * UP_TILE + UP_EXP, (tile + 1) * UP_TILE))
                    act.wait_ge(picks_turned.sem, tile + 1)
                    nc.scalar.activation(picks_t[:, :, tile * P:(tile + 1) * P], psum[:, 4, 0:3 * P].rearrange("p (r t) -> p r t", r=3),
                                         ACT.Copy).then_inc(picks_copied.sem, 1)

            def by_keys(eng, side):
                hot_h = hot[:, side, :, :].rearrange("p (h k) a -> p h k a", h=PEER_HEADS)
                keys_h = top_f[:, side::2, :].unsqueeze(2).to_broadcast([P, PEER_HEADS, TOPK, TOPK])
                return eng.tensor_tensor(hot_h, hot_h, keys_h, ALU.mult)

            @block.gpsimd
            def _(pool):
                for tile in range(TT):
                    for k in range(tile * UP_TILE, (tile + 1) * UP_TILE):
                        if k == tile * UP_TILE + UP_EXP:
                            pool.wait_ge(first_j.sem, tile + 1)
                            by_keys(nc.gpsimd, 1).then_inc(second.sem, 1)
                        weights.lo_step(pool, None, k + weights.AHEAD, None)

            @block.vector
            def _(dve):
                dve.wait_ge(keys_loaded.sem, 32)
                for tile in range(TT):
                    n0 = TOP_STEPS * tile
                    dve.wait_ge(list_copied.sem, tile + 1)
                    s = scores_sb[:, tile % 2, :, :]
                    for l in range(LISTS):
                        nc.vector.max(top_s[:, l, 0:8], s[:, l, :]).then_inc(top.sem, 1)
                    for l in range(LISTS):
                        dve.wait_ge(top.sem, n0 + l + 1)
                        nc.vector.match_replace(rest_sb[:, l, :], top_s[:, l, 0:8], s[:, l, :], LOWEST).then_inc(top.sem, 1)
                    for l in range(LISTS):
                        nc.vector.max_index(top_i[:, l, 0:8], top_s[:, l, 0:8], s[:, l, :]).then_inc(top.sem, 1)
                    for l in range(LISTS):
                        dve.wait_ge(top.sem, n0 + LISTS + l + 1)
                        nc.vector.max(top_s[:, l, 8:16], rest_sb[:, l, :]).then_inc(top.sem, 1)
                    for l in range(LISTS):
                        dve.wait_ge(top.sem, n0 + 3 * LISTS + l + 1)
                        nc.vector.max_index(top_i[:, l, 8:16], top_s[:, l, 8:16], rest_sb[:, l, :]).then_inc(top.sem, 1)
                    n1 = n0 + 5 * LISTS
                    pairs = cand[:, :, :].rearrange("p h (a b) -> p h a b", a=TOPK)
                    nc.vector.tensor_tensor(pairs, top_s[:, 0::2, :].unsqueeze(3).to_broadcast([P, PEER_HEADS, TOPK, TOPK]),
                                            top_s[:, 1::2, :].unsqueeze(2).to_broadcast([P, PEER_HEADS, TOPK, TOPK]), ALU.add).then_inc(top.sem, 1)
                    dve.wait_ge(top.sem, n1 + 1)
                    for h in range(PEER_HEADS):
                        nc.vector.max(best[:, h, 0:8], cand[:, h, :]).then_inc(top.sem, 1)
                    for h in range(PEER_HEADS):
                        dve.wait_ge(top.sem, n1 + 1 + h + 1)
                        nc.vector.match_replace(cand_rest[:, h, :], best[:, h, 0:8], cand[:, h, :], LOWEST).then_inc(top.sem, 1)
                    for h in range(PEER_HEADS):
                        nc.vector.max_index(place[:, h * TOPK:h * TOPK + 8], best[:, h, 0:8], cand[:, h, :]).then_inc(top.sem, 1)
                    for h in range(PEER_HEADS):
                        dve.wait_ge(top.sem, n1 + 1 + PEER_HEADS + h + 1)
                        nc.vector.max(best[:, h, 8:16], cand_rest[:, h, :]).then_inc(top.sem, 1)
                    for h in range(PEER_HEADS):
                        dve.wait_ge(top.sem, n1 + 1 + 3 * PEER_HEADS + h + 1)
                        nc.vector.max_index(place[:, h * TOPK + 8:(h + 1) * TOPK], best[:, h, 8:16], cand_rest[:, h, :]).then_inc(top.sem, 1)
                    m0 = CHOOSE_STEPS * tile
                    gates = picks[:, 2, :].rearrange("p (h k) -> p h k", h=PEER_HEADS)
                    if tile:
                        dve.wait_ge(picks_turned.sem, tile)
                    nc.vector.tensor_tensor(gates, best[:, :, :], best[:, :, 0:1].to_broadcast([P, PEER_HEADS, TOPK]), ALU.subtract).then_inc(choose.sem, 1)
                    dve.wait_ge(top.sem, n0 + TOP_STEPS)
                    nc.vector.tensor_scalar(place_a[:], place[:], 4, None, ALU.logical_shift_right).then_inc(choose.sem, 1)
                    nc.vector.tensor_scalar(place_b[:], place[:], TOPK - 1, None, ALU.bitwise_and).then_inc(choose.sem, 1)
                    nc.vector.tensor_copy(top_f[:, :, :], top_i[:, :, :])
                    dve.wait_ge(choose.sem, m0 + 3)
                    nc.vector.tensor_copy(places[:, 0, :], place_a[:]).then_inc(choose.sem, 1)
                    nc.vector.tensor_copy(places[:, 1, :], place_b[:]).then_inc(choose.sem, 1)
                    dve.wait_ge(choose.sem, m0 + 5)
                    for side, one_hots in ((1, first_j), (0, choose)):
                        nc.vector.tensor_tensor(hot[:, side, :, :], iota[:, 0:TOPK].unsqueeze(1).to_broadcast([P, PICKS, TOPK]),
                                                places[:, side, :].unsqueeze(2).to_broadcast([P, PICKS, TOPK]), ALU.is_equal).then_inc(one_hots.sem, 1)
                    dve.wait_ge(choose.sem, m0 + 6)
                    by_keys(nc.vector, 0).then_inc(choose.sem, 1)
                    dve.wait_ge(choose.sem, m0 + 7)
                    nc.vector.tensor_reduce(picks[:, 0, :], hot[:, 0, :, :], AX.X, ALU.add).then_inc(choose.sem, 1)
                    dve.wait_ge(second.sem, tile + 1)
                    nc.vector.tensor_reduce(picks[:, 1, :], hot[:, 1, :, :], AX.X, ALU.add).then_inc(choose.sem, 1)
                    dve.wait_ge(gate_exp.sem, tile + 1)
                    nc.vector.tensor_reduce(gate_sum[:, 0, :], gates, AX.X, ALU.add).then_inc(choose.sem, 1)
                    dve.wait_ge(choose.sem, m0 + 10)
                    nc.vector.reciprocal(gate_sum[:, 1, :], gate_sum[:, 0, :]).then_inc(gate_inv.sem, 1)
                    dve.wait_ge(gate_inv.sem, tile + 1)
                    nc.vector.tensor_tensor(gates, gates, gate_sum[:, 1, :].unsqueeze(2).to_broadcast([P, PEER_HEADS, TOPK]), ALU.mult).then_inc(choose.sem, 1)
        weights.u0 += TT * UP_TILE
        if stop == 2:
            return

        hot1_ready, hot2_ready, dense_ready, dense_copied = (sig(n) for n in ("first_one_hots_ready", "gated_one_hots_ready", "dense_gates_ready", "dense_gates_copied"))
        hot2_raw, hot2_gated = sig("odd_second_one_hots_ready"), sig("odd_second_one_hots_gated")
        gates_stored = [sig(f"gates_stored{k}") for k in range(2)]
        ups_loaded = sig("up_group_loaded")
        group = sb("up_group", [P, C, T], F32, peer_stack)
        QUAD = 4
        HOTS = 4
        GSTEPS = GT // QUAD
        LOOP_TOKENS = 2 * GT
        LOOP_STEPS = LOOP_TOKENS // QUAD
        LOOP_UNITS = UP_DENSE * LOOP_TOKENS // T

        def load_ups(sp, g):
            sp.dma_start(group[:, :, :], ups_dram[bass.ds(g * C, C)].rearrange("c p t -> p c t")).then_inc(ups_loaded.sem, 16)
        with ExitStack() as local, nc.Block() as block:
            hot1 = [sb("hot1", [P, QUAD, P], F32, local) for _ in range(HOTS)]
            hot2 = [sb("hot2", [P, QUAD, P], F32, local) for _ in range(HOTS)]
            stage = sb("gates_stage", [P, 2, N_KEYS, GT], F32, local)
            ups = Ups(UP_DENSE + UP_TAIL, 5, local)
            tail = range(UP_DENSE, UP_DENSE + UP_TAIL)

            @block.vector
            def _(dve):
                def one_hots(hot, r, i, k):
                    return nc.vector.tensor_tensor(hot[:, :, :], iota[:, :].unsqueeze(1).to_broadcast([P, QUAD, P]),
                                                   picks_t[:, r, bass.ds(i * (HOTS * QUAD) + k * QUAD, QUAD)].unsqueeze(2).to_broadcast([P, QUAD, P]),
                                                   ALU.is_equal)
                with dve.Fori(0, T // QUAD // HOTS) as i:
                    for k in range(HOTS):
                        dve.wait_ge(dense_ready.sem, i * HOTS + (k + 1))
                        one_hots(hot1[k], 0, i, k).then_inc(hot1_ready.sem, 1)
                        if k % 2:
                            one_hots(hot2[k], 1, i, k).then_inc(hot2_raw.sem, 1)
                            continue
                        for t in range(QUAD):
                            token = i * (HOTS * QUAD) + (k * QUAD + t)
                            ins = nc.vector.tensor_scalar(hot2[k][:, t, :], iota[:, :], picks_t[:, 1, bass.ds(token, 1)], picks_t[:, 2, bass.ds(token, 1)],
                                                          ALU.is_equal, ALU.mult)
                        ins.then_inc(hot2_ready.sem, 1)

            @block.gpsimd
            def _(pool):
                with pool.Fori(0, T // LOOP_TOKENS) as i:
                    for u in range(LOOP_UNITS):
                        for n in range(u * C // 2, (u + 1) * C // 2):
                            if n == u * C // 2 + 1:
                                weights.lo_step(pool, i, u + weights.AHEAD, LOOP_UNITS)
                            pool.wait_ge(hot2_raw.sem, i * (LOOP_STEPS // 2) + (n + 1))
                            hot = hot2[(2 * n + 1) % HOTS]
                            nc.gpsimd.tensor_tensor(hot[:, :, :], hot[:, :, :],
                                                    picks_t[:, 2, bass.ds(i * LOOP_TOKENS + (2 * n + 1) * QUAD, QUAD)].unsqueeze(2).to_broadcast([P, QUAD, P]),
                                                    ALU.mult).then_inc(hot2_gated.sem, 1)
                for k in tail:
                    weights.lo_step(pool, None, k + weights.AHEAD, None)

            @block.tensor
            def _(pe):
                pe.sem_inc(dense_copied.sem, 2)
                pe.sem_inc(dense_ready.sem, HOTS)
                with pe.Fori(0, T // LOOP_TOKENS) as i:
                    for u in range(LOOP_UNITS):
                        ups.free_bank(pe, i, u, LOOP_UNITS)
                        for c in range(C):
                            n, k = u * C + c, c % 2
                            pe.wait_ge(hot1_ready.sem, i * LOOP_STEPS + (n + 1))
                            gated_hots = hot2_gated if k else hot2_ready
                            pe.wait_ge(gated_hots.sem, i * (LOOP_STEPS // 2) + (n // 2 + 1))
                            pe.wait_ge(dense_copied.sem, i * LOOP_STEPS + (n + 1))
                            for t in range(QUAD):
                                mm = nc.tensor.matmul(psum[:, k, t * P:(t + 1) * P], hot1[c % HOTS][:, t, :], hot2[c % HOTS][:, t, :], start=True, stop=True)
                            mm.then_inc(dense_ready.sem, 1)
                            mm = weights.multiply_chunk(pe, i, u, LOOP_UNITS, psum[:, ups.bank + u % 2, :], (act_hi, act_lo), c)
                        mm.then_inc(weights.unit_done.sem, 1)
                for k in tail:
                    ups.product(pe, k)

            @block.scalar
            def _(act):
                act.sem_inc(gates_stored[0].sem, 16)
                act.sem_inc(gates_stored[1].sem, 16)
                with act.Fori(0, T // LOOP_TOKENS) as i:
                    for u in range(LOOP_UNITS):
                        half = u * C // GSTEPS
                        if u * C % GSTEPS == 0:
                            act.wait_ge(gates_stored[half].sem, i * 16 + 16)
                        weights.hi_step(act, i, u + weights.AHEAD, LOOP_UNITS)
                        for c in range(C):
                            n = u * C + c
                            act.wait_ge(dense_ready.sem, i * LOOP_STEPS + (n + HOTS + 1))
                            nc.scalar.activation(stage[:, half, :, n % GSTEPS * QUAD:(n % GSTEPS + 1) * QUAD],
                                                 psum[:, c % 2, :].rearrange("p (t j) -> p j t", t=QUAD), ACT.Copy).then_inc(dense_copied.sem, 1)
                        ups.copy(act, i, u, LOOP_UNITS)
                for k in tail:
                    weights.hi_step(act, None, k + weights.AHEAD, None)
                    ups.copy(act, None, k, None)

            @block.sync
            def _(sp):
                load_ups(sp, 0)
                dram, index = weights.source(weights.u0)
                with sp.Fori(0, T // LOOP_TOKENS) as i:
                    for u in range(LOOP_UNITS):
                        weights.load(sp, i * LOOP_UNITS + (u + RING), (weights.u0 + u) % RING, dram, i * LOOP_UNITS + (index + u + RING))
                        ups.store(sp, i, u, LOOP_UNITS)
                        if (u + 1) * C % GSTEPS == 0:
                            half = u * C // GSTEPS
                            sp.wait_ge(dense_copied.sem, i * LOOP_STEPS + ((u + 1) * C + 2))
                            sp.dma_start(gates_dram[i * 2 + half], stage[:, half, :, :].rearrange("p j t -> p (j t)")).then_inc(gates_stored[half].sem, 16)
                for k in tail:
                    weights.load(sp, k + RING, (weights.u0 + k) % RING, dram, index + k + RING)
                    ups.store(sp, None, k, None)
                for half in range(2):
                    sp.wait_ge(gates_stored[half].sem, 16 * (GBLOCKS // 2 + 1))
                ups.all_stored(sp)
        weights.u0 += UP_DENSE + UP_TAIL

        activated = sig("ffn_activated")
        read = sig("ffn_up_scaled")
        gated, ffn_hi, ffn_lo = sig("ffn_gated"), sig("ffn_hi_ready"), sig("ffn_lo_ready")
        gates_loaded = sig("gates_loaded")
        started = [False]

        def gates_of(g):
            return gates_dram[:, :, bass.ds(g * (C * GT), C * GT)].rearrange("b i n -> i b n")

        def feed_forward(groups, acts, function, gates, h_hi, h_lo, raw_act, raw_gated, gate_tile=None, first_group=0):
            w = weights
            u0, base, per = w.u0, out_free.base, 2 * C
            a0, g0, h0, r0 = activated.base, gated.base, ffn_lo.base, read.base
            first = not started[0]
            started[0] = True
            with nc.Block() as block:
                @block.sync
                def _(sp):
                    if gates:
                        sp.dma_start(gate_tile[:, :, :], gates_of(first_group)).then_inc(gates_loaded.sem, 16)
                    dram, index = w.source(u0)
                    with sp.Fori(0, groups - 1) as i:
                        for k in range(per):
                            w.load(sp, i * per + (k + RING), (u0 + k) % RING, dram, i * per + (index + k + RING))
                            if gates and k == per - RING - 1:
                                sp.wait_ge(gated.sem, i * C + (g0 + C))
                                sp.dma_start(gate_tile[:, :, :], gates_of(i + (first_group + 1))).then_inc(gates_loaded.sem, 16)
                    for k in range(per):
                        v = u0 + (groups - 1) * per + k + RING
                        if v < w.total:
                            dram, index = w.source(v)
                            w.load(sp, (groups - 1) * per + k + RING, v % RING, dram, index)

                @block.tensor
                def _(pe):
                    if first:
                        pe.sem_inc(read.sem, RING)
                    with pe.Fori(0, groups) as i:
                        for k in range(C):
                            pe.wait_ge(read.sem, i * C + (r0 + k + 1))
                            w.multiply(pe, i, k, per, psum[:, k % RING, :], acts).then_inc(w.unit_done.sem, 1)
                        for d in range(C):
                            pe.wait_ge(out_free.sem, i * C + (base + d + 1))
                            bank = psum[:, 4 + d % RING, :]
                            for c in range(C):
                                if d == 0:
                                    pe.wait_ge(ffn_lo.sem, i * C + (h0 + c + 1))
                                mm = w.multiply_chunk(pe, i, C + d, per, bank, (h_hi, h_lo), c)
                            mm.then_inc(w.unit_done.sem, 1)
                    pe.wait_ge(out_free.sem, groups * C + (base + RING))
                    sum_squares(pe, raw_gated)

                @block.scalar
                def _(act):
                    def body(i, last):
                        for k in range(per):
                            if not (last and w.u0 + (groups - 1) * per + k + w.AHEAD >= w.total):
                                w.hi_step(act, i, k + w.AHEAD, per)
                            if last and k > C:
                                square(act, k - C - 1)
                            if k < C:
                                act.wait_ge(read.sem, i * C + (r0 + RING + k + 1))
                                nc.scalar.activation(raw_act[:, k % 2, :], raw_act[:, k % 2, :], function).then_inc(activated.sem, 1)
                                act.wait_ge(gated.sem, i * C + (g0 + k + 1))
                                nc.scalar.activation(h_hi[:, k, :], raw_gated[:, k % 2, :], ACT.Copy).then_inc(ffn_hi.sem, 1)

                    def square(act, d):
                        act.wait_ge(out_free.sem, base + RING + (groups - 1) * C + d + 1)
                        if d >= 2:
                            act.wait_ge(norm_acc.sem, norm_acc.at(d - 1))
                        nc.scalar.activation(raw_act[:, d % 2, :], x[:, d, :], ACT.Square).then_inc(norm_sq.sem, 1)
                    with act.Fori(0, groups - 1) as i:
                        body(i, False)
                    body(groups - 1, True)
                    square(act, C - 1)
                    root(act)

                @block.vector
                def _(dve):
                    def body(i, last):
                        for k in range(per):
                            def lo_ahead():
                                if not (last and w.u0 + (groups - 1) * per + k + w.AHEAD >= w.total):
                                    w.lo_step(dve, i, k + w.AHEAD, per)
                            if k < C:
                                dve.wait_ge(w.unit_done.sem, i * per + w.done(k))
                                nc.vector.tensor_tensor(raw_act[:, k % 2, :], psum[:, k % RING, :], rstd[:], ALU.mult).then_inc(read.sem, 1)
                            if k != C - 1:
                                lo_ahead()
                            if k < C:
                                dve.wait_ge(activated.sem, i * C + (a0 + k + 1))
                                if gates and k == 0:
                                    dve.wait_ge(gates_loaded.sem, i * 16 + (gates_loaded.base + 16))
                                other = gate_tile[:, :, k * GT:(k + 1) * GT] if gates else raw_act[:, k % 2, :]
                                one = raw_act[:, k % 2, :]
                                out = raw_gated[:, k % 2, :]
                                if gates:
                                    one, out = (a.rearrange("p (b t) -> p b t", t=GT) for a in (one, out))
                                nc.vector.tensor_tensor(out, one, other, ALU.mult).then_inc(gated.sem, 1)
                                dve.wait_ge(ffn_hi.sem, i * C + (g0 + k + 1))
                                nc.vector.tensor_tensor(h_lo[:, k, :], raw_gated[:, k % 2, :], h_hi[:, k, :].bitcast(F32),
                                                        ALU.subtract).then_inc(ffn_lo.sem, 1)
                                if k == C - 1:
                                    lo_ahead()
                            else:
                                d = k - C
                                dve.wait_ge(w.unit_done.sem, i * per + w.done(k))
                                nc.vector.tensor_tensor(x[:, d, :], x[:, d, :], psum[:, 4 + d % RING, :], ALU.add).then_inc(out_free.sem, 1)
                                if last and d:
                                    add_squares(raw_act, raw_gated, d - 1, 2)
                    with dve.Fori(0, groups - 1) as i:
                        body(i, False)
                    body(groups - 1, True)
                    add_squares(raw_act, raw_gated, C - 1, 2)
            norm_done()
            w.u0 += groups * per
            for s in (activated, read, gated, ffn_hi, ffn_lo, out_free):
                s.base += groups * C

        ups_scaled, ups_gelu = sig("up_group_scaled"), sig("up_group_activated")
        inner_free = sig("inner_chunk_free")

        def stored_groups(local):
            w = weights
            ups = Ups(UP_FIRST, 0, local)
            base, first = out_free.base, UP_FIRST
            last_group = range(first + (GROUPS_AHEAD - 1) * C, first + GROUPS_AHEAD * C)
            with nc.Block() as block:
                def load_gates(sp, g):
                    sp.dma_start(gate_tile[:, :, :], gates_of(g)).then_inc(gates_loaded.sem, 16)

                @block.sync
                def _(sp):
                    load_gates(sp, 0)
                    dram, index = w.source(w.u0)
                    for k in range(first):
                        w.load(sp, k + RING, (w.u0 + k) % RING, dram, index + k + RING)
                        ups.store(sp, None, k, None)
                    ups.all_stored(sp)
                    with sp.Fori(0, GROUPS_AHEAD - 1) as i:
                        for k in range(first, first + C):
                            w.load(sp, i * C + (k + RING), (w.u0 + k) % RING, dram, i * C + (index + k + RING))
                            if k == first:
                                sp.wait_ge(ffn_lo.sem, i * C + C)
                                load_ups(sp, i + 1)
                                load_gates(sp, i + 1)
                    for k in last_group:
                        w.load(sp, k + RING, (w.u0 + k) % RING, dram, index + k + RING)

                @block.tensor
                def _(pe):
                    for k in range(first):
                        ups.product(pe, k)
                    with pe.Fori(0, GROUPS_AHEAD) as i:
                        for d in range(C):
                            pe.wait_ge(out_free.sem, i * C + (base + d + 1))
                            for c in range(C):
                                if d == 0:
                                    pe.wait_ge(ffn_lo.sem, i * C + (c + 1))
                                mm = w.multiply_chunk(pe, i, first + d, C, psum[:, 4 + d % RING, :], (inner_hi, inner_lo), c)
                                if d == C - 1 and c < C - 1:
                                    mm.then_inc(inner_free.sem, 1)
                            mm.then_inc(w.unit_done.sem, 1)

                def next_group(i):
                    return 0 if i is None else i * C + C

                @block.gpsimd
                def _(pool):
                    def scale(i):
                        pool.wait_ge(ups_loaded.sem, 16 if i is None else i * 16 + 32)
                        for c in range(C):
                            nc.gpsimd.tensor_tensor(group[:, c, :], group[:, c, :], rstd[:], ALU.mult).then_inc(ups_scaled.sem, 1)
                    scale(None)
                    with pool.Fori(0, GROUPS_AHEAD - 1) as i:
                        scale(i)

                @block.scalar
                def _(act):
                    def gelu(i, c):
                        act.wait_ge(ups_scaled.sem, next_group(i) + (c + 1))
                        nc.scalar.activation(group[:, c, :], group[:, c, :], ACT.Gelu).then_inc(ups_gelu.sem, 1)

                    def inner(i, c):
                        act.wait_ge(gated.sem, next_group(i) + (c + 1))
                        if i is not None and c < C - 1:
                            act.wait_ge(inner_free.sem, i * (C - 1) + (c + 1))
                        elif i is not None:
                            act.wait_ge(w.unit_done.sem, i * C + w.done(first + C - 1))
                        nc.scalar.activation(inner_hi[:, c, :], group[:, c, :], ACT.Copy).then_inc(ffn_hi.sem, 1)
                    for k in range(first):
                        w.hi_step(act, None, k + w.AHEAD, None)
                        if k == first - 2:
                            for c in range(C):
                                gelu(None, c)
                        if k == first - 1:
                            for c in range(C):
                                inner(None, c)
                        ups.copy(act, None, k, None)
                    with act.Fori(0, GROUPS_AHEAD - 1) as i:
                        for d in range(C):
                            w.hi_step(act, i, first + d + w.AHEAD, C)
                            if d in (3, 4):
                                for c in range(4 * (d - 3), 4 * (d - 2)):
                                    gelu(i, c)
                        for c in range(C):
                            inner(i, c)
                    for k in last_group:
                        w.hi_step(act, None, k + w.AHEAD, None)

                @block.vector
                def _(dve):
                    def gate(i, c):
                        if c == 0:
                            dve.wait_ge(gates_loaded.sem, 16 if i is None else i * 16 + 32)
                        dve.wait_ge(ups_gelu.sem, next_group(i) + (c + 1))
                        chunk = group[:, c, :].rearrange("p (b t) -> p b t", t=GT)
                        nc.vector.tensor_tensor(chunk, chunk, gate_tile[:, :, c * GT:(c + 1) * GT], ALU.mult).then_inc(gated.sem, 1)

                    def inner_lo_step(i, c):
                        dve.wait_ge(ffn_hi.sem, next_group(i) + (c + 1))
                        nc.vector.tensor_tensor(inner_lo[:, c, :], group[:, c, :], inner_hi[:, c, :].bitcast(F32),
                                                ALU.subtract).then_inc(ffn_lo.sem, 1)

                    def add(i, d):
                        dve.wait_ge(w.unit_done.sem, w.done(last_group[d]) if i is None else i * C + w.done(first + d))
                        nc.vector.tensor_tensor(x[:, d, :], x[:, d, :], psum[:, 4 + d % RING, :], ALU.add).then_inc(out_free.sem, 1)
                    for k in range(first):
                        w.lo_step(dve, None, k + w.AHEAD, None)
                    gate(None, 0)
                    for c in range(C):
                        if c + 1 < C:
                            gate(None, c + 1)
                        inner_lo_step(None, c)
                    with dve.Fori(0, GROUPS_AHEAD - 1) as i:
                        for d in range(C - 1):
                            w.lo_step(dve, i, first + d + w.AHEAD, C)
                            add(i, d)
                            if d in (5, 6):
                                for c in range(4 * (d - 5), 4 * (d - 4)):
                                    gate(i, c)
                        for c in range(C):
                            inner_lo_step(i, c)
                        w.lo_step(dve, i, first + C - 1 + w.AHEAD, C)
                        add(i, C - 1)
                    for d in range(C):
                        w.lo_step(dve, None, last_group[d] + w.AHEAD, None)
                        add(None, d)
            w.u0 += first + GROUPS_AHEAD * C
            for s in (gated, ffn_hi, ffn_lo, out_free):
                s.base += GROUPS_AHEAD * C
            gates_loaded.base += 16 * GROUPS_AHEAD

        with ExitStack() as local:
            inner_hi = sb("inner_hi", [P, C, T], F32R, local)
            inner_lo = sb("inner_lo", [P, C, T], F32R, local)
            raw_act = sb("inner_activated", [P, 2, T], F32, local)
            raw_gated = sb("inner_gated", [P, 2, T], F32, local)
            gate_tile = sb("gates_of_group", [P, GBLOCKS, C * GT], F32, local)
            with ExitStack() as ahead:
                stored_groups(ahead)
            feed_forward(EXPERT_GROUPS - GROUPS_AHEAD, (act_hi, act_lo), ACT.Gelu, True, inner_hi, inner_lo, raw_act, raw_gated,
                         gate_tile, GROUPS_AHEAD)
        peer_stack.close()
        if stop == 3:
            return

        y = sb("rwkv_out", [P, 4, T], F32)
        rwkv_stack = ExitStack()
        ctx.enter_context(rwkv_stack)
        rw = sb("rwkv_projections", [P, RWKV_SLABS, T + 1], F32, rwkv_stack)
        vecs = sb("rwkv_vectors_sb", [P, 64], F32, rwkv_stack)
        mu, kkv, kav, rkv, a0v, lnw, lnb = vecs[:, 0:15], vecs[:, 16:20], vecs[:, 20:24], vecs[:, 24:28], vecs[:, 28:32], vecs[:, 32:36], vecs[:, 36:40]
        block_ones = sb("block_ones", [P, P], F32, rwkv_stack)
        block_avg = sb("block_average", [P, P], F32, rwkv_stack)
        lora = sb("rwkv_lora", [P, 3, T], F32, rwkv_stack)
        w0_row = sb("rwkv_w0", [1, T], F32, rwkv_stack)
        ln_eps = sb("rwkv_eps", [P, 1], F32, rwkv_stack)
        mid_decay = sb("mid_decay", [P, 2, 4, TT], F32, rwkv_stack)
        sum_masks = sb("decay_sum_masks", [P, 2, P], F32, rwkv_stack)
        rwkv_loaded = sig("rwkv_loaded")

        def load_rwkv(sp):
            for dst, src in ((vecs[:, 0:40], rwkv["vectors"]), (block_ones[:], rwkv["block_ones"]), (block_avg[:], rwkv["block_average"]),
                             (lora[:, 0, :], rwkv["lora_wa"]), (lora[:, 1, :], rwkv["lora_g"][0:P, :]),
                             (lora[0:32, 2, :], rwkv["lora_g"][P:P + 32, :]), (w0_row[:, :], rwkv["w0"]), (sum_masks[:, :, :], rwkv["sum_masks"])):
                sp.dma_start(dst, src).then_inc(rwkv_loaded.sem, 16)
        load_rwkv.arrived = None

        def R(n):
            return rw[:, n, 1:T + 1]

        shift_diff, shifted = sig("shift_difference_ready"), sig("token_shifted")
        with ExitStack() as local:
            act_hi = sb("act_hi", [P, C, T], F32R, local)
            act_lo = sb("act_lo", [P, C, T], F32R, local)
            diff = sb("shift_difference", [P, 2, T], F32, local)

            def gpsimd_along(pool, before_first):
                nc.gpsimd.memset(rw[:, :, 0:1], 0.0).then_inc(shift_diff.sem, 1)
                nc.gpsimd.memset(ln_eps[:], RWKV_LN_EPS)
                pool.wait_ge(shift_diff.sem, 1)
                for n in range(RWKV_SLABS):
                    pool.wait_ge(out_free.sem, before_first + n + 1)
                    if n >= 2:
                        pool.wait_ge(shifted.sem, n - 1)
                    nc.gpsimd.tensor_tensor(diff[:, n % 2, :], rw[:, n, 0:T], rw[:, n, 1:T + 1], ALU.subtract).then_inc(shift_diff.sem, 1)

            def shift(n):
                nc.vector.wait_ge(shift_diff.sem, n + 2)
                nc.vector.scalar_tensor_tensor(R(n), diff[:, n % 2, :], mu[:, n:n + 1], R(n), ALU.mult, ALU.add).then_inc(shifted.sem, 1)

            def vector_along(k):
                if k == 1:
                    nc.vector.wait_ge(rwkv_loaded.sem, 8 * 16)
                if k:
                    shift(k - 1)
                if k == RWKV_SLABS - 1:
                    shift(k)
            linear(RWKV_SLABS, (act_hi, act_lo), scaled(lambda n: rw[:, n, 1:T + 1]), "vector", norm=(x, 3, 2), before=load_rwkv,
                   along=(lambda k: None, vector_along, gpsimd_along))

        R_, K_, V_, WA_, G_ = 0, 4, 8, 12, 13
        kk = sb("rwkv_kk", [P, 4, T], F32, rwkv_stack)
        bb = sb("rwkv_b", [P, 4, T], F32, rwkv_stack)
        bonus = sb("rwkv_bonus", [P, 4, T], F32, rwkv_stack)
        turned_stack = ExitStack()
        rwkv_stack.enter_context(turned_stack)
        decay_in = sb("decay_gate", [P, TT, T], F32, turned_stack)

        lora_in, decay_product = sig("lora_inputs_ready"), sig("decay_product_ready")
        a_product = sig("a_product_ready")
        with nc.Block() as block:
            @block.vector
            def _(dve):
                for j in range(4):
                    nc.vector.tensor_scalar(kk[:, j, :], R(K_ + j), kkv[:, j:j + 1], None, ALU.mult)

            @block.tensor
            def _(pe):
                pe.wait_ge(rwkv_loaded.sem, 8 * 16)
                pe.wait_ge(lora_in.sem, 1)
                for tile in range(TT):
                    tokens = slice(1 + tile * P, 1 + (tile + 1) * P)
                    nc.tensor.matmul(psum[:, tile, :], rw[0:64, WA_, tokens], lora[0:64, 0, :], start=True, stop=False)
                    nc.tensor.matmul(psum[:, tile, :], ones[0:1, :], w0_row[0:1, :], start=False, stop=True).then_inc(decay_product.sem, 1)
                for j in range(4):
                    nc.tensor.matmul(psum[:, 4 + j, :], lora[64:128, 0, j * P:(j + 1) * P], rw[64:128, WA_, 1:T + 1],
                                     start=True, stop=True).then_inc(a_product.sem, 1)

            @block.scalar
            def _(act):
                nc.scalar.activation(rw[0:64, WA_, 1:T + 1], rw[0:64, WA_, 1:T + 1], ACT.Tanh).then_inc(lora_in.sem, 1)
                nc.scalar.activation(R(G_), R(G_), ACT.Sigmoid)
                nc.scalar.activation(rw[0:32, G_ + 1, 1:T + 1], rw[0:32, G_ + 1, 1:T + 1], ACT.Sigmoid)
                for tile in range(TT):
                    act.wait_ge(decay_product.sem, tile + 1)
                    nc.scalar.activation(decay_in[:, tile, :], psum[:, tile, :], ACT.Sigmoid)
                act.wait_ge(rwkv_loaded.sem, 8 * 16)
                for j in range(4):
                    act.wait_ge(a_product.sem, j + 1)
                    nc.scalar.activation(bb[:, j, :], psum[:, 4 + j, :], ACT.Sigmoid, bias=a0v[:, j:j + 1])

        head_norm(kk, block_ones[:], 0.0, center=False, floor=1e-24)

        KAPPA = math.exp(-0.5)
        sums_ready, sums_read = sig("decay_sums_ready"), sig("decay_sums_read")
        ops, bonus_sum, k_step = sig("rwkv_operand_ready"), sig("bonus_sum_ready"), sig("k_factor_ready")
        with ExitStack() as local, nc.Block() as block:
            till = sb("decay_till", [P, 4, T], F32, local)
            before = sb("decay_before", [P, 4, T], F32, local)
            back = sb("decay_inverse", [P, 4, T], F32, local)
            factor = sb("k_factor", [P, 4, T], F32, local)

            @block.tensor
            def _(pe):
                for j in range(4):
                    for pair in range(2):
                        n = 2 * j + pair
                        if n >= 4:
                            pe.wait_ge(sums_read.sem, n - 3)
                        for half in range(2):
                            tile = 2 * pair + half
                            mm = nc.tensor.matmul(psum[:, n % 4, half * 2 * P:(half + 1) * 2 * P], decay_in[:, tile, j * P:(j + 1) * P],
                                                  sum_masks[:, :, :], start=True, stop=True)
                        mm.then_inc(sums_ready.sem, 1)
                for j in range(4):
                    pe.wait_ge(ops.sem, j + 1)
                    nc.tensor.matmul(psum[:, 4 + j, :], block_ones[:], bonus[:, j, :], start=True, stop=True).then_inc(bonus_sum.sem, 1)

            @block.scalar
            def _(act):
                for j in range(4):
                    for pair in range(2):
                        n = 2 * j + pair
                        act.wait_ge(sums_ready.sem, n + 1)
                        sums = psum[:, n % 4, :].rearrange("p (h m t) -> p h m t", h=2, m=2)
                        span = slice(2 * pair * P, 2 * (pair + 1) * P)

                        def two(buf):
                            return buf[:, j, span].rearrange("p (h t) -> p h t", h=2)
                        nc.scalar.activation(two(till), sums[:, :, 0, :], ACT.Exp, scale=-KAPPA)
                        nc.scalar.activation(two(back), sums[:, :, 0, :], ACT.Exp, scale=KAPPA)
                        nc.scalar.activation(two(before), sums[:, :, 1, :], ACT.Exp, scale=-KAPPA)
                        nc.scalar.activation(mid_decay[:, 1, j, 2 * pair:2 * pair + 2], sums[:, :, 0, P - 1], ACT.Exp, scale=-KAPPA)
                        nc.scalar.activation(mid_decay[:, 0, j, 2 * pair:2 * pair + 2], sums[:, :, 1, 0], ACT.Exp, scale=KAPPA).then_inc(sums_read.sem, 1)

            @block.vector
            def _(dve):
                for j in range(4):
                    nc.vector.tensor_scalar(factor[:, j, :], bb[:, j, :], 1.0, kav[:, j:j + 1], ALU.subtract, ALU.mult).then_inc(k_step.sem, 1)
                for j in range(4):
                    dve.wait_ge(k_step.sem, j + 1)
                    nc.vector.scalar_tensor_tensor(R(K_ + j), factor[:, j, :], 1.0, R(K_ + j), ALU.add, ALU.mult).then_inc(k_step.sem, 1)
                for j in range(4):
                    dve.wait_ge(k_step.sem, 4 + j + 1)
                    nc.vector.scalar_tensor_tensor(bonus[:, j, :], R(R_ + j), rkv[:, j:j + 1], R(K_ + j), ALU.mult, ALU.mult).then_inc(ops.sem, 1)
                for j in range(4):
                    nc.vector.tensor_tensor(bb[:, j, :], bb[:, j, :], kk[:, j, :], ALU.mult).then_inc(k_step.sem, 1)
                for j in range(4):
                    dve.wait_ge(bonus_sum.sem, j + 1)
                    nc.vector.tensor_tensor(bonus[:, j, :], R(V_ + j), psum[:, 4 + j, :], ALU.mult)
                for j in range(4):
                    dve.wait_ge(sums_read.sem, 2 * (j + 1))
                    dve.wait_ge(k_step.sem, 8 + j + 1)
                    nc.vector.tensor_tensor(bb[:, j, :], bb[:, j, :], back[:, j, :], ALU.mult)
                    nc.vector.scalar_tensor_tensor(kk[:, j, :], kk[:, j, :], -1.0, before[:, j, :], ALU.mult, ALU.mult)

            @block.gpsimd
            def _(pool):
                for j in range(4):
                    pool.wait_ge(sums_read.sem, 2 * (j + 1))
                    pool.wait_ge(ops.sem, j + 1)
                    nc.gpsimd.tensor_tensor(R(K_ + j), R(K_ + j), back[:, j, :], ALU.mult)
                    nc.gpsimd.tensor_tensor(R(R_ + j), R(R_ + j), till[:, j, :], ALU.mult)
        turned_stack.close()

        tok_turned, tok_copied = sig("operand_transposed"), sig("operand_copied")
        v_t = sb("rwkv_v_by_token", [P, TT, T], F32, rwkv_stack)
        k_t = sb("rwkv_k_by_token", [P, TT, T], F32, rwkv_stack)
        b_t = sb("rwkv_b_by_token", [P, TT, T], F32, rwkv_stack)
        with nc.Block() as block:
            turns = [(dst, get, tile) for dst, get in ((v_t, lambda j: R(V_ + j)), (k_t, lambda j: R(K_ + j)), (b_t, lambda j: bb[:, j, :]))
                     for tile in range(TT)]

            @block.tensor
            def _(pe):
                for n, (dst, get, tile) in enumerate(turns):
                    if n >= 4:
                        pe.wait_ge(tok_copied.sem, n - 3)
                    for j in range(4):
                        mm = nc.tensor.transpose(psum[:, n % 4, j * P:(j + 1) * P], get(j)[:, tile * P:(tile + 1) * P], ident[:])
                    mm.then_inc(tok_turned.sem, 1)

            @block.scalar
            def _(act):
                for n, (dst, get, tile) in enumerate(turns):
                    act.wait_ge(tok_turned.sem, n + 1)
                    nc.scalar.activation(dst[:, tile, :], psum[:, n % 4, :], ACT.Copy).then_inc(tok_copied.sem, 1)

        LEVELS = 6
        PAIRS = 5
        pair_mm, pair_done = sig("pair_products_ready"), sig("pair_products_masked")
        inverse_first, inverse_t_first = sig("first_inverse_ready"), sig("first_inverse_t_ready")
        part_ready, times_l, prod_copied = sig("joining_blocks_ready"), sig("l_times_inverse_ready"), sig("l_times_inverse_copied")
        joined, inverse_stepped, stepped = sig("joined_blocks_ready"), sig("inverse_stepped"), sig("inverse_t_stepped")
        unit_added = sig("inverse_t_first_step")
        x0_mm, x0_copied, sa_mm, sa_copied = sig("x0_ready"), sig("x0_copied"), sig("sa_ready"), sig("sa_copied")
        y_mm, y_copied, state_mm, state_done, state_step = sig("y_ready"), sig("y_copied"), sig("state_product_ready"), sig("state_updated"), sig("state_step")
        chunk_masks_loaded = sig("chunk_masks_loaded")
        with ExitStack() as local, nc.Block() as block:
            masks = sb("chunk_masks", [P, 11, P], F32, local)
            lak, lrb, lrk, low, inv, inv_t, prod, part = (sb(n, [P, 8, P], F32, local) for n in (
                "chunk_lak", "chunk_lrb", "chunk_lrk", "chunk_l_t", "chunk_inverse", "chunk_inverse_t", "chunk_l_inverse", "chunk_l_part"))
            state = sb("state", [P, 4, 64], F32, local)
            x0 = sb("chunk_x0", [P, 8, 64], F32, local)
            sa = sb("chunk_sa", [P, 8, 64], F32, local)

            def at_head(h):
                return (h % 2) * 4 + h // 2

            def rows(h):
                return slice(64 * (h % 2), 64 * (h % 2) + 64)

            def both(b):
                return psum[:, b:b + 2, :].rearrange("p b (h t) -> p (b h) t", t=P)

            def half(buf, g):
                return buf[:, 4 * g:4 * g + 4, :]

            def bank4(b):
                return psum[:, b, :].rearrange("p (h t) -> p h t", t=P)

            def mask(m, n):
                return masks[:, m, :].unsqueeze(1).to_broadcast([P, n, P])

            @block.sync
            def _(sp):
                sp.dma_start(masks[:, :, :], rwkv["chunk_masks"]).then_inc(chunk_masks_loaded.sem, 16)

            @block.tensor
            def _(pe):
                for c in range(TT):
                    tok, tok1 = slice(c * P, (c + 1) * P), slice(1 + c * P, 1 + (c + 1) * P)

                    def a_(h): return kk[rows(h), h // 2, tok]
                    def b_(h): return bb[rows(h), h // 2, tok]
                    def k_(h): return rw[rows(h), K_ + h // 2, tok1]
                    def r_(h): return rw[rows(h), R_ + h // 2, tok1]
                    if c:
                        pe.wait_ge(y_copied.sem, c)
                        pe.wait_ge(state_done.sem, c)
                    for n, (one, two) in enumerate(((a_, b_), (b_, a_), (k_, a_), (b_, r_), (k_, r_))):
                        m = c * PAIRS + n
                        if m >= 2:
                            pe.wait_ge(pair_done.sem, m - 1)
                        for h in range(8):
                            mm = nc.tensor.matmul(both(2 * (m % 2))[:, at_head(h), :], one(h), two(h), start=True, stop=True)
                        mm.then_inc(pair_mm.sem, 1)
                    for l in range(LEVELS):
                        for g in range(2):
                            n = (c * LEVELS + l) * 2 + g
                            pe.wait_ge(part_ready.sem, n + 1)
                            if l == 0:
                                pe.wait_ge(inverse_first.sem, c + 1)
                            else:
                                pe.wait_ge(inverse_stepped.sem, (c * (LEVELS - 1) + l - 1) * 2 + g + 1)
                            for h in range(g, 8, 2):
                                mm = nc.tensor.matmul(psum[:, 4 + g, (h // 2) * P:(h // 2 + 1) * P], part[:, at_head(h), :], inv[:, at_head(h), :],
                                                      start=True, stop=True)
                            mm.then_inc(times_l.sem, 1)
                        for g in range(2):
                            n = (c * LEVELS + l) * 2 + g
                            pe.wait_ge(prod_copied.sem, n + 1)
                            if l == 0:
                                pe.wait_ge(inverse_t_first.sem, c + 1)
                            else:
                                pe.wait_ge(stepped.sem, n - 1)
                            for h in range(g, 8, 2):
                                mm = nc.tensor.matmul(psum[:, 6 + g, (h // 2) * P:(h // 2 + 1) * P], prod[:, at_head(h), :], inv_t[:, at_head(h), :],
                                                      start=True, stop=True)
                            if l < LEVELS - 1:
                                for h in range(g, 8, 2):
                                    mm = nc.tensor.matmul(psum[:, 4 + g, (h // 2) * P:(h // 2 + 1) * P], inv_t[:, at_head(h), :], prod[:, at_head(h), :],
                                                          start=True, stop=True)
                            mm.then_inc(joined.sem, 1)
                    pe.wait_ge(pair_done.sem, PAIRS * (c + 1))
                    for h in range(8):
                        out = psum[:, h % 2, (h // 2) * 64:(h // 2 + 1) * 64]
                        if c:
                            nc.tensor.matmul(out, a_(h), state[rows(h), h // 2, :], start=True, stop=False)
                        mm = nc.tensor.matmul(out, lak[:, at_head(h), :], v_t[:, c, h * 64:(h + 1) * 64], start=not c, stop=True)
                    mm.then_inc(x0_mm.sem, 1)
                    pe.wait_ge(x0_copied.sem, c + 1)
                    pe.wait_ge(stepped.sem, 2 * LEVELS * (c + 1))
                    for h in range(8):
                        mm = nc.tensor.matmul(psum[:, 2, at_head(h) * 64:(at_head(h) + 1) * 64], inv_t[:, at_head(h), :], x0[:, at_head(h), :],
                                              start=True, stop=True)
                    mm.then_inc(sa_mm.sem, 1)
                    pe.wait_ge(sa_copied.sem, c + 1)
                    for h in range(8):
                        out = psum[rows(h), h % 2, (h // 2) * P:(h // 2 + 1) * P]
                        if c:
                            nc.tensor.matmul(out, state[rows(h), h // 2, :], r_(h), start=True, stop=False)
                        nc.tensor.matmul(out, sa[:, at_head(h), :], lrb[:, at_head(h), :], start=not c, stop=False)
                        mm = nc.tensor.matmul(out, v_t[:, c, h * 64:(h + 1) * 64], lrk[:, at_head(h), :], start=False, stop=True)
                    mm.then_inc(y_mm.sem, 1)
                    for h in range(8):
                        out = psum[rows(h), 2 + h % 2, (h // 2) * 64:(h // 2 + 1) * 64]
                        nc.tensor.matmul(out, b_t[:, c, h * 64:(h + 1) * 64], sa[:, at_head(h), :], start=True, stop=False)
                        mm = nc.tensor.matmul(out, k_t[:, c, h * 64:(h + 1) * 64], v_t[:, c, h * 64:(h + 1) * 64], start=False, stop=True)
                    mm.then_inc(state_mm.sem, 1)

            @block.scalar
            def _(act):
                for c in range(TT):
                    for l in range(LEVELS):
                        for g in range(2):
                            n = (c * LEVELS + l) * 2 + g
                            act.wait_ge(times_l.sem, n + 1)
                            nc.scalar.activation(half(prod, g), bank4(4 + g), ACT.Copy).then_inc(prod_copied.sem, 1)
                    act.wait_ge(x0_mm.sem, c + 1)
                    nc.scalar.activation(x0[:, :, :].rearrange("p (g h) v -> p g (h v)", g=2), psum[:, 0:2, 0:256], ACT.Copy).then_inc(x0_copied.sem, 1)
                    act.wait_ge(sa_mm.sem, c + 1)
                    nc.scalar.activation(sa[:, :, :].rearrange("p h v -> p (h v)"), psum[:, 2, :], ACT.Copy).then_inc(sa_copied.sem, 1)
                    act.wait_ge(y_mm.sem, c + 1)
                    for g in range(2):
                        part_rows = slice(64 * g, 64 * g + 64)
                        copied = nc.scalar.activation(y[part_rows, :, c * P:(c + 1) * P], bank4(g)[part_rows, :, :], ACT.Copy)
                    copied.then_inc(y_copied.sem, 1)

            @block.gpsimd
            def _(pool):
                pool.wait_ge(chunk_masks_loaded.sem, 16)
                for c in range(TT):
                    pool.wait_ge(pair_done.sem, PAIRS * c + 2)
                    nc.gpsimd.tensor_tensor(inv_t[:, :, :], low[:, :, :], mask(8, 8), ALU.mult).then_inc(unit_added.sem, 1)
                    pool.wait_ge(unit_added.sem, c + 1)
                    nc.gpsimd.tensor_tensor(inv_t[:, :, :], inv_t[:, :, :], mask(10, 8), ALU.add).then_inc(inverse_t_first.sem, 1)
                    for l in range(LEVELS):
                        for g in range(2):
                            n = (c * LEVELS + l) * 2 + g
                            if n >= 2:
                                pool.wait_ge(times_l.sem, n - 1)
                            nc.gpsimd.tensor_tensor(half(part, g), half(low, g), mask(2 + l, 4), ALU.mult).then_inc(part_ready.sem, 1)

            @block.vector
            def _(dve):
                dve.wait_ge(chunk_masks_loaded.sem, 16)
                for c in range(TT):
                    if c:
                        dve.wait_ge(part_ready.sem, 2 * LEVELS * c)
                    for n, (dst, m) in enumerate(((inv, 9), (low, 0), (lak, 0), (lrb, 1), (lrk, 1))):
                        dve.wait_ge(pair_mm.sem, PAIRS * c + n + 1)
                        nc.vector.tensor_tensor(dst[:, :, :], both(2 * ((PAIRS * c + n) % 2)), mask(m, 8), ALU.mult).then_inc(pair_done.sem, 1)
                        if n == 1:
                            dve.wait_ge(pair_done.sem, PAIRS * c + 1)
                            nc.vector.tensor_tensor(inv[:, :, :], inv[:, :, :], mask(10, 8), ALU.add).then_inc(inverse_first.sem, 1)
                    for l in range(LEVELS):
                        for g in range(2):
                            n = (c * LEVELS + l) * 2 + g
                            dve.wait_ge(joined.sem, n + 1)
                            if l < LEVELS - 1:
                                nc.vector.tensor_tensor(half(inv, g), half(inv, g), bank4(4 + g), ALU.add).then_inc(inverse_stepped.sem, 1)
                            nc.vector.tensor_tensor(half(inv_t, g), half(inv_t, g), bank4(6 + g), ALU.add).then_inc(stepped.sem, 1)
                    dve.wait_ge(state_mm.sem, c + 1)
                    if c < TT - 1:
                        for g in range(2):
                            part_rows = slice(64 * g, 64 * g + 64)
                            new = psum[part_rows, 2 + g, 0:256].rearrange("p (h v) -> p h v", v=64)
                            if c:
                                step = nc.vector.tensor_tensor(state[part_rows, :, :], state[part_rows, :, :], new, ALU.add)
                            else:
                                step = nc.vector.tensor_copy(state[part_rows, :, :], new)
                        step.then_inc(state_step.sem, 1)
                        dve.wait_ge(state_step.sem, 2 * c + 1)
                        nc.vector.tensor_tensor(state[:, :, :], state[:, :, :], mid_decay[:, 1, :, c].unsqueeze(2).to_broadcast([P, 4, 64]),
                                                ALU.mult).then_inc(state_step.sem, 1)
                        dve.wait_ge(state_step.sem, 2 * c + 2)
                        nc.vector.tensor_tensor(state[:, :, :], state[:, :, :], mid_decay[:, 0, :, c + 1].unsqueeze(2).to_broadcast([P, 4, 64]),
                                                ALU.mult).then_inc(state_done.sem, 1)

        gate_product, out_step = sig("rwkv_gate_ready"), sig("rwkv_out_step")

        def gate_products(pe):
            for j in range(4):
                cols = slice(j * P, (j + 1) * P)
                nc.tensor.matmul(psum[:, 4 + j, :], lora[:, 1, cols], R(G_), start=True, stop=False)
                nc.tensor.matmul(psum[:, 4 + j, :], lora[0:32, 2, cols], rw[0:32, G_ + 1, 1:T + 1], start=False, stop=True).then_inc(gate_product.sem, 1)

        def finish_y(dve):
            for j in range(4):
                dve.wait_ge(gn_out.sem, gn_out.at(j + 1))
                nc.vector.tensor_scalar(y[:, j, :], y[:, j, :], lnw[:, j:j + 1], lnb[:, j:j + 1], ALU.mult, ALU.add).then_inc(out_step.sem, 1)
            for j in range(4):
                dve.wait_ge(out_step.sem, j + 1)
                nc.vector.tensor_tensor(y[:, j, :], y[:, j, :], bonus[:, j, :], ALU.add).then_inc(out_step.sem, 1)
            for j in range(4):
                dve.wait_ge(out_step.sem, 4 + j + 1)
                dve.wait_ge(gate_product.sem, j + 1)
                nc.vector.tensor_tensor(y[:, j, :], y[:, j, :], psum[:, 4 + j, :], ALU.mult)
        head_norm(y, block_avg[:], ln_eps[:, 0:1], center=True, products=gate_products, finish=finish_y)
        rwkv_stack.close()
        if stop == 4:
            return

        mem_stack = ExitStack()
        ctx.enter_context(mem_stack)
        mem_sb = sb("memory", [P, C, M], F32, mem_stack)
        mem_loaded = sig("memory_loaded")
        branch_stack = ExitStack()
        ctx.enter_context(branch_stack)
        branch_hi = sb("branch_hi", [P, C, T], F32R, branch_stack)
        branch_lo = sb("branch_lo", [P, C, T], F32R, branch_stack)
        act_hi = sb("act_hi", [P, C, T], F32R, branch_stack)
        act_lo = sb("act_lo", [P, C, T], F32R, branch_stack)
        conv_u, conv_acc, conv_w_loaded = sig("conv_input_ready"), sig("conv_step"), sig("conv_weights_loaded")
        conv_done = sig("conv_ready")
        with ExitStack() as local:
            cv = sb("conv_projections", [P, 12, T], F32, local)
            acc = sb("conv_out", [P, 4, T], F32, local)
            taps = sb("conv_taps", [P, 4, 3], F32, local)

            def load_conv(sp):
                sp.dma_start(taps[:, :, :], conv_taps).then_inc(conv_w_loaded.sem, 16)
                sp.dma_start(mem_sb[:, :, :], mem_t).then_inc(mem_loaded.sem, 16)
            load_conv.arrived = None
            def gpsimd_along(pool, before_first):
                for j in range(4):
                    pool.wait_ge(out_free.sem, before_first + 8 + j + 1)
                    nc.gpsimd.tensor_tensor(cv[:, 4 + j, :], cv[:, 4 + j, :], cv[:, 8 + j, :], ALU.mult).then_inc(conv_u.sem, 1)

            def convolve(j):
                nc.vector.wait_ge(conv_u.sem, j + 1)
                u, a = cv[:, 4 + j, :], acc[:, j, :]
                nc.vector.tensor_scalar(a, u, taps[:, j, 2:3], None, ALU.mult).then_inc(conv_acc.sem, 1)
                for back, tap in ((1, 1), (2, 0)):
                    nc.vector.wait_ge(conv_acc.sem, 3 * j + back)
                    nc.vector.scalar_tensor_tensor(acc[:, j, back:T], cv[:, 4 + j, 0:T - back], taps[:, j, tap:tap + 1], acc[:, j, back:T],
                                                   ALU.mult, ALU.add).then_inc(conv_acc.sem, 1)
                nc.vector.wait_ge(conv_acc.sem, 3 * j + 3)
                nc.vector.tensor_tensor(a, a, cv[:, j, :], ALU.mult).then_inc(conv_done.sem, 1)

            def conv_lo(j):
                nc.vector.wait_ge(split_hi_ready.sem, split_hi_ready.at(j + 1))
                nc.vector.tensor_tensor(branch_lo[:, 4 + j, :], acc[:, j, :], branch_hi[:, 4 + j, :].bitcast(F32), ALU.subtract)

            def vector_along(k):
                if k == 9:
                    nc.vector.wait_ge(conv_w_loaded.sem, 16)
                if k >= 9:
                    convolve(k - 9)
                if k >= 10:
                    conv_lo(k - 10)
                if k == 11:
                    convolve(3)
                    conv_lo(2)
                    conv_lo(3)

            def scalar_along(k):
                for j in {10: [0], 11: [1, 2, 3]}.get(k, []):
                    nc.scalar.wait_ge(conv_done.sem, j + 1)
                    nc.scalar.activation(branch_hi[:, 4 + j, :], acc[:, j, :], ACT.Copy).then_inc(split_hi_ready.sem, 1)
            linear(12, (act_hi, act_lo), scaled(lambda n: cv[:, n, :]), "vector",
                   parts=[(c, x[:, c, :], gains[:, 3, c:c + 1], None) for c in range(C)],
                   more=[(branch_hi[:, j, :], branch_lo[:, j, :], y[:, j, :]) for j in range(4)],
                   before=load_conv, along=(scalar_along, vector_along, gpsimd_along))
            split_hi_ready.base += 4

        gate_sig, gate_a, merged_f, merged_hi_ready = sig("merge_gates_ready"), sig("merge_gated"), sig("merged_ready"), sig("merged_hi_ready")
        gate_bias_loaded, gate_in = sig("gate_bias_loaded"), sig("merge_gates_scaled")
        inner_hi = sb("inner_hi", [P, C, T], F32R, branch_stack)
        inner_lo = sb("inner_lo", [P, C, T], F32R, branch_stack)
        with ExitStack() as local, nc.Block() as block:
            gate_bias = sb("gate_bias", [P, 2, C], F32, local)
            opened = sb("merge_gates", [P, 2, T], F32, local)
            gate_raw = sb("merge_gates_raw", [P, 2, T], F32, local)
            gated_b = sb("merge_gated_branches", [P, 2, T], F32, local)
            merged = sb("merged", [P, 2, T], F32, local)
            w, u0, per, turn = weights, weights.u0, 12, 4

            @block.sync
            def _(sp):
                sp.dma_start(gate_bias[:, :, :], gate_bias_in).then_inc(gate_bias_loaded.sem, 16)
                w.load_stage(sp, 3 * C)

            @block.tensor
            def _(pe):
                pe.sem_inc(merged_f.sem, 2)
                with pe.Fori(0, C // turn) as i:
                    for q in range(turn):
                        b = 4 * (q % 2)
                        pe.wait_ge(merged_f.sem, i * turn + (q + 1))
                        w.multiply(pe, i, 3 * q, per, psum[:, b, :], (branch_hi[:, 0:4, :], branch_lo[:, 0:4, :]), chunks=range(4))
                        w.multiply(pe, i, 3 * q, per, psum[:, b + 1, :], (branch_hi[:, 4:8, :], branch_lo[:, 4:8, :]),
                                   chunks=range(4, 8)).then_inc(w.unit_done.sem, 1)
                        for g in range(2):
                            w.multiply(pe, i, 3 * q + 1 + g, per, psum[:, b + 2 + g, :], (act_hi, act_lo)).then_inc(w.unit_done.sem, 1)

            @block.scalar
            def _(act):
                act.wait_ge(gate_bias_loaded.sem, 16)
                act.sem_inc(gate_a.sem, 2)
                with act.Fori(0, C // turn) as i:
                    for q in range(turn):
                        for g in range(3):
                            w.hi_step(act, i, 3 * q + g + w.AHEAD, per)
                            if g:
                                act.wait_ge(gate_in.sem, i * (2 * turn) + (2 * q + g))
                                act.wait_ge(gate_a.sem, i * (2 * turn) + (2 * q + g))
                                nc.scalar.activation(opened[:, g - 1, :], gate_raw[:, g - 1, :], ACT.Sigmoid,
                                                     bias=gate_bias[:, g - 1, bass.ds(i * turn + q, 1)]).then_inc(gate_sig.sem, 1)
                        act.wait_ge(merged_f.sem, i * turn + (q + 3))
                        nc.scalar.activation(inner_hi[:, bass.ds(i * turn + q, 1), :], merged[:, q % 2, :].unsqueeze(1), ACT.Copy).then_inc(merged_hi_ready.sem, 1)

            @block.vector
            def _(dve):
                with dve.Fori(0, C // turn) as i:
                    for q in range(turn):
                        for g in range(3):
                            w.lo_step(dve, i, 3 * q + g + w.AHEAD, per)
                            if g:
                                dve.wait_ge(w.unit_done.sem, i * per + w.done(3 * q + g))
                                nc.vector.tensor_tensor(gate_raw[:, g - 1, :], psum[:, 4 * (q % 2) + 1 + g, :], rstd[:], ALU.mult).then_inc(gate_in.sem, 1)
                                dve.wait_ge(gate_sig.sem, i * (2 * turn) + (2 * q + g))
                                nc.vector.tensor_tensor(gated_b[:, g - 1, :], opened[:, g - 1, :],
                                                        psum[:, 4 * (q % 2) + g - 1, :], ALU.mult).then_inc(gate_a.sem, 1)
                        dve.wait_ge(gate_a.sem, i * (2 * turn) + (2 * q + 4))
                        nc.vector.tensor_tensor(merged[:, q % 2, :], gated_b[:, 0, :], gated_b[:, 1, :], ALU.add).then_inc(merged_f.sem, 1)
                        dve.wait_ge(merged_hi_ready.sem, i * turn + (q + 1))
                        nc.vector.tensor_tensor(inner_lo[:, bass.ds(i * turn + q, 1), :], merged[:, q % 2, :].unsqueeze(1),
                                                inner_hi[:, bass.ds(i * turn + q, 1), :].bitcast(F32), ALU.subtract)
            w.u0 += 3 * C

        def add_to_x(loop, k, bank):
            return nc.vector.tensor_tensor(x[:, at(loop, k), :], x[:, at(loop, k), :], bank, ALU.add)

        linear(C, (inner_hi, inner_lo), add_to_x, "vector")
        branch_stack.close()
        if stop == 5:
            return

        mlp_hi = sb("mlp_act_hi", [P, C, T], F32R, mem_stack)
        mlp_lo = sb("mlp_act_lo", [P, C, T], F32R, mem_stack)
        out_stack = ExitStack()
        ctx.enter_context(out_stack)
        out_f = sb("memory_out", [P, C, T], F32, out_stack)
        kv_stack = ExitStack()
        ctx.enter_context(kv_stack)
        kv = sb("memory_kv", [P, 2 * C, M], F32, kv_stack)
        v_m = sb("memory_v_by_token", [P, M // P, D], F32, kv_stack)
        queries = sb("memory_queries", [P, C, T], F32, kv_stack)
        with ExitStack() as local:
            mem_hi = sb("memory_hi", [P, C, M], F32R, local)
            mem_lo = sb("memory_lo", [P, C, M], F32R, local)

            def before_memory(sp):
                pass

            def memory_arrived(eng, c):
                if c == 0 or c is None:
                    eng.wait_ge(mem_loaded.sem, 16)
            before_memory.arrived = memory_arrived
            linear(2 * C, (mem_hi, mem_lo), scaled(lambda n: kv[:, n, :], M), "vector", tokens=M, norm=(mem_sb, 5), before=before_memory)
        linear(C, (mlp_hi, mlp_lo), scaled(lambda n: queries[:, n, :]), "vector", norm=(x, 4))
        x_scored, x_max, x_neg, x_exp, x_inv, x_prob = (sig(n) for n in (
            "memory_scores_ready", "memory_max_ready", "memory_neg_max_ready", "memory_exp_ready", "memory_inverse_sum_ready", "memory_probs_ready"))
        x_turned, x_copied, x_out, v_m_turned, v_m_copied = (sig(n) for n in (
            "memory_probs_transposed", "memory_probs_copied", "memory_out_ready", "memory_v_transposed", "memory_v_copied"))
        x_out_copied = sig("memory_out_copied")
        XH = 4
        MT = M // P
        with ExitStack() as local, nc.Block() as block:
            pr = sb("memory_probs", [P, 2, M], F32, local)
            pr_t = sb("memory_probs_t", [P, 2, MT, T], F32, local)
            st = sb("memory_stats", [P, XH * TT, 4], F32, local)
            x_scale = 256 ** -0.5

            @block.tensor
            def _(pe):
                for mt in range(MT):
                    for half_c in range(2):
                        n = 2 * mt + half_c
                        if n >= 2:
                            pe.wait_ge(v_m_copied.sem, n - 1)
                        for j in range(4):
                            mm = nc.tensor.transpose(psum[:, 4 + n % 2, j * P:(j + 1) * P], kv[:, C + 4 * half_c + j, mt * P:(mt + 1) * P], ident[:])
                        mm.then_inc(v_m_turned.sem, 1)

                def scores(it):
                    h, tile = divmod(it, TT)
                    if it >= 3:
                        pe.wait_ge(x_exp.sem, it - 2)
                    for e in range(2):
                        mm = nc.tensor.matmul(psum[:, it % 3, 0:M], queries[:, 2 * h + e, tile * P:(tile + 1) * P], kv[:, 2 * h + e, :],
                                              start=e == 0, stop=e == 1)
                    mm.then_inc(x_scored.sem, 1)
                scores(0)
                scores(1)
                for it in range(XH * TT):
                    h, tile = divmod(it, TT)
                    if it + 2 < XH * TT:
                        scores(it + 2)
                    pe.wait_ge(x_prob.sem, it + 1)
                    if it >= 1:
                        pe.wait_ge(x_copied.sem, it)
                    for mt in range(MT):
                        mm = nc.tensor.transpose(psum[:, 3, mt * P:(mt + 1) * P], pr[:, it % 2, mt * P:(mt + 1) * P], ident[:])
                    mm.then_inc(x_turned.sem, 1)
                    if tile == TT - 1:
                        pe.wait_ge(x_copied.sem, it + 1)
                        pe.wait_ge(v_m_copied.sem, 2 * MT)
                        if h >= 1:
                            pe.wait_ge(x_out_copied.sem, 2 * h)
                        for e in range(2):
                            for mt in range(MT):
                                mm = nc.tensor.matmul(psum[:, 6 + e, :], v_m[:, mt, (2 * h + e) * P:(2 * h + e + 1) * P], pr_t[:, h % 2, mt, :],
                                                      start=mt == 0, stop=mt == MT - 1)
                            mm.then_inc(x_out.sem, 1)

            @block.scalar
            def _(act):
                for n in range(2 * MT):
                    act.wait_ge(v_m_turned.sem, n + 1)
                    nc.scalar.activation(v_m[:, n // 2, (n % 2) * T:(n % 2 + 1) * T], psum[:, 4 + n % 2, :], ACT.Copy).then_inc(v_m_copied.sem, 1)

                def exps(it):
                    act.wait_ge(x_neg.sem, it + 1)
                    if it >= 2:
                        act.wait_ge(x_turned.sem, it - 1)
                    nc.scalar.activation(pr[:, it % 2, :], psum[:, it % 3, 0:M], ACT.Exp, bias=st[:, it, 1:2], scale=x_scale,
                                         accum_out=st[:, it, 2:3]).then_inc(x_exp.sem, 1)
                exps(0)
                for it in range(XH * TT):
                    h, tile = divmod(it, TT)
                    if it + 1 < XH * TT:
                        exps(it + 1)
                    act.wait_ge(x_turned.sem, it + 1)
                    if h >= 2:
                        act.wait_ge(x_out.sem, 2 * (h - 1))
                    nc.scalar.activation(pr_t[:, h % 2, :, tile * P:(tile + 1) * P], psum[:, 3, 0:M].rearrange("p (m t) -> p m t", m=MT),
                                         ACT.Copy).then_inc(x_copied.sem, 1)
                    if tile == TT - 1:
                        for e in range(2):
                            act.wait_ge(x_out.sem, 2 * h + e + 1)
                            nc.scalar.activation(out_f[:, 2 * h + e, :], psum[:, 6 + e, :], ACT.Copy).then_inc(x_out_copied.sem, 1)

            @block.vector
            def _(dve):
                def maxima(it):
                    dve.wait_ge(x_scored.sem, it + 1)
                    nc.vector.tensor_reduce(st[:, it, 0:1], psum[:, it % 3, 0:M], AX.X, ALU.max).then_inc(x_max.sem, 1)
                    dve.wait_ge(x_max.sem, it + 1)
                    nc.vector.tensor_scalar(st[:, it, 1:2], st[:, it, 0:1], -x_scale, None, ALU.mult).then_inc(x_neg.sem, 1)
                maxima(0)
                maxima(1)
                for it in range(XH * TT):
                    dve.wait_ge(x_exp.sem, it + 1)
                    nc.vector.reciprocal(st[:, it, 3:4], st[:, it, 2:3]).then_inc(x_inv.sem, 1)
                    dve.wait_ge(x_inv.sem, it + 1)
                    nc.vector.tensor_scalar(pr[:, it % 2, :], pr[:, it % 2, :], st[:, it, 3:4], None, ALU.mult).then_inc(x_prob.sem, 1)
                    if it + 2 < XH * TT:
                        maxima(it + 2)
        kv_stack.close()
        with ExitStack() as local:
            out_hi = sb("memory_out_hi", [P, C, T], F32R, local)
            out_lo = sb("memory_out_lo", [P, C, T], F32R, local)
            linear(C, (out_hi, out_lo), add_to_x, "vector", parts=[(j, out_f[:, j, :], 1.0, None) for j in range(C)],
                   then=(6, mlp_hi, mlp_lo))
        out_stack.close()
        if stop == 6:
            return

        with ExitStack() as local:
            inner_hi = sb("inner_hi", [P, C, T], F32R, local)
            inner_lo = sb("inner_lo", [P, C, T], F32R, local)
            raw_act = sb("inner_activated", [P, 2, T], F32, local)
            raw_gated = sb("inner_gated", [P, 2, T], F32, local)
            feed_forward(MLP_GROUPS, (mlp_hi, mlp_lo), ACT.Relu, False, inner_hi, inner_lo, raw_act, raw_gated)
        scale_x(7, store=out_t)


def unit_layout(w):
    import numpy as np
    k, n = w.shape
    return np.ascontiguousarray(w.reshape(C, P, n // P, P).transpose(2, 1, 0, 3)).reshape(n // P, P, UNIT)


def constants():
    import numpy as np
    f = np.float32
    pos = np.arange(T, dtype=f)

    def rope(inv, dim, block):
        half = len(inv)
        ang = (pos[:, None] * inv[None, :]).astype(f)
        cos, sin = np.ones((block, T), f), np.zeros((block, T), f)
        swap = np.zeros((block, block), f)
        cos[:half] = cos[half:2 * half] = np.cos(ang).T
        sin[:half], sin[half:2 * half] = -np.sin(ang).T, np.sin(ang).T
        for i in range(half):
            swap[i, i + half] = swap[i + half, i] = 1
        n = P // block
        return np.tile(cos, (n, 1)), np.tile(sin, (n, 1)), np.kron(np.eye(n, dtype=f), swap)

    inv_d = np.power(f(500000.0), -np.arange(8, dtype=f) * f(2.0) / f(16)).astype(f)
    inv_r = (f(1.0) / np.power(f(10000.0), np.linspace(0.0, 1.0, 32, dtype=f))).astype(f)
    cd, sd, swd = rope(inv_d, 16, 64)
    cr, sr, swr = rope(inv_r, 64, 64)
    span = T + (TT - 1) * P
    ahead = (np.arange(span)[None, :] - (TT - 1) * P - np.arange(P)[:, None]).astype(f)
    n = np.arange(P)
    s, t = n[:, None], n[None, :]
    levels = [((s // m) % 2 == 0) & (t // m == s // m + 1) for m in (2, 4, 8, 16, 32, 64)]
    join0 = (s % 2 == 0) & (t == s + 1)
    blocks = np.kron(np.eye(2, dtype=f), np.ones((64, 64), f))
    return {
        "rwkv_sum_masks": np.ascontiguousarray(np.stack([(s <= t) * 1.0 - (s < 64), (s < t) * 1.0 - (s < 64)], 1).astype(f)),
        "rwkv_chunk_masks": np.ascontiguousarray(np.stack([s < t, s <= t, *levels, join0, join0.T, s == t], 1).astype(f)),
        "rwkv_block_ones": blocks,
        "rwkv_block_average": blocks / f(64),
        "rope_tables": np.ascontiguousarray(np.stack([cd, sd, cr, sr], 1)),
        "swap": np.ascontiguousarray(np.stack([swd, swr], 1)),
        "iota_in": np.tile(np.arange(P, dtype=f), (P, 1)),
        "ident_in": np.eye(P, dtype=f),
        "distance": np.ascontiguousarray(np.stack([np.maximum(ahead, 0), np.maximum(-ahead, 0)], 1)),
    }


def expert_units(u, v):
    import numpy as np
    up = u.reshape(P, EXPERT_GROUPS, C, C, P).transpose(1, 2, 4, 3, 0)
    down = v.reshape(P, EXPERT_GROUPS, C, C, P).transpose(1, 3, 0, 2, 4)
    up, down, n = up.reshape(-1, C, P, UNIT), down.reshape(-1, C, P, UNIT), GROUPS_AHEAD
    rest = np.concatenate([up[n:], down[n:]], 1)
    return np.concatenate([part.reshape(-1, P, UNIT) for part in (up[:n], down[:n], rest)])


def mlp_units(up, down):
    import numpy as np
    groups = down.shape[0] // D
    ups = unit_layout(up).reshape(groups, C, P, UNIT)
    downs = down.reshape(groups, C, P, C, P).transpose(0, 3, 2, 1, 4).reshape(groups, C, P, UNIT)
    return np.concatenate([ups, downs], 1).reshape(-1, P, UNIT)


def host_layout(inputs):
    import numpy as np

    def by_feature(v):
        return np.ascontiguousarray(v.reshape(-1, P).T)

    def tokens_last(a):
        return np.ascontiguousarray(a.T.reshape(-1, P, a.shape[0]).transpose(1, 0, 2))

    g = {k: np.asarray(v) for k, v in inputs.items()}
    w2 = g["w_in_2"][0]
    rwkv_cols, conv_cols = 1824, 3 * 512
    w_rwkv = np.concatenate([w2[:, :rwkv_cols], np.zeros((D, RWKV_SLABS * P - rwkv_cols), w2.dtype)], 1)
    w_merge = np.stack([unit_layout(np.concatenate([g["w_proj_a_2"][0], g["w_proj_b_2"][0]], 0)),
                        unit_layout(w2[:, rwkv_cols + conv_cols:rwkv_cols + conv_cols + D]),
                        unit_layout(w2[:, rwkv_cols + conv_cols + D:])], 1).reshape(-1, P, UNIT)
    mu = np.concatenate([g["mu_shift_2"][0], np.zeros(RWKV_SLABS * P - rwkv_cols, w2.dtype)])
    vectors = np.concatenate([by_feature(mu), np.zeros((P, 1), w2.dtype)]
                             + [by_feature(g[n][0].reshape(-1)) for n in ("k_k_2", "k_a_2", "r_k_2", "a0_2", "ln_x_w_2", "ln_x_b_2")], 1)
    gains = [g[n].reshape(-1) for n in ("attn_norm_g", "ffn_norm_g", "final_norm_g", "norm_mix_2", "norm_xattn_2",
                                        "norm_mem_2", "norm_mlp_2", "norm_final_2")]
    arrays = {
        "x_t": tokens_last(g["x"][0]),
        "mem_t": tokens_last(g["mem_2"][0]),
        "norm_gains": np.ascontiguousarray(np.stack([by_feature(v) for v in gains], 1)),
        "lam_in": np.ascontiguousarray(np.tile(g["diff_lambda"], (P, 1, 1))),
        "diff_gain": np.ascontiguousarray(g["diff_norm_g"][0].reshape(P, 1)),
        "ret_decay": np.ascontiguousarray(np.tile(g["ret_log_decay"].reshape(1, -1), (P, 1))),
        "ret_gain": np.ascontiguousarray(g["ret_norm_g"][0].T),
        "keys_t": np.ascontiguousarray(g["peer_sub_keys"][0].reshape(LISTS, N_KEYS, P).transpose(2, 0, 1)),
        "rwkv_vectors": np.ascontiguousarray(vectors),
        "rwkv_lora_wa": np.ascontiguousarray(np.concatenate([g["w_lora_w_2"][0], g["w_lora_a_2"][0]], 0)),
        "rwkv_lora_g": np.ascontiguousarray(g["w_lora_g_2"][0]),
        "rwkv_w0": np.ascontiguousarray(g["w0_2"]),
        "conv_taps": np.ascontiguousarray(g["conv_w_2"][0, :, 0, :].T.reshape(4, P, 3).transpose(1, 0, 2)),
        "gate_bias_in": np.ascontiguousarray(g["b_gate_2"][0].reshape(2, C, P).transpose(2, 0, 1)),
        "u_in": unit_layout(g["w_in"][0]),
        "u_out": unit_layout(g["w_out"][0]),
        "u_query": unit_layout(g["peer_w_query"][0]),
        "u_experts": expert_units(g["peer_u"][0], g["peer_v"][0]),
        "u_rwkv": unit_layout(w_rwkv),
        "u_conv": unit_layout(w2[:, rwkv_cols:rwkv_cols + conv_cols]),
        "u_merge": w_merge,
        "u_out_mix": unit_layout(g["w_out_mix_2"][0]),
        "u_kv": unit_layout(g["w_kv_2"][0]),
        "u_q": unit_layout(g["w_q_2"][0]),
        "u_xo": unit_layout(g["w_xo_2"][0]),
        "u_mlp": mlp_units(g["w_up_2"][0], g["w_down_2"][0]),
    }
    arrays.update(constants())
    return arrays


def kernel(**inputs):
    import numpy as np
    import concourse.bacc as bacc
    from concourse.bass_utils import run_bass_kernel_spmd
    arrays = host_layout(inputs)
    nc = bacc.Bacc("TRN2", target_bir_lowering=False, num_devices=1)
    aps = {k: nc.dram_tensor("in_" + k, v.shape, mybir.dt.from_np(v.dtype), kind="ExternalInput").ap() for k, v in arrays.items()}
    out = nc.dram_tensor("out_0_dram", (P, C, T), mybir.dt.float32, kind="ExternalOutput").ap()
    build_program(nc, aps, out)
    r = run_bass_kernel_spmd(nc, [{"in_" + k: v for k, v in arrays.items()}], core_ids=[0])
    got = np.asarray(r.results[0]["out_0_dram"])
    return np.ascontiguousarray(got.transpose(2, 1, 0).reshape(1, T, D))
```
